# Optimizing a Trainium2 kernel written in Bass

```python
import jax, jax.numpy as jnp
from jax import lax
import numpy as np

D_MODEL = 1024
BATCH = 1
SEQ = 2048
DEPTH = 1

D_LRU = D_MODEL // 2
D_CM = D_MODEL - D_LRU
D_MIX = D_LRU + D_CM
LRU_HEADS = 8
LRU_HEAD_DIM = D_LRU // LRU_HEADS
CM_GROUPS = 8
CONV_SHORT = 4
CONV_LONG = 31
LRU_C = 8.0
D_FF = ((8 * D_MODEL + 3 * 256 - 1) // (3 * 256)) * 256
D_IN = 2 * D_LRU + 2 * D_CM
EPS = 1e-6

kernel_name = "hymba_style_rglru_conformer_hybrid"

def rmsnorm(x, g):
    xf = x.astype(jnp.float32)
    y = xf * lax.rsqrt(jnp.mean(xf * xf, axis=-1, keepdims=True) + EPS)
    return (y * g.astype(jnp.float32)).astype(x.dtype)

def layernorm(x, g, b):
    xf = x.astype(jnp.float32)
    mu = jnp.mean(xf, axis=-1, keepdims=True)
    var = jnp.mean(jnp.square(xf - mu), axis=-1, keepdims=True)
    y = (xf - mu) * lax.rsqrt(var + EPS)
    return (y * g.astype(jnp.float32) + b.astype(jnp.float32)).astype(x.dtype)

def causal_depthwise_conv(x, w, b):
    k = w.shape[0]
    c = x.shape[-1]
    y = lax.conv_general_dilated(
        x, w[:, None, :].astype(x.dtype), window_strides=(1,), padding=[(k - 1, 0)],
        dimension_numbers=('NWC', 'WIO', 'NWC'), feature_group_count=c)
    return y + b.astype(x.dtype)

def _lru_combine(left, right):
    a_l, b_l = left
    a_r, b_r = right
    return a_l * a_r, a_r * b_l + b_r

def rg_lru(x, w_a, b_a, w_x, b_x, lam):
    bsz, s, _ = x.shape
    xh = x.reshape(bsz, s, LRU_HEADS, LRU_HEAD_DIM)
    r = jax.nn.sigmoid(jnp.einsum('bshi,hij->bshj', xh, w_a).reshape(bsz, s, D_LRU) + b_a)
    i = jax.nn.sigmoid(jnp.einsum('bshi,hij->bshj', xh, w_x).reshape(bsz, s, D_LRU) + b_x)
    log_a = -LRU_C * r.astype(jnp.float32) * jax.nn.softplus(-lam.astype(jnp.float32))
    a = jnp.exp(log_a)
    mult = jnp.sqrt(-jnp.expm1(2.0 * log_a))
    b_in = mult * (i * x).astype(jnp.float32)
    _, h = lax.associative_scan(_lru_combine, (a, b_in), axis=1)
    return h.astype(x.dtype)

def setup_inputs(seed: int = 0) -> dict:
    key = jax.random.key(seed)
    ks = jax.random.split(key, 24)
    f32 = jnp.float32

    def nrm(k, shape, fan_in, scale=1.0):
        return jax.random.normal(k, shape, f32) * (scale * fan_in ** -0.5)

    def gain(k, shape):
        return 1.0 + 0.05 * jax.random.normal(k, shape, f32)

    def bias(k, shape):
        return 0.02 * jax.random.normal(k, shape, f32)

    u = jax.random.uniform(ks[9], (DEPTH, D_LRU), f32, 0.9, 0.999)
    a0 = u ** (1.0 / LRU_C)
    lru_lambda = jnp.log(a0) - jnp.log1p(-a0)

    return {
        "x": jax.random.normal(ks[0], (BATCH, SEQ, D_MODEL), f32),
        "norm_mix": gain(ks[1], (DEPTH, D_MODEL)),
        "w_in": nrm(ks[2], (DEPTH, D_MODEL, D_IN), D_MODEL),
        "conv4_w": nrm(ks[3], (DEPTH, CONV_SHORT, D_LRU), CONV_SHORT),
        "conv4_b": bias(ks[4], (DEPTH, D_LRU)),
        "gate_a_w": nrm(ks[5], (DEPTH, LRU_HEADS, LRU_HEAD_DIM, LRU_HEAD_DIM), LRU_HEAD_DIM),
        "gate_a_b": bias(ks[6], (DEPTH, D_LRU)),
        "gate_x_w": nrm(ks[7], (DEPTH, LRU_HEADS, LRU_HEAD_DIM, LRU_HEAD_DIM), LRU_HEAD_DIM),
        "gate_x_b": bias(ks[8], (DEPTH, D_LRU)),
        "lru_lambda": lru_lambda,
        "dw31_w": nrm(ks[10], (DEPTH, CONV_LONG, D_CM), CONV_LONG),
        "dw31_b": bias(ks[11], (DEPTH, D_CM)),
        "cm_ln_g": gain(ks[12], (DEPTH, D_CM)),
        "cm_ln_b": bias(ks[13], (DEPTH, D_CM)),
        "out_norm_lru": gain(ks[14], (DEPTH, D_LRU)),
        "out_norm_cm": gain(ks[15], (DEPTH, D_CM)),
        "w_out": nrm(ks[16], (DEPTH, D_MIX, D_MODEL), D_MIX, 0.5),
        "norm_ffn": gain(ks[17], (DEPTH, D_MODEL)),
        "w_gate": nrm(ks[18], (DEPTH, D_MODEL, D_FF), D_MODEL),
        "w_up": nrm(ks[19], (DEPTH, D_MODEL, D_FF), D_MODEL),
        "w_down": nrm(ks[20], (DEPTH, D_FF, D_MODEL), D_FF, 0.5),
        "norm_final": gain(ks[21], (D_MODEL,)),
    }

def reference(x, norm_mix, w_in, conv4_w, conv4_b, gate_a_w, gate_a_b, gate_x_w, gate_x_b,
              lru_lambda, dw31_w, dw31_b, cm_ln_g, cm_ln_b, out_norm_lru, out_norm_cm,
              w_out, norm_ffn, w_gate, w_up, w_down, norm_final):
    for l in range(DEPTH):
        h = rmsnorm(x, norm_mix[l])
        proj = jnp.einsum('bsd,de->bse', h, w_in[l])
        x_lru = proj[..., :D_LRU]
        g_lru = proj[..., D_LRU:2 * D_LRU]
        v_cm = proj[..., 2 * D_LRU:2 * D_LRU + D_CM]
        g_cm = proj[..., 2 * D_LRU + D_CM:]

        c = causal_depthwise_conv(x_lru, conv4_w[l], conv4_b[l])
        y_lru = rg_lru(c, gate_a_w[l], gate_a_b[l], gate_x_w[l], gate_x_b[l], lru_lambda[l])
        y_lru = y_lru * jax.nn.gelu(g_lru)

        glu = v_cm * jax.nn.sigmoid(g_cm)
        d = causal_depthwise_conv(glu, dw31_w[l], dw31_b[l])
        y_cm = jax.nn.silu(layernorm(d, cm_ln_g[l], cm_ln_b[l]))

        y = jnp.concatenate([rmsnorm(y_lru, out_norm_lru[l]),
                             rmsnorm(y_cm, out_norm_cm[l])], axis=-1)
        x = x + jnp.einsum('bse,ed->bsd', y, w_out[l])

        h = rmsnorm(x, norm_ffn[l])
        f = jax.nn.silu(jnp.einsum('bsd,df->bsf', h, w_gate[l])) * jnp.einsum('bsd,df->bsf', h, w_up[l])
        x = x + jnp.einsum('bsf,fd->bsd', f, w_down[l])
    return rmsnorm(x, norm_final)


_drawn_inputs = setup_inputs


def setup_inputs(seed=0):
    import zlib

    import numpy as np

    out = dict(_drawn_inputs(seed))
    spreads = {}
    factors = {'gate_a_b': 8.0,
     'gate_x_b': 8.0,
     'dw31_b': 4.316,
     'cm_ln_g': 2.988,
     'cm_ln_b': 8.0,
     'out_norm_lru': 4.092,
     'out_norm_cm': 3.473,
     'norm_ffn': 3.088}
    for name, (base, spread) in spreads.items():
        noise = np.random.default_rng([zlib.crc32(name.encode()), seed]).standard_normal(out[name].shape)
        drawn = base * np.exp(spread * noise) if base else spread * noise
        out[name] = __import__('jax').numpy.asarray(drawn.astype(out[name].dtype))
    for name, factor in factors.items():
        out[name] = (out[name] * factor).astype(out[name].dtype)
    return out
```

```python
from contextlib import ExitStack

import concourse.bass as bass
from concourse import mybir

ALU = mybir.AluOpType
ACT = mybir.ActivationFunctionType
F32 = mybir.dt.float32
F32R = mybir.dt.float32r
BF16 = mybir.dt.bfloat16

P = 128
TILE = 512
KIB = 1024
EPS = 1e-6
LRU_C = 8.0
SCRATCH = 1024


def hybrid_block(nc, x, norm_mix, w_in, conv4_w, conv4_b, gate_a_w, gate_a_b, gate_x_w, gate_x_b,
                 lru_lambda, dw31_w, dw31_b, cm_ln_g, cm_ln_b, out_norm_lru, out_norm_cm,
                 w_out, norm_ffn, w_gate, w_up, w_down, norm_final, out):
    S, D = x.shape[1], x.shape[2]
    CH = conv4_b.shape[1]
    NJ = CH // P
    KD = D // P
    F = w_gate.shape[2]
    TAPS4, TAPS31 = conv4_w.shape[1], dw31_w.shape[1]
    HALF = 2 * TILE
    NH = S // HALF
    NS = HALF // TILE
    NT = S // P
    TPH = HALF // P
    UNITS = NH * NJ
    PPAIRS = 2 * UNITS
    FI = F // P // 2
    WOQ = KD // 2
    HD = gate_a_w.shape[2]
    PAD4, PAD31 = TAPS4 - 1, TAPS31 - 1
    assert D == 2 * CH == 1024 and F % (2 * P) == 0 and S == NH * HALF and NH == 2

    xr = x.rearrange("a (t p) d -> (a t) p d", p=P)
    outr = out.rearrange("a (t p) d -> (a t) p d", p=P)
    w_in_r = w_in.rearrange("a (k p) n -> p (a k) n", p=P)
    w_out_r = w_out.rearrange("a (k p) n -> p (a k) n", p=P)
    w_gate_r = w_gate.rearrange("a (k p) n -> p (a k) n", p=P)
    w_up_r = w_up.rearrange("a (k p) n -> p (a k) n", p=P)
    w_down_r = w_down.rearrange("a (k p) n -> p (a k) n", p=P)

    R_DW, R_DWB = 0, TAPS31
    R_C4 = R_DWB + 1
    R_C4B = R_C4 + TAPS4
    R_BA, R_BX, R_LAM, R_LNG, R_LNB, R_ONL, R_ONC = range(R_C4B + 1, R_C4B + 8)
    NR = R_ONC + 1

    d_scr = nc.dram_tensor("d_scr", [NJ, P, S], F32).ap()
    y_scr = nc.dram_tensor("y_scr", [NJ, P, S], F32).ap()
    hhi_scr = nc.dram_tensor("hhi_scr", [P, KD, HALF], F32).ap()
    hlo_scr = nc.dram_tensor("hlo_scr", [P, KD, HALF], F32).ap()
    x2_scr = nc.dram_tensor("x2_scr", [TPH, P, D], F32).ap()

    with ExitStack() as ctx:
        base = (nc.sbuf_base + 63) // 64 * 64

        def at(name, shape, dt, offset):
            return nc.alloc_sbuf_tensor_at(name, shape, dt, offset=base + offset)

        def sem(name):
            return ctx.enter_context(nc.semaphore(name))

        h_hi = at("h_hi", [P, KD, HALF], F32R, 0)
        h_lo = at("h_lo", [P, KD, HALF], F32R, 32 * KIB)
        w_hi = [at(f"w_hi{s}", [P, 2, KD, P], F32R, (64 + 16 * s) * KIB) for s in range(2)]
        w_lo = [at(f"w_lo{s}", [P, 2, KD, P], F32R, (72 + 16 * s) * KIB) for s in range(2)]
        wo_hi = at("wo_hi", [P, KD, D], F32R, 64 * KIB)
        wo_lo = at("wo_lo", [P, KD, D], F32R, 96 * KIB)
        wd_hi = at("wd_hi", [P, 2, D], F32R, 96 * KIB)
        wd_lo = at("wd_lo", [P, 2, D], F32R, 104 * KIB)
        f_hi = [at(f"f_hi{b}", [P, HALF], F32R, (112 + 4 * b) * KIB) for b in range(2)]
        f_lo = [at(f"f_lo{b}", [P, HALF], F32R, (120 + 4 * b) * KIB) for b in range(2)]
        w_raw = [at(f"w_raw{s}", [P, 2, KD, P], F32, (128 + 8 * s) * KIB) for s in range(2)]
        wd_raw = at("wd_raw", [P, 2, D], F32, 144 * KIB)
        y_raw = [at(f"y_raw{s}", [P, KD, P], F32, (144 + 4 * s) * KIB) for s in range(2)]
        y_hi = [at(f"y_hi{s}", [P, KD, P], F32R, (152 + 8 * s) * KIB) for s in range(2)]
        y_lo = [at(f"y_lo{s}", [P, KD, P], F32R, (156 + 8 * s) * KIB) for s in range(2)]
        act_gate = [at(f"act_gate{n}", [P, TILE], F32, (152 + 2 * n) * KIB) for n in range(4)]
        x2 = at("x2", [P, TPH, D], F32, 168 * KIB)
        gel = [at(f"gel{s}", [P, HALF], F32, (96 + 4 * s) * KIB) for s in range(2)]
        cv = [at(f"cv{s}", [P, HALF], F32, (104 + 4 * s) * KIB) for s in range(2)]
        c_hi = at("c_hi", [P, HALF], F32R, 112 * KIB)
        c_lo = at("c_lo", [P, HALF], F32R, 116 * KIB)
        gw_hi = at("gw_hi", [P, NJ, 2, P], F32R, 120 * KIB)
        gw_lo = at("gw_lo", [P, NJ, 2, P], F32R, 124 * KIB)
        uw = at("uw", [P, HALF], F32, 144 * KIB)
        su = at("su", [P, HALF], F32, 148 * KIB)
        ib = at("ib", [P, HALF], F32, 152 * KIB)
        sg = at("sg", [P, HALF], F32, 156 * KIB)
        dst = [at(f"dst{s}", [P, HALF], F32, (160 + 4 * s) * KIB) for s in range(2)]
        xt = [at(f"xt{s}", [P, D], F32, (168 + 4 * s) * KIB) for s in range(3)]
        gw_raw = at("gw_raw", [P, NJ, 2, P], F32, 180 * KIB)
        xl = at("xl", [P, HALF + 32], F32, 184 * KIB)
        glu = [at(f"glu{s}", [P, HALF + 32], F32, 184 * KIB + 4224 * (1 + s)) for s in range(2)]
        nd = [at(f"nd{s}", [P, NJ, TILE], F32, (144 + 26 * s) * KIB) for s in range(2)]
        ny = [at(f"ny{s}", [P, NJ, TILE], F32, (152 + 26 * s) * KIB) for s in range(2)]
        nsq = [at(f"nsq{s}", [P, NJ, TILE], F32, (160 + 26 * s) * KIB) for s in range(2)]
        nrs = [at(f"nrs{s}", [P, TILE], F32, (168 + 26 * s) * KIB) for s in range(2)]
        g_row = at("g_row", [P, D], F32, 200 * KIB)
        gfin = at("gfin", [P, D], F32, 204 * KIB)
        hn = [at(f"hn{s}", [P, D], F32, (208 + 4 * s) * KIB) for s in range(2)]
        junk = at("junk", [P, D], BF16, 216 * KIB)
        o = 218 * KIB

        def small(name, n, dt=F32):
            nonlocal o
            t = at(name, [P, n], dt, o)
            o += (4 * n + 31) // 32 * 32
            return t

        ident = small("ident", P)
        mean_w = small("mean_w", P)
        par = small("par", NJ * NR)
        rate = small("rate", NJ)
        sp = [small(f"sp{n}", NJ) for n in range(4)]
        ssq = small("ssq", NT)
        rstd = small("rstd", NT)
        rms = small("rms", 2 * NT)
        xh = small("xh", NJ * PAD4)
        gh = small("gh", NJ * PAD31)
        hl = small("hl", NJ)
        eps = small("eps", 1)
        assert base + o <= nc.sbuf_usable_end, (base, o)
        par_rows = hn[0]

        def col(j, r):
            return par[:, j * NR + r:j * NR + r + 1]

        ps = [ctx.enter_context(nc.psum_tensor(f"ps{b}", [P, TILE], F32)) for b in range(4)]
        acc = ctx.enter_context(nc.psum_tensor("acc", [P, HALF], F32))
        ps += [acc[:, 0:TILE], acc[:, TILE:HALF]]
        ps += [ctx.enter_context(nc.psum_tensor(f"ps{b}", [P, TILE], F32)) for b in (6, 7)]
        ps = [b[:, :] for b in ps]
        f32 = lambda ap: ap.bitcast(F32)

        s_par = sem("par_loaded")
        s_gw = sem("gate_weights_loaded")
        s_gmix = sem("g_row_loaded")
        s_gfin = sem("gfin_loaded")
        s_init = sem("pool_constants")
        s_part = sem("par_transposed")
        s_parc = sem("par_copied")
        s_rate = sem("rate_ready")
        s_dve = sem("dve_step")
        s_act = sem("act_step")
        s_gws = sem("gate_weights_split")
        s_x = [sem(f"x_loaded{s}") for s in range(3)]
        s_std = sem("std_ready")
        s_xn = sem("x_normed")
        s_hhi = sem("h_hi_ready")
        s_hlo = sem("h_lo_ready")
        s_aux_done = [sem(f"aux_done{b}") for b in range(2)]
        s_rr = sem("r_ready")
        s_w = [sem(f"w_loaded{s}") for s in range(2)]
        s_whi = sem("w_hi_ready")
        s_wlo = sem("w_lo_ready")
        s_pair = [sem(f"pair_done{b}") for b in range(4)]
        s_free = [sem(f"pair_free{b}") for b in range(4)]
        s_tap0 = sem("tap0_done")
        s_conv4 = sem("conv4_done")
        s_chi = sem("c_hi_ready")
        s_clo = sem("c_lo_ready")
        s_glu = sem("glu_done")
        s_conv31 = sem("conv31_done")
        s_dcopy = sem("d_copied")
        s_ir = sem("i_ready")
        s_uw = sem("uw_ready")
        s_ic = sem("ic_done")
        s_fin = sem("unit_final")
        s_dst = [sem(f"d_stored{s}") for s in range(2)]
        s_yst = [sem(f"y_stored{s}") for s in range(2)]
        s_nld = [sem(f"norm_loaded{s}") for s in range(2)]
        s_mean = sem("mean_done")
        s_dc = sem("centred")
        s_sq = sem("squares_ready")
        s_var = sem("var_done")
        s_nstd = sem("ln_std")
        s_dn = sem("ln_scaled")
        s_ysw = sem("swish_done")
        s_sq2 = sem("squares2_ready")
        s_sqy = sem("squares_lru_ready")
        s_rm1 = sem("rms_cm_done")
        s_rm2 = sem("rms_lru_done")
        s_rstd8 = sem("rms_std")
        s_rms = sem("rms_ready")
        s_yswst = [sem(f"swish_stored{s}") for s in range(2)]
        s_yl = [sem(f"y_loaded{s}") for s in range(2)]
        s_yhi = sem("y_hi_ready")
        s_ylo = sem("y_lo_ready")
        s_out = [sem(f"out_bank_done{b}") for b in range(4)]
        s_outf = [sem(f"out_bank_read{b}") for b in range(4)]
        s_xr = [sem(f"residual_loaded{n}") for n in range(4)]
        s_tr = [sem(f"turned{b}") for b in range(2)]
        s_trf = [sem(f"turned_read{b}") for b in range(2)]
        s_std2 = sem("std2_ready")
        s_hn = sem("hn_ready")
        s_h2hi = sem("h2_hi_ready")
        s_h2lo = sem("h2_lo_ready")
        s_h2st = [sem(f"h2_stored{n}") for n in range(2)]
        s_x2st = [sem(f"x2_stored{n}") for n in range(2)]
        s_wd = sem("w_down_loaded")
        s_wdhi = sem("wd_hi_ready")
        s_wdlo = sem("wd_lo_ready")
        s_fhi = sem("f_hi_ready")
        s_flo = sem("f_lo_ready")
        s_h2ld = sem("h2_reloaded")
        s_x2ld = sem("x2_reloaded")
        s_fsq = sem("final_squares")
        s_fstd = sem("final_std")
        s_o = sem("out_row_ready")
        s_ost = [sem(f"out_stored{n}") for n in range(2)]

        ORDER = list(range(TPH, NT)) + list(range(TPH))

        def aux_x(g):
            return g if g < TPH else g + NS * NJ

        def aux_g(u, st):
            return TPH * (1 + u // NJ) + NS * u + st

        AUX_USES = NT + NS * UNITS

        block = ctx.enter_context(nc.Block())

        @block.sync
        def _(sp_):
            def load_pair_from(q, a, b):
                sp_.dma_start(w_raw[q % 2][:, 0], a).then_inc(s_w[q % 2], 16)
                sp_.dma_start(w_raw[q % 2][:, 1], b).then_inc(s_w[q % 2], 16)

            def load_pair(q):
                u, which = divmod(q, 2)
                j = u % NJ
                if q >= 2:
                    sp_.wait_ge(s_wlo, q - 1)
                c0 = 2 * CH * which + j * P
                load_pair_from(q, w_in_r[:, :, c0:c0 + P], w_in_r[:, :, c0 + CH:c0 + CH + P])

            def load_x(g):
                if g >= 3:
                    sp_.wait_ge(s_aux_done[1], aux_x(g - 3) + 1)
                sp_.dma_start(xt[g % 3][:, :], xr[g]).then_inc(s_x[g % 3], 16)

            def store_unit(u):
                h, j = divmod(u, NJ)
                sp_.wait_ge(s_fin, u + 1)
                sp_.dma_start(y_scr[j, :, h * HALF:(h + 1) * HALF], gel[u % 2][:, :]).then_inc(s_yst[u % 2], 16)
                sp_.wait_ge(s_dcopy, u + 1)
                sp_.dma_start(d_scr[j, :, h * HALF:(h + 1) * HALF], dst[u % 2][:, :]).then_inc(s_dst[u % 2], 16)

            load_x(0)
            sp_.dma_start(g_row[:, :], norm_mix.broadcast_to([P, D])).then_inc(s_gmix, 16)
            load_x(1)
            load_pair(0)
            load_x(2)
            rows = [(dw31_w[0], R_DW, TAPS31), (dw31_b, R_DWB, 1), (conv4_w[0], R_C4, TAPS4), (conv4_b, R_C4B, 1),
                    (gate_a_b, R_BA, 1), (gate_x_b, R_BX, 1), (lru_lambda, R_LAM, 1), (cm_ln_g, R_LNG, 1),
                    (cm_ln_b, R_LNB, 1), (out_norm_lru, R_ONL, 1), (out_norm_cm, R_ONC, 1)]
            for src, r, n in rows:
                sp_.dma_start(par_rows[r:r + n, 0:CH], src).then_inc(s_par, 16)
            sp_.wait_ge(s_init, 1)
            for g, w in enumerate((gate_a_w, gate_x_w)):
                for b in range(P // HD):
                    sp_.dma_start(gw_raw[b * HD:(b + 1) * HD, :, g, b * HD:(b + 1) * HD],
                                  w[0].rearrange("(j b) i o -> b i j o", b=P // HD)[b]).then_inc(s_gw, 16)
            for g in range(3, TPH):
                load_x(g)
                if g == 4:
                    load_pair(1)
            for u in range(UNITS):
                for q in (2 * u + 2, 2 * u + 3):
                    if q < PPAIRS:
                        load_pair(q)
                if u >= 1:
                    store_unit(u - 1)
                if u == NJ - 2:
                    for g in range(TPH, TPH + 3):
                        load_x(g)
                if u == NJ - 1:
                    for g in range(TPH + 3, NT):
                        load_x(g)
            for n in range(WOQ):
                q = PPAIRS + n
                sp_.wait_ge(s_wlo, q - 1)
                for e in range(2):
                    sp_.dma_start(w_raw[q % 2][:, e].rearrange("p k c -> p (k c)"),
                                  w_out_r[:, 2 * n + e]).then_inc(s_w[q % 2], 16)
                if n == 1:
                    store_unit(UNITS - 1)
                    sp_.wait_ge(s_hlo, 2 * NT)
                    sp_.dma_start(g_row[:, :], norm_ffn.broadcast_to([P, D])).then_inc(s_gmix, 16)
                    sp_.dma_start(gfin[:, :], norm_final.rearrange("(a d) -> a d", a=1).broadcast_to([P, D])
                                  ).then_inc(s_gfin, 16)
                    for s in range(2):
                        sp_.wait_ge(s_dst[s], 16 * UNITS // 2)
                        sp_.wait_ge(s_yst[s], 16 * UNITS // 2)
                    for m in range(2):
                        cols = slice(m * TILE, (m + 1) * TILE)
                        sp_.dma_start(nd[m][:, :, :], d_scr[:, :, cols].rearrange("j p s -> p j s")).then_inc(s_nld[m], 16)
                        sp_.dma_start(ny[m][:, :, :], y_scr[:, :, cols].rearrange("j p s -> p j s")).then_inc(s_nld[m], 16)
            for m in range(S // TILE):
                cols = slice(m * TILE, (m + 1) * TILE)
                sp_.wait_ge(s_ysw, NJ * (m + 1))
                sp_.dma_start(d_scr[:, :, cols].rearrange("j p s -> p j s"), nd[m % 2][:, :, :]).then_inc(s_yswst[m % 2], 16)
                if m + 2 < S // TILE:
                    cols = slice((m + 2) * TILE, (m + 3) * TILE)
                    sp_.wait_ge(s_yswst[m % 2], 16 * (m // 2 + 1))
                    sp_.wait_ge(s_rm1, m + 1)
                    sp_.wait_ge(s_rm2, m + 1)
                    sp_.dma_start(nd[m % 2][:, :, :], d_scr[:, :, cols].rearrange("j p s -> p j s")).then_inc(s_nld[m % 2], 16)
                    sp_.dma_start(ny[m % 2][:, :, :], y_scr[:, :, cols].rearrange("j p s -> p j s")).then_inc(s_nld[m % 2], 16)
            for s in range(2):
                sp_.wait_ge(s_yswst[s], 16 * (S // TILE) // 2)
            sp_.wait_ge(s_rms, S // TILE)

            def load_y(w):
                g = ORDER[w]
                if w >= 2:
                    sp_.wait_ge(s_ylo, w - 1)
                cols = slice(g * P, (g + 1) * P)
                sp_.dma_start(y_raw[w % 2][:, 0:NJ], y_scr[:, :, cols].rearrange("j p s -> p j s")).then_inc(s_yl[w % 2], 16)
                sp_.dma_start(y_raw[w % 2][:, NJ:KD], d_scr[:, :, cols].rearrange("j p s -> p j s")).then_inc(s_yl[w % 2], 16)

            def load_residual(w):
                i = w % TPH
                if w >= TPH:
                    sp_.wait_ge(s_x2st[i % 2], 16 * (i // 2 + 1))
                sp_.dma_start(x2[:, i], xr[ORDER[w]]).then_inc(s_xr[w % 4], 16)

            def store_h2(w):
                i = w
                cols = slice(i * P, (i + 1) * P)
                sp_.wait_ge(s_hn, w + 1)
                sp_.dma_start(x2_scr[i], x2[:, i]).then_inc(s_x2st[i % 2], 16)
                sp_.wait_ge(s_h2lo, 2 * (w + 1))
                sp_.dma_start(hhi_scr[:, :, cols], f32(h_hi[:, :, cols])).then_inc(s_h2st[i % 2], 16)
                sp_.dma_start(hlo_scr[:, :, cols], f32(h_lo[:, :, cols])).then_inc(s_h2st[i % 2], 16)

            for w in range(4):
                load_residual(w)
            for w in range(2):
                load_y(w)
            for w in range(NT):
                if w + 2 < NT:
                    load_y(w + 2)
                if 1 <= w <= TPH:
                    store_h2(w - 1)
                if w + 4 < NT:
                    load_residual(w + 4)

            def load_ffn(q, b, f0):
                load_pair_from(q, w_gate_r[:, :, f0], w_up_r[:, :, f0])

            Q0 = PPAIRS + WOQ
            for b in range(2):
                sp_.wait_ge(s_wlo, Q0 + b - 1)
                load_ffn(Q0 + b, b, slice(b * P, (b + 1) * P))
            sp_.wait_ge(s_ylo, NT)
            sp_.dma_start(wd_raw[:, :, :], w_down_r[:, 0:2]).then_inc(s_wd, 16)
            for h in range(NH):
                with sp_.Fori(0, FI - 1) as i:
                    for b in range(2):
                        sp_.wait_ge(s_wlo, Q0 + 2 * FI * h + b + 1 + 2 * i)
                        load_ffn(b, b, bass.ds((i + 1) * (2 * P) + b * P, P))
                    sp_.wait_ge(s_wdlo, FI * h + 1 + i)
                    sp_.dma_start(wd_raw[:, :, :], w_down_r[:, bass.ds((i + 1) * 2, 2)]).then_inc(s_wd, 16)
                for b in range(2):
                    sp_.wait_ge(s_wlo, Q0 + 2 * FI * (h + 1) + b - 1)
                    load_ffn(b, b, slice(b * P, (b + 1) * P))
                sp_.wait_ge(s_wdlo, FI * (h + 1))
                sp_.dma_start(wd_raw[:, :, :], w_down_r[:, 0:2]).then_inc(s_wd, 16)
                if h + 1 < NH:
                    for n in range(2):
                        sp_.wait_ge(s_h2st[n], 16 * TPH)
                    sp_.wait_ge(s_pair[3], PPAIRS + 2 * FI * (h + 1))
                    for k in range(KD):
                        sp_.dma_start(f32(h_hi[:, k]), hhi_scr[:, k]).then_inc(s_h2ld, 16)
                        sp_.dma_start(f32(h_lo[:, k]), hlo_scr[:, k]).then_inc(s_h2ld, 16)
                for i in range(TPH):
                    n = h * TPH + i
                    sp_.wait_ge(s_o, n + 1)
                    sp_.dma_start(outr[n], hn[n % 2][:, :]).then_inc(s_ost[n % 2], 16)
                    if h + 1 < NH:
                        sp_.dma_start(x2[:, i], x2_scr[i]).then_inc(s_x2ld, 16)
            for n in range(2):
                sp_.wait_ge(s_ost[n], 16 * NT // 2)

        @block.gpsimd
        def _(pool):
            g = nc.gpsimd
            g.memset(gw_raw[:, :, :, :], 0.0).then_inc(s_init, 1)
            g.memset(ident[:, :], 0.0).then_inc(s_init, 1)
            g.memset(mean_w[:, :], 1.0 / CH).then_inc(s_init, 1)
            g.memset(eps[:, :], EPS).then_inc(s_init, 1)
            g.memset(xl[:, 0:PAD4], 0.0).then_inc(s_init, 1)
            g.memset(glu[0][:, 0:PAD31], 0.0).then_inc(s_init, 1)
            g.memset(glu[1][:, 0:PAD31], 0.0).then_inc(s_init, 1)
            pool.wait_ge(s_init, 7)
            g.affine_select(out=ident[:, :], in_=ident[:, :], compare_op=ALU.not_equal, fill=1.0, base=0,
                            pattern=[[-1, P]], channel_multiplier=1).then_inc(s_init, 1)

            def split_lo(q):
                pool.wait_ge(s_whi, q + 1)
                g.tensor_tensor(w_lo[q % 2][:, :, :, :], w_raw[q % 2][:, :, :, :], f32(w_hi[q % 2][:, :, :, :]),
                                ALU.subtract).then_inc(s_wlo, 1)

            split_lo(0)
            split_lo(1)
            for u in range(UNITS):
                h, j = divmod(u, NJ)
                s = u % 2
                if 2 * u + 2 < PPAIRS:
                    split_lo(2 * u + 2)
                for st in range(NS):
                    t = glu[s][:, PAD31 + st * TILE:PAD31 + (st + 1) * TILE]
                    pool.wait_ge(s_free[2 * st], 2 * u + 2)
                    pool.wait_ge(s_free[2 * st + 1], 2 * u + 2)
                    g.tensor_tensor(t, t, sg[:, st * TILE:(st + 1) * TILE], ALU.mult).then_inc(s_glu, 1)
                halo = gh[:, j * PAD31:(j + 1) * PAD31]
                if h == 0:
                    pool.wait_ge(s_glu, (NS + 1) * u + NS)
                    g.tensor_copy(halo, glu[s][:, HALF:HALF + PAD31]).then_inc(s_glu, 1)
                else:
                    pool.wait_ge(s_conv31, u - 1)
                    g.tensor_copy(glu[s][:, 0:PAD31], halo).then_inc(s_glu, 1)
                if 2 * u + 3 < PPAIRS:
                    split_lo(2 * u + 3)
                pool.wait_ge(s_chi, u + 1)
                g.tensor_tensor(c_lo[:, :], cv[s][:, :], f32(c_hi[:, :]), ALU.subtract).then_inc(s_clo, 1)
                pool.wait_ge(s_ir, NS * (u + 1))
                pool.wait_ge(s_clo, u + 1)
                g.tensor_tensor(cv[s][:, :], cv[s][:, :], ib[:, :], ALU.mult).then_inc(s_ic, 1)
            for n in range(WOQ):
                q = PPAIRS + n
                pool.wait_ge(s_whi, q + 1)
                g.tensor_tensor(wo_lo[:, 2 * n:2 * n + 2, :], w_raw[q % 2][:, :, :, :].rearrange("p e k c -> p e (k c)"),
                                f32(wo_hi[:, 2 * n:2 * n + 2, :]), ALU.subtract).then_inc(s_wlo, 1)
            for w in range(NT):
                pool.wait_ge(s_yhi, w + 1)
                g.tensor_tensor(y_lo[w % 2][:, :, :], y_raw[w % 2][:, :, :], f32(y_hi[w % 2][:, :, :]),
                                ALU.subtract).then_inc(s_ylo, 1)
            Q0 = PPAIRS + WOQ

            def split_down(count):
                pool.wait_ge(s_wdhi, count)
                g.tensor_tensor(wd_lo[:, :, :], wd_raw[:, :, :], f32(wd_hi[:, :, :]), ALU.subtract).then_inc(s_wdlo, 1)

            def split_ffn(b, count):
                pool.wait_ge(s_whi, count)
                g.tensor_tensor(w_lo[b][:, :, :, :], w_raw[b][:, :, :, :], f32(w_hi[b][:, :, :, :]),
                                ALU.subtract).then_inc(s_wlo, 1)

            split_ffn(0, Q0 + 1)
            split_ffn(1, Q0 + 2)
            split_down(1)
            with pool.Fori(0, NH * FI) as i:
                split_ffn(0, Q0 + 3 + 2 * i)
                split_ffn(1, Q0 + 4 + 2 * i)
                split_down(2 + i)

        @block.scalar
        def _(act):
            a = nc.scalar
            steps = [0]

            def step(ins):
                steps[0] += 1
                ins.then_inc(s_act, 1)
                act.wait_ge(s_act, steps[0])

            def split_hi(q):
                act.wait_ge(s_w[q % 2], 32 * (q // 2 + 1))
                if q >= 2:
                    act.wait_ge(s_pair[3], q - 1)
                a.copy(w_hi[q % 2][:, :, :, :], w_raw[q % 2][:, :, :, :]).then_inc(s_whi, 1)

            def x_std(g):
                act.wait_ge(s_x[g % 3], 16 * (g // 3 + 1))
                step(a.activation(junk[:, :], xt[g % 3][:, :], ACT.Square, accum_out=ssq[:, g:g + 1]))
                a.activation(rstd[:, g:g + 1], ssq[:, g:g + 1], ACT.Sqrt, bias=eps[:, 0:1], scale=1.0 / D).then_inc(s_std, 1)

            def x_hi(g):
                i = g % TPH
                for b in range(2):
                    act.wait_ge(s_aux_done[b], aux_x(g) + 1)
                    if g == TPH and b == 0:
                        act.wait_ge(s_pair[3], PPAIRS // NH)
                    a.copy(h_hi[:, 4 * b:4 * b + 4, i * P:(i + 1) * P],
                           ps[6 + b].rearrange("p (k s) -> p k s", k=4)).then_inc(s_hhi, 1)

            def x_half(h):
                for g in range(h * TPH, (h + 1) * TPH):
                    x_std(g)
                    if g > h * TPH:
                        x_hi(g - 1)
                x_hi((h + 1) * TPH - 1)

            def copy_d(u):
                act.wait_ge(s_conv31, u + 1)
                if u >= 2:
                    act.wait_ge(s_dst[u % 2], 16 * (u // 2))
                a.copy(dst[u % 2][:, :], acc[:, :]).then_inc(s_dcopy, 1)

            act.wait_ge(s_init, 8)
            x_std(0)
            split_hi(0)
            act.wait_ge(s_parc, 2)
            a.activation(sp[1][:, :], sp[0][:, :], ACT.Exp).then_inc(s_rate, 1)
            act.wait_ge(s_gw, 16 * 4)
            a.copy(gw_hi[:, :, :, :], gw_raw[:, :, :, :]).then_inc(s_gws, 1)
            for g in range(1, TPH):
                x_std(g)
                x_hi(g - 1)
                if g == 3:
                    split_hi(1)
            x_hi(TPH - 1)
            for u in range(UNITS):
                h, j = divmod(u, NJ)
                s = u % 2
                halo = xh[:, j * PAD4:(j + 1) * PAD4]
                for st in range(NS):
                    cols = slice(st * TILE, (st + 1) * TILE)
                    act.wait_ge(s_pair[2 * st], 2 * u + 1)
                    if st == 0 and u >= 1:
                        act.wait_ge(s_conv4, u)
                    a.copy(xl[:, PAD4 + st * TILE:PAD4 + (st + 1) * TILE], ps[2 * st]).then_inc(s_free[2 * st], 1)
                    act.wait_ge(s_pair[2 * st + 1], 2 * u + 1)
                    if st == 0 and u >= 2:
                        act.wait_ge(s_yst[s], 16 * (u // 2))
                    a.activation(gel[s][:, cols], ps[2 * st + 1], ACT.Gelu_apprx_tanh).then_inc(s_free[2 * st + 1], 1)
                if h == 0:
                    act.wait_ge(s_free[2], 2 * u + 1)
                    step(a.copy(halo, xl[:, HALF:HALF + PAD4]))
                else:
                    step(a.copy(xl[:, 0:PAD4], halo))
                act.wait_ge(s_free[2], 2 * u + 1)
                if u == 0:
                    act.wait_ge(s_parc, 1)
                if u >= 2:
                    act.wait_ge(s_fin, u - 1)
                a.activation(cv[s][:, :], xl[:, 0:HALF], ACT.Identity, scale=col(j, R_C4), bias=col(j, R_C4B)
                             ).then_inc(s_tap0, 1)
                if 2 * u + 2 < PPAIRS:
                    split_hi(2 * u + 2)
                for st in range(NS):
                    act.wait_ge(s_pair[2 * st], 2 * u + 2)
                    if st == 0 and u >= 2:
                        act.wait_ge(s_conv31, u - 1)
                        act.wait_ge(s_glu, (NS + 1) * (u - 1))
                    a.copy(glu[s][:, PAD31 + st * TILE:PAD31 + (st + 1) * TILE], ps[2 * st]).then_inc(s_free[2 * st], 1)
                    act.wait_ge(s_pair[2 * st + 1], 2 * u + 2)
                    if u >= 1:
                        act.wait_ge(s_glu, (NS + 1) * (u - 1) + st + 1)
                    a.activation(sg[:, st * TILE:(st + 1) * TILE], ps[2 * st + 1], ACT.Sigmoid
                                 ).then_inc(s_free[2 * st + 1], 1)
                if 2 * u + 3 < PPAIRS:
                    split_hi(2 * u + 3)
                if u >= 1:
                    copy_d(u - 1)
                act.wait_ge(s_conv4, u + 1)
                if u >= 1:
                    act.wait_ge(s_aux_done[1], aux_g(u - 1, NS - 1) + 1)
                a.copy(c_hi[:, :], cv[s][:, :]).then_inc(s_chi, 1)
                for st in range(NS):
                    cols = slice(st * TILE, (st + 1) * TILE)
                    act.wait_ge(s_aux_done[0], aux_g(u, st) + 1)
                    if st == 0 and u >= 1:
                        act.wait_ge(s_fin, u)
                    a.activation(uw[:, cols], ps[6], ACT.Sigmoid, bias=col(j, R_BA)).then_inc(s_rr, 1)
                    act.wait_ge(s_aux_done[1], aux_g(u, st) + 1)
                    if st == 0 and u >= 1:
                        act.wait_ge(s_ic, u)
                    a.activation(ib[:, cols], ps[7], ACT.Sigmoid, bias=col(j, R_BX)).then_inc(s_ir, 1)
                act.wait_ge(s_rr, NS * (u + 1))
                if u == 0:
                    act.wait_ge(s_rate, 2)
                step(a.activation(uw[:, :], uw[:, :], ACT.Tanh, scale=rate[:, j:j + 1]))
                step(a.activation(su[:, :], uw[:, :], ACT.Sqrt))
                a.activation(uw[:, :], uw[:, :], ACT.Identity, bias=1.0).then_inc(s_uw, 1)
                if u == NJ - 1:
                    x_half(1)
            copy_d(UNITS - 1)

            for n in range(WOQ):
                q = PPAIRS + n
                act.wait_ge(s_w[q % 2], 32 * (q // 2 + 1))
                if n == 0:
                    act.wait_ge(s_pair[3], PPAIRS)
                    act.wait_ge(s_fin, UNITS)
                    for s in range(2):
                        act.wait_ge(s_yst[s], 16 * UNITS // 2)
                for e in range(2):
                    k = 2 * n + e
                    gain = col(k % NJ, R_ONL if k < NJ else R_ONC)
                    t = w_raw[q % 2][:, e].rearrange("p k c -> p (k c)")
                    step(a.activation(t, t, ACT.Copy, scale=gain))
                a.copy(wo_hi[:, 2 * n:2 * n + 2, :], w_raw[q % 2][:, :, :, :].rearrange("p e k c -> p e (k c)")
                       ).then_inc(s_whi, 1)

            for m0 in range(0, S // TILE, 2):
                for m in (m0, m0 + 1):
                    act.wait_ge(s_dc, m + 1)
                    a.activation(nsq[m % 2][:, :, :], nd[m % 2][:, :, :], ACT.Square).then_inc(s_sq, 1)
                for m in (m0, m0 + 1):
                    s = m % 2
                    act.wait_ge(s_var, m + 1)
                    a.activation(nrs[s][:, :], ps[1], ACT.Sqrt, bias=eps[:, 0:1]).then_inc(s_nstd, 1)
                for m in (m0, m0 + 1):
                    s = m % 2
                    act.wait_ge(s_dn, m + 1)
                    for j in range(NJ):
                        a.activation(nd[s][:, j], nd[s][:, j], ACT.Silu, scale=col(j, R_LNG), bias=col(j, R_LNB)
                                     ).then_inc(s_ysw, 1)
                    act.wait_ge(s_ysw, NJ * (m + 1))
                    a.activation(nsq[s][:, :, :], nd[s][:, :, :], ACT.Square).then_inc(s_sq2, 1)
                    act.wait_ge(s_rm1, m + 1)
                    a.activation(nsq[s][:, :, :], ny[s][:, :, :], ACT.Square).then_inc(s_sqy, 1)
                for m in (m0, m0 + 1):
                    act.wait_ge(s_rm2, m0 + 2)
                    a.activation(rms[:, 8 * m:8 * m + 8], ps[2][:, 8 * (m % 2):8 * (m % 2) + 8], ACT.Sqrt,
                                 bias=eps[:, 0:1]).then_inc(s_rstd8, 1)

            def y_split(w):
                act.wait_ge(s_yl[w % 2], 32 * (w // 2 + 1))
                if w == 0:
                    act.wait_ge(s_rms, S // TILE)
                if w >= 2:
                    act.wait_ge(s_out[3], w - 1)
                a.copy(y_hi[w % 2][:, :, :], y_raw[w % 2][:, :, :]).then_inc(s_yhi, 1)

            def h2_hi(w):
                i = w % TPH
                for b in range(2):
                    act.wait_ge(s_tr[b], w + 1)
                    if w >= TPH and b == 0:
                        act.wait_ge(s_h2st[i % 2], 32 * (i // 2 + 1))
                    a.copy(h_hi[:, 4 * b:4 * b + 4, i * P:(i + 1) * P],
                           ps[2 + b].rearrange("p (k s) -> p k s", k=4)).then_inc(s_h2hi, 1)

            y_split(0)
            for w in range(NT):
                if w + 1 < NT:
                    y_split(w + 1)
                if w >= 1:
                    h2_hi(w - 1)
                act.wait_ge(s_outf[3], w + 1)
                step(a.activation(junk[:, :], x2[:, w % TPH], ACT.Square, accum_out=ssq[:, w:w + 1]))
                a.activation(rstd[:, w:w + 1], ssq[:, w:w + 1], ACT.Sqrt, bias=eps[:, 0:1], scale=1.0 / D
                             ).then_inc(s_std2, 1)
            h2_hi(NT - 1)

            Q0 = PPAIRS + WOQ

            def ffn_hi(b, loaded, used):
                act.wait_ge(s_w[b], loaded)
                if used is not None:
                    act.wait_ge(s_pair[3], used)
                a.copy(w_hi[b][:, :, :, :], w_raw[b][:, :, :, :]).then_inc(s_whi, 1)

            def down_hi(loaded, used):
                act.wait_ge(s_wd, loaded)
                if used is not None:
                    act.wait_ge(s_out[3], used)
                a.copy(wd_hi[:, :, :], wd_raw[:, :, :]).then_inc(s_wdhi, 1)

            act.wait_ge(s_out[3], NT)
            for b in range(2):
                ffn_hi(b, 16 * (Q0 + 2), None)
            down_hi(16, None)
            for h in range(NH):
                with act.Fori(0, FI) as i:
                    for b in range(2):
                        pairs = PPAIRS + 2 * FI * h + b + 1
                        for st in range(NS):
                            n = 2 * b + st
                            act.wait_ge(s_pair[2 * st], pairs + 2 * i)
                            a.activation(act_gate[n][:, :], ps[2 * st], ACT.Silu).then_inc(s_free[2 * st], 1)
                            act.wait_ge(s_free[2 * st + 1], pairs + 2 * i)
                            if n % 2 == 0:
                                act.wait_ge(s_out[3], NT + 4 * FI * h + 4 * i)
                            a.copy(f_hi[b][:, st * TILE:(st + 1) * TILE], act_gate[n][:, :]).then_inc(s_fhi, 1)
                        ffn_hi(b, 16 * (Q0 + 2 * FI * h + 4) + 32 * i, pairs + 2 * i)
                    down_hi(16 * (FI * h + 2) + 16 * i, NT + 4 * (FI * h + 1) + 4 * i)
                for i in range(TPH):
                    if i == 0:
                        act.wait_ge(s_outf[3], NT + 4 * FI * (h + 1))
                        if h == 1:
                            act.wait_ge(s_o, TPH)
                    a.activation(junk[:, :], x2[:, i], ACT.Square, accum_out=ssq[:, i:i + 1]).then_inc(s_fsq, 1)
                    act.wait_ge(s_fsq, TPH * h + i + 1)
                a.activation(rstd[:, 0:TPH], ssq[:, 0:TPH], ACT.Sqrt, bias=eps[:, 0:1], scale=1.0 / D).then_inc(s_fstd, 1)

        @block.vector
        def _(dve):
            v = nc.vector
            steps = [0]

            def step(ins):
                steps[0] += 1
                ins.then_inc(s_dve, 1)
                dve.wait_ge(s_dve, steps[0])

            def x_norm(g):
                dve.wait_ge(s_std, g + 1)
                step(v.reciprocal(rstd[:, g:g + 1], rstd[:, g:g + 1]))
                if g == 0:
                    dve.wait_ge(s_gmix, 16)
                v.scalar_tensor_tensor(out=xt[g % 3][:, :], in0=xt[g % 3][:, :], scalar=rstd[:, g:g + 1],
                                       in1=g_row[:, :], op0=ALU.mult, op1=ALU.mult).then_inc(s_xn, 1)

            def x_lo(g):
                i = g % TPH
                for b in range(2):
                    dve.wait_ge(s_hhi, 2 * g + b + 1)
                    cols = slice(i * P, (i + 1) * P)
                    v.tensor_tensor(h_lo[:, 4 * b:4 * b + 4, cols], ps[6 + b].rearrange("p (k s) -> p k s", k=4),
                                    f32(h_hi[:, 4 * b:4 * b + 4, cols]), ALU.subtract).then_inc(s_hlo, 1)

            def parameters():
                dve.wait_ge(s_part, 1)
                v.tensor_copy(par[:, :], ps[0][:, 0:NJ * NR]).then_inc(s_parc, 1)
                dve.wait_ge(s_parc, 1)
                lam = par[:, R_LAM:NJ * NR:NR]
                step(v.tensor_scalar(sp[1][:, :], lam, -1.0, None, ALU.mult))
                v.tensor_tensor(sp[0][:, :], lam, sp[1][:, :], ALU.min).then_inc(s_parc, 1)

            def decay_rate():
                lam = par[:, R_LAM:NJ * NR:NR]
                e, z, z2, poly = sp[1], sp[0], sp[2], sp[3]
                dve.wait_ge(s_rate, 1)
                step(v.tensor_scalar(z[:, :], e[:, :], 2.0, None, ALU.add))
                step(v.reciprocal(z[:, :], z[:, :]))
                step(v.tensor_tensor(z[:, :], z[:, :], e[:, :], ALU.mult))
                step(v.tensor_tensor(z2[:, :], z[:, :], z[:, :], ALU.mult))
                top = 10
                step(v.tensor_scalar(poly[:, :], z2[:, :], 1.0 / (2 * top + 1), 1.0 / (2 * top - 1), ALU.mult, ALU.add))
                for n in range(top - 2, -1, -1):
                    step(v.tensor_tensor(poly[:, :], poly[:, :], z2[:, :], ALU.mult))
                    step(v.tensor_scalar(poly[:, :], poly[:, :], 1.0 / (2 * n + 1), None, ALU.add))
                step(v.tensor_tensor(poly[:, :], poly[:, :], z[:, :], ALU.mult))
                step(v.tensor_scalar(z2[:, :], lam, -1.0, 0.0, ALU.mult, ALU.max))
                step(v.scalar_tensor_tensor(out=poly[:, :], in0=poly[:, :], scalar=2.0, in1=z2[:, :],
                                            op0=ALU.mult, op1=ALU.add))
                v.tensor_scalar(rate[:, :], poly[:, :], LRU_C / 2, None, ALU.mult).then_inc(s_rate, 1)

            def gate_weights_lo():
                dve.wait_ge(s_gws, 1)
                v.tensor_tensor(gw_lo[:, :, :, :], gw_raw[:, :, :, :], f32(gw_hi[:, :, :, :]), ALU.subtract
                                ).then_inc(s_gws, 1)

            x_norm(0)
            parameters()
            decay_rate()
            gate_weights_lo()
            for g in range(1, TPH):
                x_norm(g)
                x_lo(g - 1)
            x_lo(TPH - 1)

            def conv31(u, taps):
                h, j = divmod(u, NJ)
                t = glu[u % 2]
                for k in taps:
                    if k == 0:
                        dve.wait_ge(s_glu, (NS + 1) * (u + 1))
                        if u >= 1:
                            dve.wait_ge(s_dcopy, u)
                        step(v.tensor_scalar(acc[:, :], t[:, 0:HALF], col(j, R_DW), col(j, R_DWB), ALU.mult, ALU.add))
                        continue
                    ins = v.scalar_tensor_tensor(out=acc[:, :], in0=t[:, k:k + HALF], scalar=col(j, R_DW + k),
                                                 in1=acc[:, :], op0=ALU.mult, op1=ALU.add)
                    if k == TAPS31 - 1:
                        ins.then_inc(s_conv31, 1)
                    else:
                        step(ins)

            for u in range(UNITS):
                h, j = divmod(u, NJ)
                s = u % 2
                dve.wait_ge(s_tap0, u + 1)
                for k in range(1, TAPS4):
                    ins = v.scalar_tensor_tensor(out=cv[s][:, :], in0=xl[:, k:k + HALF], scalar=col(j, R_C4 + k),
                                                 in1=cv[s][:, :], op0=ALU.mult, op1=ALU.add)
                    if k == TAPS4 - 1:
                        ins.then_inc(s_conv4, 1)
                    else:
                        step(ins)
                if u == NJ - 1:
                    conv31(u, range(TAPS31 // 2))
                    for g in range(TPH, NT):
                        x_norm(g)
                        if g > TPH:
                            x_lo(g - 1)
                    x_lo(NT - 1)
                    conv31(u, range(TAPS31 // 2, TAPS31))
                else:
                    conv31(u, range(TAPS31))
                dve.wait_ge(s_uw, u + 1)
                step(v.reciprocal(uw[:, :], uw[:, :]))
                step(v.scalar_tensor_tensor(out=su[:, :], in0=su[:, :], scalar=2.0, in1=uw[:, :],
                                            op0=ALU.mult, op1=ALU.mult))
                step(v.tensor_scalar(uw[:, :], uw[:, :], 2.0, -1.0, ALU.mult, ALU.add))
                dve.wait_ge(s_ic, u + 1)
                step(v.tensor_tensor(su[:, :], su[:, :], cv[s][:, :], ALU.mult))
                step(v.tensor_tensor_scan(cv[s][:, :], uw[:, :], su[:, :], 0.0 if h == 0 else hl[:, j:j + 1],
                                          ALU.mult, ALU.add))
                if h == 0:
                    step(v.tensor_copy(hl[:, j:j + 1], cv[s][:, HALF - 1:HALF]))
                v.tensor_tensor(gel[s][:, :], gel[s][:, :], cv[s][:, :], ALU.mult).then_inc(s_fin, 1)

            for m0 in range(0, S // TILE, 2):
                for m in (m0, m0 + 1):
                    s = m % 2
                    dve.wait_ge(s_mean, m + 1)
                    v.tensor_tensor(nd[s][:, :, :], nd[s][:, :, :], ps[0][:, None, :].broadcast_to([P, NJ, TILE]),
                                    ALU.subtract).then_inc(s_dc, 1)
                for m in (m0, m0 + 1):
                    s = m % 2
                    dve.wait_ge(s_nstd, m + 1)
                    step(v.reciprocal(nrs[s][:, :], nrs[s][:, :]))
                    dve.wait_ge(s_sq, m + 1)
                    v.tensor_tensor(nd[s][:, :, :], nd[s][:, :, :], nrs[s][:, None, :].broadcast_to([P, NJ, TILE]),
                                    ALU.mult).then_inc(s_dn, 1)
                for m in (m0, m0 + 1):
                    dve.wait_ge(s_rstd8, m + 1)
                    v.reciprocal(rms[:, 8 * m:8 * m + 8], rms[:, 8 * m:8 * m + 8]).then_inc(s_rms, 1)
            dve.wait_ge(s_rms, S // TILE)

            def h2_lo(w):
                i = w % TPH
                cols = slice(i * P, (i + 1) * P)
                for b in range(2):
                    dve.wait_ge(s_h2hi, 2 * w + b + 1)
                    v.tensor_tensor(h_lo[:, 4 * b:4 * b + 4, cols], ps[2 + b].rearrange("p (k s) -> p k s", k=4),
                                    f32(h_hi[:, 4 * b:4 * b + 4, cols]), ALU.subtract).then_inc(s_h2lo, 1)

            for w in range(NT):
                i, g = w % TPH, ORDER[w]
                dve.wait_ge(s_xr[w % 4], 16 * (w // 4 + 1))
                for dh in range(2):
                    cols = slice(dh * TILE, (dh + 1) * TILE)
                    dve.wait_ge(s_out[2 * dh], w + 1)
                    v.scalar_tensor_tensor(out=x2[:, i, cols], in0=ps[4 + 2 * dh], scalar=rms[:, 2 * g:2 * g + 1],
                                           in1=x2[:, i, cols], op0=ALU.mult, op1=ALU.add).then_inc(s_outf[2 * dh], 1)
                    dve.wait_ge(s_out[2 * dh + 1], w + 1)
                    dve.wait_ge(s_outf[2 * dh], w + 1)
                    v.scalar_tensor_tensor(out=x2[:, i, cols], in0=ps[5 + 2 * dh], scalar=rms[:, 2 * g + 1:2 * g + 2],
                                           in1=x2[:, i, cols], op0=ALU.mult, op1=ALU.add).then_inc(s_outf[2 * dh + 1], 1)
                if w >= 1:
                    h2_lo(w - 1)
                dve.wait_ge(s_std2, w + 1)
                step(v.reciprocal(rstd[:, w:w + 1], rstd[:, w:w + 1]))
                if w == 0:
                    dve.wait_ge(s_gmix, 32)
                if w >= 2:
                    dve.wait_ge(s_tr[1], w - 1)
                v.scalar_tensor_tensor(out=hn[w % 2][:, :], in0=x2[:, i], scalar=rstd[:, w:w + 1], in1=g_row[:, :],
                                       op0=ALU.mult, op1=ALU.mult).then_inc(s_hn, 1)
            h2_lo(NT - 1)

            for h in range(NH):
                with dve.Fori(0, FI) as i:
                    for b in range(2):
                        pairs = PPAIRS + 2 * FI * h + b + 1
                        for st in range(NS):
                            n = 2 * b + st
                            done = 4 * FI * h + n + 1
                            dve.wait_ge(s_free[2 * st], pairs + 2 * i)
                            dve.wait_ge(s_pair[2 * st + 1], pairs + 2 * i)
                            v.tensor_tensor(act_gate[n][:, :], act_gate[n][:, :], ps[2 * st + 1], ALU.mult
                                            ).then_inc(s_free[2 * st + 1], 1)
                            dve.wait_ge(s_fhi, done + 4 * i)
                            v.tensor_tensor(f_lo[b][:, st * TILE:(st + 1) * TILE], act_gate[n][:, :],
                                            f32(f_hi[b][:, st * TILE:(st + 1) * TILE]), ALU.subtract
                                            ).then_inc(s_flo, 1)
                    for e in range(2 * TPH):
                        t, dh = divmod(e, 2)
                        bank, use = e % 4, e // 4
                        if e == 0:
                            for q in range(4):
                                dve.wait_ge(s_outf[q], NT + 4 * FI * h + 4 * i)
                        dve.wait_ge(s_out[bank], NT + 4 * FI * h + use + 1 + 4 * i)
                        v.tensor_tensor(x2[:, t, dh * TILE:(dh + 1) * TILE], x2[:, t, dh * TILE:(dh + 1) * TILE],
                                        ps[4 + bank], ALU.add).then_inc(s_outf[bank], 1)
                dve.wait_ge(s_fstd, h + 1)
                if h == 0:
                    dve.wait_ge(s_gfin, 16)
                step(v.reciprocal(rstd[:, 0:TPH], rstd[:, 0:TPH]))
                for i in range(TPH):
                    n = h * TPH + i
                    if n >= 2:
                        dve.wait_ge(s_ost[n % 2], 16 * (n // 2))
                    v.scalar_tensor_tensor(out=hn[n % 2][:, :], in0=x2[:, i], scalar=rstd[:, i:i + 1], in1=gfin[:, :],
                                           op0=ALU.mult, op1=ALU.mult).then_inc(s_o, 1)
                if h + 1 < NH:
                    dve.wait_ge(s_x2ld, 16 * TPH)

        @block.tensor
        def _(pe):
            def product(bank, lhs, rhs, chunks, start=True, stop=True):
                for n, c in enumerate(chunks):
                    first, last = start and n == 0, stop and n == len(chunks) - 1
                    pe.matmul(bank, lhs[0](c), rhs[0](c), start=first, stop=False)
                    pe.matmul(bank, lhs[0](c), rhs[1](c), start=False, stop=False)
                    mm = pe.matmul(bank, lhs[1](c), rhs[0](c), start=False, stop=last)
                return mm

            def pair(s, used, tile_ready=None):
                for st in range(NS):
                    cols = slice(st * TILE, (st + 1) * TILE)
                    if tile_ready:
                        tile_ready(st)
                    for e in range(2):
                        if used is not None:
                            pe.wait_ge(s_free[2 * st + e], used)
                        product(ps[2 * st + e],
                                (lambda k: w_hi[s][:, e, k], lambda k: w_lo[s][:, e, k]),
                                (lambda k: h_hi[:, k, cols], lambda k: h_lo[:, k, cols]),
                                range(KD)).then_inc(s_pair[2 * st + e], 1)

            def turn_x(g):
                pe.wait_ge(s_xn, g + 1)
                for b in range(2):
                    free_aux(b, aux_x(g))
                    for k in range(4):
                        c = (4 * b + k) * P
                        mm = pe.transpose(ps[6 + b][:, k * P:(k + 1) * P], xt[g % 3][:, c:c + P], ident[:, :])
                    mm.then_inc(s_aux_done[b], 1)

            def free_aux(b, use):
                turned = sum(aux_x(g) < use for g in range(NT))
                gates = sum(aux_g(u, st) < use for u in range(UNITS) for st in range(NS))
                if turned:
                    pe.wait_ge(s_hlo, 2 * (turned - 1) + b + 1)
                if gates:
                    pe.wait_ge(s_rr if b == 0 else s_ir, gates)

            pe.wait_ge(s_init, 8)
            turn_x(0)
            pe.wait_ge(s_par, 16 * 11)
            for j in range(NJ):
                mm = pe.transpose(ps[0][:, j * NR:(j + 1) * NR], par_rows[0:NR, j * P:(j + 1) * P], ident[0:NR, 0:NR])
            mm.then_inc(s_part, 1)
            for g in range(1, TPH):
                turn_x(g)
            for u in range(UNITS):
                h, j = divmod(u, NJ)
                s = u % 2
                for q in (2 * u, 2 * u + 1):
                    pe.wait_ge(s_wlo, q + 1)
                    if q == 0:
                        pe.wait_ge(s_parc, 1)

                    def tiles(st):
                        pe.wait_ge(s_hlo, 2 * (h * TPH + (st + 1) * TILE // P))

                    pair(q % 2, q if q else None, tiles if q % (2 * NJ) == 0 else None)
                pe.wait_ge(s_clo, u + 1)
                if u == 0:
                    pe.wait_ge(s_gws, 2)
                for st in range(NS):
                    cols = slice(st * TILE, (st + 1) * TILE)
                    for e in range(2):
                        free_aux(e, aux_g(u, st))
                        product(ps[6 + e], (lambda c: gw_hi[:, j, e], lambda c: gw_lo[:, j, e]),
                                (lambda c: c_hi[:, cols], lambda c: c_lo[:, cols]), range(1)
                                ).then_inc(s_aux_done[e], 1)
                if u == NJ - 1:
                    for g in range(TPH, NT):
                        turn_x(g)

            for b in range(3):
                pe.wait_ge(s_free[b], PPAIRS)
            for m0 in range(0, S // TILE, 2):
                for m in (m0, m0 + 1):
                    s = m % 2
                    pe.wait_ge(s_nld[s], 32 * (m // 2 + 1))
                    if m:
                        pe.wait_ge(s_dc, m)
                    for j in range(NJ):
                        mm = pe.matmul(ps[0], mean_w[:, :], nd[s][:, j], start=j == 0, stop=j == NJ - 1)
                    mm.then_inc(s_mean, 1)
                for m in (m0, m0 + 1):
                    s = m % 2
                    pe.wait_ge(s_sq, m + 1)
                    if m:
                        pe.wait_ge(s_nstd, m)
                    for j in range(NJ):
                        mm = pe.matmul(ps[1], mean_w[:, :], nsq[s][:, j], start=j == 0, stop=j == NJ - 1)
                    mm.then_inc(s_var, 1)
                for m in (m0, m0 + 1):
                    s = m % 2
                    if m == m0 and m:
                        pe.wait_ge(s_rstd8, m)
                    for group, ready, done in ((1, s_sq2, s_rm1), (0, s_sqy, s_rm2)):
                        pe.wait_ge(ready, m + 1)
                        for t in range(TILE // P):
                            c = 8 * s + 2 * t + group
                            for j in range(NJ):
                                mm = pe.matmul(ps[2][:, c:c + 1], nsq[s][:, j, t * P:(t + 1) * P], mean_w[:, 0:1],
                                               start=j == 0, stop=j == NJ - 1)
                        mm.then_inc(done, 1)

            def turn_h2(w):
                pe.wait_ge(s_hn, w + 1)
                for b in range(2):
                    if w:
                        pe.wait_ge(s_h2lo, 2 * (w - 1) + b + 1)
                    for k in range(4):
                        c = (4 * b + k) * P
                        mm = pe.transpose(ps[2 + b][:, k * P:(k + 1) * P], hn[w % 2][:, c:c + P], ident[:, :])
                    mm.then_inc(s_tr[b], 1)

            pe.wait_ge(s_rms, S // TILE)
            pe.wait_ge(s_free[3], PPAIRS)
            pe.wait_ge(s_dcopy, UNITS)
            free_aux(0, AUX_USES)
            free_aux(1, AUX_USES)
            pe.wait_ge(s_wlo, PPAIRS + WOQ)
            for w in range(NT):
                s = w % 2
                pe.wait_ge(s_ylo, w + 1)
                for dh in range(2):
                    cols = slice(dh * TILE, (dh + 1) * TILE)
                    for group in range(2):
                        if w:
                            pe.wait_ge(s_outf[2 * dh + group], w)
                        product(ps[4 + 2 * dh + group],
                                (lambda k: y_hi[s][:, k], lambda k: y_lo[s][:, k]),
                                (lambda k: wo_hi[:, k, cols], lambda k: wo_lo[:, k, cols]),
                                range(group * NJ, (group + 1) * NJ)).then_inc(s_out[2 * dh + group], 1)
                if w >= 1:
                    turn_h2(w - 1)
            turn_h2(NT - 1)

            Q0 = PPAIRS + WOQ
            pe.wait_ge(s_h2lo, 2 * NT)
            for h in range(NH):
                if h:
                    pe.wait_ge(s_h2ld, 32 * KD)
                with pe.Fori(0, FI) as i:
                    for b in range(2):
                        pe.wait_ge(s_wlo, Q0 + 2 * FI * h + b + 1 + 2 * i)
                        pair(b, PPAIRS + 2 * FI * h + b + 2 * i)
                    pe.wait_ge(s_wdlo, FI * h + 1 + i)
                    for t0 in range(0, TPH, 2):
                        for c in range(2):
                            if c == 0 and t0 == 0:
                                pe.wait_ge(s_flo, 4 * FI * h + 2 + 4 * i)
                            if c == 1 and t0 in (0, TPH // 2):
                                pe.wait_ge(s_flo, 4 * FI * h + (3 if t0 == 0 else 4) + 4 * i)
                            for e in range(4):
                                t, dh = t0 + e // 2, e % 2
                                rows, cols = slice(t * P, (t + 1) * P), slice(dh * TILE, (dh + 1) * TILE)
                                if c == 0:
                                    pe.wait_ge(s_outf[e], NT + 4 * FI * h + t0 // 2 + 4 * i)
                                mm = product(ps[4 + e], (lambda n: f_hi[n][:, rows], lambda n: f_lo[n][:, rows]),
                                             (lambda n: wd_hi[:, n, cols], lambda n: wd_lo[:, n, cols]),
                                             [c], start=c == 0, stop=c == 1)
                                if c == 1:
                                    mm.then_inc(s_out[e], 1)


_INS = ["x", "norm_mix", "w_in", "conv4_w", "conv4_b", "gate_a_w", "gate_a_b", "gate_x_w", "gate_x_b",
        "lru_lambda", "dw31_w", "dw31_b", "cm_ln_g", "cm_ln_b", "out_norm_lru", "out_norm_cm", "w_out",
        "norm_ffn", "w_gate", "w_up", "w_down", "norm_final"]


def kernel(**inputs):
    import numpy as np
    from concourse import bacc
    from concourse.bass_utils import run_bass_kernel_spmd

    nc = bacc.Bacc("TRN2", target_bir_lowering=False, num_devices=1, dynamic_dma_scratch_size=SCRATCH)
    arrays, args = {}, []
    for name in _INS:
        a = np.ascontiguousarray(inputs[name])
        arrays[f"in_{name}"] = a
        args.append(nc.dram_tensor(f"in_{name}", a.shape, mybir.dt.from_np(a.dtype), kind="ExternalInput").ap())
    shape = inputs["x"].shape
    args.append(nc.dram_tensor("out_block", shape, F32, kind="ExternalOutput").ap())
    hybrid_block(nc, *args)
    r = run_bass_kernel_spmd(nc, [arrays], core_ids=[0])
    return r.results[0]["out_block"]
```

```python
from contextlib import ExitStack

import concourse.bass as bass
from concourse import mybir

ALU = mybir.AluOpType
ACT = mybir.ActivationFunctionType
F32 = mybir.dt.float32
F32R = mybir.dt.float32r
BF16 = mybir.dt.bfloat16

P = 128
TILE = 512
KIB = 1024
EPS = 1e-6
LRU_C = 8.0
SCRATCH = 1024


def hybrid_block(nc, x, norm_mix, w_in, conv4_w, conv4_b, gate_a_w, gate_a_b, gate_x_w, gate_x_b,
                 lru_lambda, dw31_w, dw31_b, cm_ln_g, cm_ln_b, out_norm_lru, out_norm_cm,
                 w_out, norm_ffn, w_gate, w_up, w_down, norm_final, out):
    S, D = x.shape[1], x.shape[2]
    CH = conv4_b.shape[1]
    NJ = CH // P
    KD = D // P
    F = w_gate.shape[2]
    TAPS4, TAPS31 = conv4_w.shape[1], dw31_w.shape[1]
    HALF = 2 * TILE
    NH = S // HALF
    NS = HALF // TILE
    NT = S // P
    TPH = HALF // P
    UNITS = NH * NJ
    PPAIRS = 2 * UNITS
    FI = F // P // 2
    WOQ = KD // 2
    HD = gate_a_w.shape[2]
    PAD4, PAD31 = TAPS4 - 1, TAPS31 - 1
    assert D == 2 * CH == 1024 and F % (2 * P) == 0 and S == NH * HALF and NH == 2

    xr = x.rearrange("a (t p) d -> (a t) p d", p=P)
    outr = out.rearrange("a (t p) d -> (a t) p d", p=P)
    w_in_r = w_in.rearrange("a (k p) n -> p (a k) n", p=P)
    w_out_r = w_out.rearrange("a (k p) n -> p (a k) n", p=P)
    w_gate_r = w_gate.rearrange("a (k p) n -> p (a k) n", p=P)
    w_up_r = w_up.rearrange("a (k p) n -> p (a k) n", p=P)
    w_down_r = w_down.rearrange("a (k p) n -> p (a k) n", p=P)

    R_DW, R_DWB = 0, TAPS31
    R_C4 = R_DWB + 1
    R_C4B = R_C4 + TAPS4
    R_BA, R_BX, R_LAM, R_LNG, R_LNB, R_ONL, R_ONC = range(R_C4B + 1, R_C4B + 8)
    NR = R_ONC + 1

    d_scr = nc.dram_tensor("d_scr", [NJ, P, S], F32).ap()
    y_scr = nc.dram_tensor("y_scr", [NJ, P, S], F32).ap()
    hhi_scr = nc.dram_tensor("hhi_scr", [P, KD, HALF], F32).ap()
    hlo_scr = nc.dram_tensor("hlo_scr", [P, KD, HALF], F32).ap()
    x2_scr = nc.dram_tensor("x2_scr", [TPH, P, D], F32).ap()

    with ExitStack() as ctx:
        base = (nc.sbuf_base + 63) // 64 * 64

        def at(name, shape, dt, offset):
            return nc.alloc_sbuf_tensor_at(name, shape, dt, offset=base + offset)

        def sem(name):
            return ctx.enter_context(nc.semaphore(name))

        h_hi = at("h_hi", [P, KD, HALF], F32R, 0)
        h_lo = at("h_lo", [P, KD, HALF], F32R, 32 * KIB)
        wo_hi = at("wo_hi", [P, KD, D], F32R, 0)
        wo_lo = at("wo_lo", [P, KD, D], F32R, 32 * KIB)
        wf_hi = [at(f"wf_hi{s}", [P, 2, KD, P], F32R, 16 * s * KIB) for s in range(2)]
        wf_lo = [at(f"wf_lo{s}", [P, 2, KD, P], F32R, (8 + 16 * s) * KIB) for s in range(2)]
        wd_hi = at("wd_hi", [P, 2, D], F32R, 32 * KIB)
        wd_lo = at("wd_lo", [P, 2, D], F32R, 40 * KIB)
        f_hi = [at(f"f_hi{b}", [P, HALF], F32R, (48 + 4 * b) * KIB) for b in range(2)]
        f_lo = [at(f"f_lo{b}", [P, HALF], F32R, (56 + 4 * b) * KIB) for b in range(2)]
        w_hi = [at(f"w_hi{s}", [P, 2, KD, P], F32R, (64 + 16 * s) * KIB) for s in range(2)]
        w_lo = [at(f"w_lo{s}", [P, 2, KD, P], F32R, (72 + 16 * s) * KIB) for s in range(2)]
        gel = [at(f"gel{s}", [P, HALF], F32, (96 + 4 * s) * KIB) for s in range(2)]
        cv = [at(f"cv{s}", [P, HALF], F32, (104 + 4 * s) * KIB) for s in range(2)]
        c_hi = at("c_hi", [P, HALF], F32R, 112 * KIB)
        c_lo = at("c_lo", [P, HALF], F32R, 116 * KIB)
        gw_hi = at("gw_hi", [P, NJ, 2, P], F32R, 120 * KIB)
        gw_lo = at("gw_lo", [P, NJ, 2, P], F32R, 124 * KIB)
        h2_hi = at("h2_hi", [P, KD, HALF], F32R, 64 * KIB)
        h2_lo = at("h2_lo", [P, KD, HALF], F32R, 96 * KIB)
        w_raw = [at(f"w_raw{s}", [P, 2, KD, P], F32, (128 + 8 * s) * KIB) for s in range(2)]
        t_hi = [at(f"t_hi{s}", [P, KD, P], F32R, (128 + 8 * s) * KIB) for s in range(2)]
        t_lo = [at(f"t_lo{s}", [P, KD, P], F32R, (132 + 8 * s) * KIB) for s in range(2)]
        uw = at("uw", [P, HALF], F32, 144 * KIB)
        su = at("su", [P, HALF], F32, 148 * KIB)
        ib = at("ib", [P, HALF], F32, 152 * KIB)
        sg = at("sg", [P, HALF], F32, 156 * KIB)
        dst = [at(f"dst{s}", [P, HALF], F32, (160 + 4 * s) * KIB) for s in range(2)]
        y_raw = [at(f"y_raw{s}", [P, KD, P], F32, (144 + 4 * s) * KIB) for s in range(2)]
        y_hi = [at(f"y_hi{s}", [P, KD, P], F32R, (152 + 8 * s) * KIB) for s in range(2)]
        y_lo = [at(f"y_lo{s}", [P, KD, P], F32R, (156 + 8 * s) * KIB) for s in range(2)]
        wd_raw = at("wd_raw", [P, 2, D], F32, 144 * KIB)
        act_gate = [at(f"act_gate{n}", [P, TILE], F32, (152 + 2 * n) * KIB) for n in range(4)]
        xt = [at(f"xt{s}", [P, D], F32, (168 + 4 * s) * KIB) for s in range(3)]
        gw_raw = at("gw_raw", [P, NJ, 2, P], F32, 180 * KIB)
        acc2 = at("acc2", [P, HALF], F32, 180 * KIB)
        xl = at("xl", [P, HALF + 32], F32, 184 * KIB)
        glu = [at(f"glu{s}", [P, HALF + 32], F32, 184 * KIB + 4224 * (1 + s)) for s in range(2)]
        x2 = at("x2", [P, TPH, D], F32, 168 * KIB)
        nd = [at(f"nd{m}", [P, NJ, TILE], F32, o * KIB) for m, o in enumerate((168, 64, 90, 64))]
        nrs = [at(f"nrs{m}", [P, TILE], F32, o * KIB) for m, o in enumerate((176, 88, 114, 88))]
        ny = [at(f"ny{m}", [P, NJ, TILE], F32, o * KIB) for m, o in enumerate((200, 72, 98, 72))]
        nsq = [at(f"nsq{m}", [P, NJ, TILE], F32, o * KIB) for m, o in enumerate((208, 80, 106, 80))]
        g_row = at("g_row", [P, D], F32, 200 * KIB)
        gfin = at("gfin", [P, D], F32, 204 * KIB)
        hn = [at(f"hn{s}", [P, D], F32, (208 + 4 * s) * KIB) for s in range(2)]
        junk = at("junk", [P, D], BF16, 216 * KIB)
        o = 218 * KIB

        def small(name, n, dt=F32):
            nonlocal o
            t = at(name, [P, n], dt, o)
            o += (4 * n + 31) // 32 * 32
            return t

        ident = small("ident", P)
        mean_w = small("mean_w", P)
        par = small("par", NJ * NR)
        rate = small("rate", NJ)
        rate2 = small("rate2", NJ)
        sp = [small(f"sp{n}", NJ) for n in range(4)]
        ssq = small("ssq", NT)
        rstd = small("rstd", NT)
        rms = small("rms", 2 * NT)
        xh = small("xh", NJ * PAD4)
        gh = small("gh", NJ * PAD31)
        hl = small("hl", NJ)
        eps = small("eps", 1)
        one = small("one", 1)
        two = small("two", 1)
        assert base + o <= nc.sbuf_usable_end, (base, o)
        par_rows = hn[0]

        def col(j, r):
            return par[:, j * NR + r:j * NR + r + 1]

        ps = [ctx.enter_context(nc.psum_tensor(f"ps{b}", [P, TILE], F32)) for b in range(4)]
        acc = ctx.enter_context(nc.psum_tensor("acc", [P, HALF], F32))
        ps += [acc[:, 0:TILE], acc[:, TILE:HALF]]
        ps += [ctx.enter_context(nc.psum_tensor(f"ps{b}", [P, TILE], F32)) for b in (6, 7)]
        ps = [b[:, :] for b in ps]
        f32 = lambda ap: ap.bitcast(F32)

        s_par = sem("par_loaded")
        s_gw = sem("gate_weights_loaded")
        s_gmix = sem("g_row_loaded")
        s_gfin = sem("gfin_loaded")
        s_init = sem("pool_constants")
        s_part = sem("par_transposed")
        s_parc = sem("par_copied")
        s_rate = sem("rate_ready")
        s_dve = sem("dve_step")
        s_act = sem("act_step")
        s_gws = sem("gate_weights_split")
        s_x = [sem(f"x_loaded{s}") for s in range(3)]
        s_std = sem("std_ready")
        s_xn = sem("x_normed")
        s_hhi = sem("h_hi_ready")
        s_hlo = sem("h_lo_ready")
        s_aux_done = [sem(f"aux_done{b}") for b in range(2)]
        s_rr = sem("r_ready")
        s_w = [sem(f"w_loaded{s}") for s in range(2)]
        s_whi = sem("w_hi_ready")
        s_wlo = sem("w_lo_ready")
        s_pair = [sem(f"pair_done{b}") for b in range(4)]
        s_free = [sem(f"pair_free{b}") for b in range(4)]
        s_tap0 = sem("tap0_done")
        s_conv4 = sem("conv4_done")
        s_chi = sem("c_hi_ready")
        s_clo = sem("c_lo_ready")
        s_glu = sem("glu_done")
        s_conv31 = sem("conv31_done")
        s_dcopy = sem("d_copied")
        s_dadd = sem("d_complete")
        s_te = sem("tanh_and_exp_ready")
        s_p = sem("one_minus_a_ready")
        s_q = sem("a2_minus_one_ready")
        s_root = sem("root_ready")
        s_a = sem("a_ready")
        s_ir = sem("i_ready")
        s_ic = sem("ic_done")
        s_sic = sem("sqrt_times_ic")
        s_h = sem("scan_done")
        s_hl = sem("last_state_kept")
        s_fin = sem("unit_final")
        s_dst = [sem(f"d_stored{s}") for s in range(2)]
        s_yst = [sem(f"y_stored{s}") for s in range(2)]
        s_nld = [sem(f"norm_loaded{m}") for m in range(S // TILE)]
        s_mean = sem("mean_done")
        s_dc = sem("centred")
        s_sq = sem("squares_ready")
        s_var = sem("var_done")
        s_nstd = sem("ln_std")
        s_dn = sem("ln_scaled")
        s_ysw = sem("swish_done")
        s_sq2 = sem("squares2_ready")
        s_sqy = sem("squares_lru_ready")
        s_rm1 = sem("rms_cm_done")
        s_rm2 = sem("rms_lru_done")
        s_rsty = sem("rms_lru_read")
        s_rsts = sem("rms_cm_read")
        s_rms = sem("rms_ready")
        s_yswst = [sem(f"swish_stored{m}") for m in range(S // TILE)]
        s_yl = [sem(f"y_loaded{s}") for s in range(2)]
        s_yhi = sem("y_hi_ready")
        s_ylo = sem("y_lo_ready")
        s_out = [sem(f"out_bank_done{b}") for b in range(4)]
        s_outf = [sem(f"out_bank_read{b}") for b in range(4)]
        s_xr = [sem(f"residual_loaded{n}") for n in range(4)]
        s_tr = [sem(f"turned{b}") for b in range(2)]
        s_trf = [sem(f"turned_read{b}") for b in range(2)]
        s_std2 = sem("std2_ready")
        s_hn = sem("hn_ready")
        s_h2hi = sem("h2_hi_ready")
        s_h2lo = sem("h2_lo_ready")
        s_h2st = [sem(f"h2_stored{n}") for n in range(2)]
        s_x2st = [sem(f"x2_stored{n}") for n in range(2)]
        s_wd = sem("w_down_loaded")
        s_wdhi = sem("wd_hi_ready")
        s_wdlo = sem("wd_lo_ready")
        s_fhi = sem("f_hi_ready")
        s_flo = sem("f_lo_ready")
        s_h2ld = [sem(f"h2_reloaded{st}") for st in range(NS)]
        s_x2ld = sem("x2_reloaded")
        s_fstd = sem("final_std")
        s_o = sem("out_row_ready")
        s_ost = [sem(f"out_stored{n}") for n in range(2)]

        HALVES = (1, 0)
        N0 = NJ + 1
        LEAD = 3
        even, odd = list(range(0, TAPS31, 2)), list(range(1, TAPS31, 2))
        TAP_ORDER = even[:LEAD]
        for n in range(len(odd)):
            TAP_ORDER += [odd[n]] + even[LEAD + n:LEAD + n + 1]
        CONV4_AT, CENTRE_AT, SCAN_AT = 19, 24, 27
        CONV4_AT_X = 17
        SCAN_AT_LAST = 20
        TURN_FIRST = {(1, 0, 0): 0, (1, 0, 4): 1, (1, 1, 0): 2, (1, 1, 4): 3}
        GATES_REST = (0, 0, 5)
        TURN_REST = {(0, 0, 1): 4, (0, 0, 5): 5, (0, 1, 1): 6, (0, 1, 5): 7}

        def aux_x(g):
            return g if g < TPH else g + NS * (NJ - 1)

        def aux_g(u, st):
            return (TPH if u < NJ - 1 else NT) + NS * u + st

        AUX_USES = NT + NS * UNITS

        def turned(w):
            if w < TPH:
                return t_hi[w % 2], t_lo[w % 2], slice(0, P)
            return h2_hi, h2_lo, slice((w - TPH) * P, (w - TPH + 1) * P)

        block = ctx.enter_context(nc.Block())

        @block.sync
        def _(sp_):
            def load_pair_from(q, a, b):
                sp_.dma_start(w_raw[q % 2][:, 0], a).then_inc(s_w[q % 2], 16)
                sp_.dma_start(w_raw[q % 2][:, 1], b).then_inc(s_w[q % 2], 16)

            def load_pair(q):
                u, which = divmod(q, 2)
                j = u % NJ
                if q >= 2:
                    sp_.wait_ge(s_wlo, q - 1)
                c0 = 2 * CH * (1 - which) + j * P
                load_pair_from(q, w_in_r[:, :, c0:c0 + P], w_in_r[:, :, c0 + CH:c0 + CH + P])

            def load_x(g):
                if g >= 3:
                    sp_.wait_ge(s_aux_done[1], aux_x(g - 3) + 1)
                sp_.dma_start(xt[g % 3][:, :], xr[g]).then_inc(s_x[g % 3], 16)

            def store_unit(u):
                h, j = divmod(u, NJ)
                sp_.wait_ge(s_dadd, u + 1)
                sp_.dma_start(d_scr[j, :, h * HALF:(h + 1) * HALF], dst[u % 2][:, :]).then_inc(s_dst[u % 2], 16)
                sp_.wait_ge(s_fin, u + 1)
                sp_.dma_start(y_scr[j, :, h * HALF:(h + 1) * HALF], gel[u % 2][:, :]).then_inc(s_yst[u % 2], 16)

            load_x(0)
            sp_.dma_start(g_row[:, :], norm_mix.broadcast_to([P, D])).then_inc(s_gmix, 16)
            load_x(1)
            load_pair(0)
            load_x(2)
            rows = [(dw31_w[0], R_DW, TAPS31), (dw31_b, R_DWB, 1), (conv4_w[0], R_C4, TAPS4), (conv4_b, R_C4B, 1),
                    (gate_a_b, R_BA, 1), (gate_x_b, R_BX, 1), (lru_lambda, R_LAM, 1), (cm_ln_g, R_LNG, 1),
                    (cm_ln_b, R_LNB, 1), (out_norm_lru, R_ONL, 1), (out_norm_cm, R_ONC, 1)]
            for src, r, n in rows:
                sp_.dma_start(par_rows[r:r + n, 0:CH], src).then_inc(s_par, 16)
            sp_.wait_ge(s_init, 1)
            for g, w in enumerate((gate_a_w, gate_x_w)):
                for b in range(P // HD):
                    sp_.dma_start(gw_raw[b * HD:(b + 1) * HD, :, g, b * HD:(b + 1) * HD],
                                  w[0].rearrange("(j b) i o -> b i j o", b=P // HD)[b]).then_inc(s_gw, 16)
            for g in range(3, TPH):
                load_x(g)
                if g == 4:
                    load_pair(1)
            def load_norm(m):
                cols = slice(m * TILE, (m + 1) * TILE)
                sp_.dma_start(nd[m][:, :, :], d_scr[:, :, cols].rearrange("j p s -> p j s")).then_inc(s_nld[m], 16)
                sp_.dma_start(ny[m][:, :, :], y_scr[:, :, cols].rearrange("j p s -> p j s")).then_inc(s_nld[m], 16)

            def store_swish(m):
                cols = slice(m * TILE, (m + 1) * TILE)
                sp_.wait_ge(s_ysw, NJ * (m + 1))
                sp_.dma_start(d_scr[:, :, cols].rearrange("j p s -> p j s"), nd[m][:, :, :]).then_inc(s_yswst[m], 16)

            def units_stored(n):
                for s in range(2):
                    sp_.wait_ge(s_dst[s], 16 * n // 2)
                    sp_.wait_ge(s_yst[s], 16 * n // 2)

            def load_w_out(n):
                q = PPAIRS + n
                sp_.wait_ge(s_wlo, q - 1)
                for e in range(2):
                    sp_.dma_start(w_raw[q % 2][:, e].rearrange("p k c -> p (k c)"),
                                  w_out_r[:, 2 * n + e]).then_inc(s_w[q % 2], 16)

            def load_raw(q):
                if q < PPAIRS:
                    load_pair(q)
                elif q < PPAIRS + WOQ:
                    load_w_out(q - PPAIRS)

            load_raw(2)
            load_raw(3)
            for u in range(UNITS):
                if u == NJ - 1:
                    load_raw(2 * u + 4)
                    for g in range(TPH + 3, NT):
                        load_x(g)
                    load_raw(2 * u + 5)
                elif u == UNITS - 1:
                    sp_.wait_ge(s_pair[3], PPAIRS)
                    load_norm(1)
                    store_swish(0)
                    load_raw(2 * u + 4)
                else:
                    load_raw(2 * u + 4)
                    load_raw(2 * u + 5)
                if u == NJ - 2:
                    for g in range(TPH, TPH + 3):
                        load_x(g)
                if u >= 1:
                    store_unit(u - 1)
                if u == NJ:
                    units_stored(NJ)
                    sp_.wait_ge(s_aux_done[1], aux_x(NT - 1) + 1)
                    load_norm(0)
            load_raw(PPAIRS + WOQ - 1)
            store_unit(UNITS - 1)
            sp_.wait_ge(s_rm2, 1)
            sp_.dma_start(g_row[:, :], norm_ffn.broadcast_to([P, D])).then_inc(s_gmix, 16)
            sp_.dma_start(gfin[:, :], norm_final.rearrange("(a d) -> a d", a=1).broadcast_to([P, D])
                          ).then_inc(s_gfin, 16)

            def load_y(w):
                if w >= 2:
                    sp_.wait_ge(s_ylo, w - 1)
                cols = slice(w * P, (w + 1) * P)
                sp_.dma_start(y_raw[w % 2][:, 0:NJ], y_scr[:, :, cols].rearrange("j p s -> p j s")).then_inc(s_yl[w % 2], 16)
                sp_.dma_start(y_raw[w % 2][:, NJ:KD], d_scr[:, :, cols].rearrange("j p s -> p j s")).then_inc(s_yl[w % 2], 16)

            def load_residual(w):
                i = w % TPH
                if w >= 4:
                    sp_.wait_ge(s_outf[0], w - 3)
                if w >= TPH:
                    sp_.wait_ge(s_x2st[i % 2], 16 * (i // 2 + 1))
                sp_.dma_start(x2[:, i], xr[w]).then_inc(s_xr[w % 4], 16)

            def store_h2(w):
                cols = slice(w * P, (w + 1) * P)
                sp_.wait_ge(s_hn, w + 1)
                sp_.dma_start(x2_scr[w], x2[:, w]).then_inc(s_x2st[w % 2], 16)
                sp_.wait_ge(s_h2lo, 2 * (w + 1))
                sp_.dma_start(hhi_scr[:, :, cols], f32(t_hi[w % 2][:, :, :])).then_inc(s_h2st[w % 2], 16)
                sp_.dma_start(hlo_scr[:, :, cols], f32(t_lo[w % 2][:, :, :])).then_inc(s_h2st[w % 2], 16)

            sp_.wait_ge(s_fin, UNITS)
            sp_.wait_ge(s_yswst[0], 16)
            for w in range(2):
                load_y(w)
            for w in range(4):
                load_residual(w)
            units_stored(UNITS)
            load_norm(2)
            for w in range(NT):
                if w == 0:
                    store_swish(1)
                    sp_.wait_ge(s_yswst[1], 16)
                    sp_.wait_ge(s_rm2, 2)
                    sp_.wait_ge(s_rm1, 2)
                    load_norm(3)
                if w in (4, 6):
                    store_swish(w // 2)
                if w + 2 == TPH:
                    for m in (2, 3):
                        sp_.wait_ge(s_yswst[m], 16)
                if w + 2 < NT:
                    load_y(w + 2)
                if 1 <= w <= TPH:
                    store_h2(w - 1)
                if w + 4 < NT:
                    load_residual(w + 4)

            def load_ffn(q, b, f0):
                load_pair_from(q, w_gate_r[:, :, f0], w_up_r[:, :, f0])

            Q0 = PPAIRS + WOQ
            for n in range(2):
                sp_.wait_ge(s_h2st[n], 16 * TPH)
            for b in range(2):
                sp_.wait_ge(s_wlo, Q0 + b - 1)
                load_ffn(Q0 + b, b, slice(b * P, (b + 1) * P))
            sp_.wait_ge(s_ylo, NT)
            sp_.dma_start(wd_raw[:, :, :], w_down_r[:, 0:2]).then_inc(s_wd, 16)
            for h in range(NH):
                with sp_.Fori(0, FI - 1) as i:
                    for b in range(2):
                        sp_.wait_ge(s_wlo, Q0 + 2 * FI * h + b + 1 + 2 * i)
                        load_ffn(b, b, bass.ds((i + 1) * (2 * P) + b * P, P))
                    sp_.wait_ge(s_wdlo, FI * h + 1 + i)
                    sp_.dma_start(wd_raw[:, :, :], w_down_r[:, bass.ds((i + 1) * 2, 2)]).then_inc(s_wd, 16)
                for b in range(2):
                    sp_.wait_ge(s_wlo, Q0 + 2 * FI * (h + 1) + b - 1)
                    load_ffn(b, b, slice(b * P, (b + 1) * P))
                sp_.wait_ge(s_wdlo, FI * (h + 1))
                sp_.dma_start(wd_raw[:, :, :], w_down_r[:, 0:2]).then_inc(s_wd, 16)
                if h + 1 < NH:
                    for st in range(NS):
                        cols = slice(st * TILE, (st + 1) * TILE)
                        sp_.wait_ge(s_pair[2 * st + 1], PPAIRS + 2 * FI * (h + 1))
                        sp_.dma_start(f32(h2_hi[:, :, cols]), hhi_scr[:, :, cols]).then_inc(s_h2ld[st], 16)
                        sp_.dma_start(f32(h2_lo[:, :, cols]), hlo_scr[:, :, cols]).then_inc(s_h2ld[st], 16)
                for i in range(TPH):
                    n = h * TPH + i
                    sp_.wait_ge(s_o, n + 1)
                    sp_.dma_start(outr[HALVES[h] * TPH + i], hn[n % 2][:, :]).then_inc(s_ost[n % 2], 16)
                    if h + 1 < NH:
                        sp_.dma_start(x2[:, i], x2_scr[i]).then_inc(s_x2ld, 16)
            for n in range(2):
                sp_.wait_ge(s_ost[n], 16 * NT // 2)

        @block.gpsimd
        def _(pool):
            g = nc.gpsimd
            g.memset(gw_raw[:, :, :, :], 0.0).then_inc(s_init, 1)
            g.memset(ident[:, :], 0.0).then_inc(s_init, 1)
            g.memset(mean_w[:, :], 1.0 / CH).then_inc(s_init, 1)
            g.memset(eps[:, :], EPS).then_inc(s_init, 1)
            g.memset(one[:, :], 1.0).then_inc(s_init, 1)
            g.memset(two[:, :], 2.0).then_inc(s_init, 1)
            g.memset(xl[:, 0:PAD4], 0.0).then_inc(s_init, 1)
            g.memset(glu[0][:, 0:PAD31], 0.0).then_inc(s_init, 1)
            g.memset(glu[1][:, 0:PAD31], 0.0).then_inc(s_init, 1)
            pool.wait_ge(s_init, 9)
            g.affine_select(out=ident[:, :], in_=ident[:, :], compare_op=ALU.not_equal, fill=1.0, base=0,
                            pattern=[[-1, P]], channel_multiplier=1).then_inc(s_init, 1)

            def split_lo(q):
                pool.wait_ge(s_whi, q + 1)
                g.tensor_tensor(w_lo[q % 2][:, :, :, :], w_raw[q % 2][:, :, :, :], f32(w_hi[q % 2][:, :, :, :]),
                                ALU.subtract).then_inc(s_wlo, 1)

            def output(u):
                pool.wait_ge(s_h, u + 1)
                g.tensor_tensor(gel[u % 2][:, :], gel[u % 2][:, :], cv[u % 2][:, :], ALU.mult).then_inc(s_fin, 1)

            split_lo(0)
            split_lo(1)

            def gated(u):
                h, j = divmod(u, NJ)
                s = u % 2
                for st in range(NS):
                    t = glu[s][:, PAD31 + st * TILE:PAD31 + (st + 1) * TILE]
                    pool.wait_ge(s_free[2 * st], 2 * u + 1)
                    pool.wait_ge(s_free[2 * st + 1], 2 * u + 1)
                    g.tensor_tensor(t, t, sg[:, st * TILE:(st + 1) * TILE], ALU.mult).then_inc(s_glu, 1)
                halo = gh[:, j * PAD31:(j + 1) * PAD31]
                if h == 0:
                    pool.wait_ge(s_glu, (NS + 1) * u + NS)
                    g.tensor_copy(halo, glu[s][:, HALF:HALF + PAD31]).then_inc(s_glu, 1)
                else:
                    pool.wait_ge(s_conv31, u - 1)
                    g.tensor_copy(glu[s][:, 0:PAD31], halo).then_inc(s_glu, 1)

            def decay(u):
                pool.wait_ge(s_ir, NS * (u + 1))
                pool.wait_ge(s_clo, u + 1)
                g.tensor_tensor(cv[u % 2][:, :], cv[u % 2][:, :], ib[:, :], ALU.mult).then_inc(s_ic, 1)
                pool.wait_ge(s_te, 2 * (u + 1))
                g.tensor_tensor(uw[:, :], uw[:, :], one[:, 0:1].broadcast_to([P, HALF]), ALU.add).then_inc(s_p, 1)
                pool.wait_ge(s_p, 2 * u + 1)
                g.tensor_tensor(uw[:, :], uw[:, :], su[:, :], ALU.mult).then_inc(s_p, 1)
                pool.wait_ge(s_p, 2 * u + 2)
                g.tensor_tensor(su[:, :], uw[:, :], two[:, 0:1].broadcast_to([P, HALF]), ALU.subtract).then_inc(s_q, 1)
                pool.wait_ge(s_q, 2 * u + 1)
                g.tensor_tensor(su[:, :], su[:, :], uw[:, :], ALU.mult).then_inc(s_q, 1)

            def scan_input(u):
                pool.wait_ge(s_root, u + 1)
                pool.wait_ge(s_ic, u + 1)
                g.tensor_tensor(su[:, :], su[:, :], cv[u % 2][:, :], ALU.mult).then_inc(s_sic, 1)

            def complete_d(u):
                pool.wait_ge(s_dcopy, u + 1)
                g.tensor_tensor(dst[u % 2][:, :], dst[u % 2][:, :], acc2[:, :], ALU.add).then_inc(s_dadd, 1)

            def split_w_out(n):
                q = PPAIRS + n
                pool.wait_ge(s_whi, q + 1)
                g.tensor_tensor(wo_lo[:, 2 * n:2 * n + 2, :], w_raw[q % 2][:, :, :, :].rearrange("p e k c -> p e (k c)"),
                                f32(wo_hi[:, 2 * n:2 * n + 2, :]), ALU.subtract).then_inc(s_wlo, 1)

            gated(0)
            for u in range(UNITS):
                if u >= 1:
                    complete_d(u - 1)
                if 2 * u + 2 < PPAIRS:
                    split_lo(2 * u + 2)
                if u >= 1:
                    decay(u - 1)
                    scan_input(u - 1)
                if 2 * u + 3 < PPAIRS:
                    split_lo(2 * u + 3)
                pool.wait_ge(s_chi, u + 1)
                g.tensor_tensor(c_lo[:, :], cv[u % 2][:, :], f32(c_hi[:, :]), ALU.subtract).then_inc(s_clo, 1)
                if u >= 1:
                    output(u - 1)
                if u + 1 < UNITS:
                    gated(u + 1)
            decay(UNITS - 1)
            split_w_out(0)
            scan_input(UNITS - 1)
            split_w_out(1)
            complete_d(UNITS - 1)
            output(UNITS - 1)
            split_w_out(2)
            split_w_out(3)
            for w in range(NT):
                pool.wait_ge(s_yhi, w + 1)
                g.tensor_tensor(y_lo[w % 2][:, :, :], y_raw[w % 2][:, :, :], f32(y_hi[w % 2][:, :, :]),
                                ALU.subtract).then_inc(s_ylo, 1)
            Q0 = PPAIRS + WOQ

            def split_down(count):
                pool.wait_ge(s_wdhi, count)
                g.tensor_tensor(wd_lo[:, :, :], wd_raw[:, :, :], f32(wd_hi[:, :, :]), ALU.subtract).then_inc(s_wdlo, 1)

            def split_ffn(b, count):
                pool.wait_ge(s_whi, count)
                g.tensor_tensor(wf_lo[b][:, :, :, :], w_raw[b][:, :, :, :], f32(wf_hi[b][:, :, :, :]),
                                ALU.subtract).then_inc(s_wlo, 1)

            split_ffn(0, Q0 + 1)
            split_ffn(1, Q0 + 2)
            split_down(1)
            with pool.Fori(0, NH * FI) as i:
                split_ffn(0, Q0 + 3 + 2 * i)
                split_ffn(1, Q0 + 4 + 2 * i)
                split_down(2 + i)

        @block.scalar
        def _(act):
            a = nc.scalar
            steps = [0]

            def step(ins):
                steps[0] += 1
                ins.then_inc(s_act, 1)
                act.wait_ge(s_act, steps[0])

            def split_hi(q):
                act.wait_ge(s_w[q % 2], 32 * (q // 2 + 1))
                if q >= 2:
                    act.wait_ge(s_pair[3], q - 1)
                a.copy(w_hi[q % 2][:, :, :, :], w_raw[q % 2][:, :, :, :]).then_inc(s_whi, 1)

            def x_std(g):
                act.wait_ge(s_x[g % 3], 16 * (g // 3 + 1))
                step(a.activation(junk[:, :], xt[g % 3][:, :], ACT.Square, accum_out=ssq[:, g:g + 1]))
                a.activation(rstd[:, g:g + 1], ssq[:, g:g + 1], ACT.Sqrt, bias=eps[:, 0:1], scale=1.0 / D).then_inc(s_std, 1)

            def x_hi(g):
                i = g % TPH
                for b in range(2):
                    act.wait_ge(s_aux_done[b], aux_x(g) + 1)
                    if g == TPH and b == 0:
                        act.wait_ge(s_pair[1], PPAIRS // NH)
                    if g == TPH + TPH // 2 and b == 0:
                        act.wait_ge(s_pair[3], PPAIRS // NH)
                    a.copy(h_hi[:, 4 * b:4 * b + 4, i * P:(i + 1) * P],
                           ps[6 + b].rearrange("p (k s) -> p k s", k=4)).then_inc(s_hhi, 1)

            def copy_d(u):
                act.wait_ge(s_conv31, u + 1)
                if u >= 2:
                    act.wait_ge(s_dst[u % 2], 16 * (u // 2))
                a.copy(dst[u % 2][:, :], acc[:, :]).then_inc(s_dcopy, 1)

            def norm_squares(m):
                act.wait_ge(s_nld[m], 32)
                a.activation(ny[m][:, :, :], ny[m][:, :, :], ACT.Square).then_inc(s_sqy, 1)
                act.wait_ge(s_dc, m + 1)
                a.activation(nsq[m][:, :, :], nd[m][:, :, :], ACT.Square).then_inc(s_sq, 1)

            def norm_std(m, bank):
                act.wait_ge(s_var, m + 1)
                a.activation(nrs[m][:, :], ps[bank], ACT.Sqrt, bias=eps[:, 0:1]).then_inc(s_nstd, 1)

            def norm_rms_lru(m, bank):
                act.wait_ge(s_rm2, m + 1)
                a.activation(rms[:, 8 * m:8 * m + 8:2], ps[bank][:, 0:4], ACT.Sqrt, bias=eps[:, 0:1]).then_inc(s_rsty, 1)

            def norm_rms_cm(m, bank):
                act.wait_ge(s_rm1, m + 1)
                a.activation(rms[:, 8 * m + 1:8 * m + 8:2], ps[bank][:, 0:4], ACT.Sqrt, bias=eps[:, 0:1]).then_inc(s_rsts, 1)

            def norm_swish(m):
                act.wait_ge(s_dn, m + 1)
                for j in range(NJ):
                    a.activation(nd[m][:, j], nd[m][:, j], ACT.Silu, scale=col(j, R_LNG), bias=col(j, R_LNB)
                                 ).then_inc(s_ysw, 1)
                act.wait_ge(s_ysw, NJ * (m + 1))
                a.activation(nsq[m][:, :, :], nd[m][:, :, :], ACT.Square).then_inc(s_sq2, 1)

            def evacuate(u, st, first):
                s = u % 2
                cols = slice(st * TILE, (st + 1) * TILE)
                done = 2 * u + (1 if first else 2)
                act.wait_ge(s_pair[2 * st], done)
                if first:
                    if st == 0 and u >= 2:
                        act.wait_ge(s_conv31, u - 1)
                        act.wait_ge(s_glu, (NS + 1) * (u - 1))
                    a.copy(glu[s][:, PAD31 + st * TILE:PAD31 + (st + 1) * TILE], ps[2 * st]).then_inc(s_free[2 * st], 1)
                else:
                    if st == 0 and u >= 1:
                        act.wait_ge(s_conv4, u)
                    a.copy(xl[:, PAD4 + st * TILE:PAD4 + (st + 1) * TILE], ps[2 * st]).then_inc(s_free[2 * st], 1)
                act.wait_ge(s_pair[2 * st + 1], done)
                if first:
                    if u >= 1:
                        act.wait_ge(s_glu, (NS + 1) * (u - 1) + st + 1)
                    a.activation(sg[:, cols], ps[2 * st + 1], ACT.Sigmoid).then_inc(s_free[2 * st + 1], 1)
                else:
                    if st == 0 and u >= 2:
                        act.wait_ge(s_yst[s], 16 * (u // 2))
                    a.activation(gel[s][:, cols], ps[2 * st + 1], ACT.Gelu_apprx_tanh).then_inc(s_free[2 * st + 1], 1)

            def tap0(u):
                h, j = divmod(u, NJ)
                halo = xh[:, j * PAD4:(j + 1) * PAD4]
                act.wait_ge(s_free[2], 2 * u + 2)
                if h == 0:
                    step(a.copy(halo, xl[:, HALF:HALF + PAD4]))
                else:
                    step(a.copy(xl[:, 0:PAD4], halo))
                if u >= 2:
                    act.wait_ge(s_fin, u - 1)
                a.activation(cv[u % 2][:, :], xl[:, 0:HALF], ACT.Identity, scale=col(j, R_C4), bias=col(j, R_C4B)
                             ).then_inc(s_tap0, 1)

            def gates(u):
                j = u % NJ
                for st in range(NS):
                    cols = slice(st * TILE, (st + 1) * TILE)
                    act.wait_ge(s_aux_done[0], aux_g(u, st) + 1)
                    if st == 0 and u >= 1:
                        act.wait_ge(s_h, u)
                    a.activation(uw[:, cols], ps[6], ACT.Sigmoid, bias=col(j, R_BA)).then_inc(s_rr, 1)
                    act.wait_ge(s_aux_done[1], aux_g(u, st) + 1)
                    if st == 0 and u >= 1:
                        act.wait_ge(s_ic, u)
                    a.activation(ib[:, cols], ps[7], ACT.Sigmoid, bias=col(j, R_BX)).then_inc(s_ir, 1)
                act.wait_ge(s_rr, NS * (u + 1))
                if u == 0:
                    act.wait_ge(s_rate, 3)
                a.activation(su[:, :], uw[:, :], ACT.Tanh, scale=rate[:, j:j + 1]).then_inc(s_te, 1)
                a.activation(uw[:, :], uw[:, :], ACT.Exp, scale=rate2[:, j:j + 1]).then_inc(s_te, 1)

            def root(u):
                act.wait_ge(s_q, 2 * (u + 1))
                a.activation(su[:, :], su[:, :], ACT.Sqrt, scale=-1.0).then_inc(s_root, 1)
                a.activation(uw[:, :], uw[:, :], ACT.Identity, scale=-1.0, bias=1.0).then_inc(s_a, 1)

            def c_split(u):
                act.wait_ge(s_conv4, u + 1)
                if u >= 1:
                    act.wait_ge(s_aux_done[1], aux_g(u - 1, NS - 1) + 1)
                a.copy(c_hi[:, :], cv[u % 2][:, :]).then_inc(s_chi, 1)

            act.wait_ge(s_init, 10)
            x_std(0)
            split_hi(0)
            for g in range(1, TPH):
                x_std(g)
                x_hi(g - 1)
            x_hi(TPH - 1)
            act.wait_ge(s_parc, 2)
            a.activation(sp[1][:, :], sp[0][:, :], ACT.Exp).then_inc(s_rate, 1)
            split_hi(1)
            act.wait_ge(s_gw, 16 * 4)
            a.copy(gw_hi[:, :, :, :], gw_raw[:, :, :, :]).then_inc(s_gws, 1)
            for u in range(UNITS):
                evacuate(u, 0, True)
                evacuate(u, 1, True)
                if 2 * u + 2 < PPAIRS:
                    split_hi(2 * u + 2)
                if u >= 1:
                    copy_d(u - 1)
                    gates(u - 1)
                if u == NJ - 1:
                    for g in range(TPH, TPH + 3):
                        x_std(g)
                if u == N0 + 2:
                    norm_swish(0)
                evacuate(u, 0, False)
                if u == NJ - 1:
                    x_hi(TPH)
                    x_std(TPH + 3)
                    x_hi(TPH + 1)
                    x_std(TPH + 4)
                    x_hi(TPH + 2)
                    x_hi(TPH + 3)
                    x_std(TPH + 5)
                evacuate(u, 1, False)
                if u == NJ - 1:
                    x_hi(TPH + 4)
                    x_std(TPH + 6)
                tap0(u)
                if u == NJ - 1:
                    x_hi(TPH + 5)
                    x_std(TPH + 7)
                    x_hi(TPH + 6)
                if u >= 1:
                    root(u - 1)
                if u == NJ - 1:
                    x_hi(TPH + 7)
                if 2 * u + 3 < PPAIRS:
                    split_hi(2 * u + 3)
                c_split(u)
                if u == N0:
                    norm_squares(0)
                if u == N0 + 1:
                    norm_std(0, 7)
                    norm_rms_lru(0, 6)
                if u == N0 + 2:
                    norm_rms_cm(0, 6)

            def split_w_out(n):
                q = PPAIRS + n
                act.wait_ge(s_w[q % 2], 32 * (q // 2 + 1))
                if n == 0:
                    act.wait_ge(s_pair[3], PPAIRS)
                for e in range(2):
                    k = 2 * n + e
                    gain = col(k % NJ, R_ONL if k < NJ else R_ONC)
                    t = w_raw[q % 2][:, e].rearrange("p k c -> p (k c)")
                    step(a.activation(t, t, ACT.Copy, scale=gain))
                a.copy(wo_hi[:, 2 * n:2 * n + 2, :], w_raw[q % 2][:, :, :, :].rearrange("p e k c -> p e (k c)")
                       ).then_inc(s_whi, 1)

            gates(UNITS - 1)
            split_w_out(0)
            norm_squares(1)
            root(UNITS - 1)
            split_w_out(1)
            norm_std(1, 1)
            copy_d(UNITS - 1)
            norm_rms_lru(1, 0)
            split_w_out(2)
            norm_swish(1)
            split_w_out(3)
            norm_rms_cm(1, 1)

            def y_split(w):
                act.wait_ge(s_yl[w % 2], 32 * (w // 2 + 1))
                if w >= 2:
                    act.wait_ge(s_out[3], w - 1)
                a.copy(y_hi[w % 2][:, :, :], y_raw[w % 2][:, :, :]).then_inc(s_yhi, 1)

            def h2_hi(w):
                hi, _, cols = turned(w)
                if w == 0:
                    act.wait_ge(s_wlo, PPAIRS + WOQ)
                elif 2 <= w < TPH:
                    act.wait_ge(s_h2st[w % 2], 32 * (w // 2))
                elif w == TPH:
                    for m in (2, 3):
                        act.wait_ge(s_yswst[m], 16)
                for b in range(2):
                    act.wait_ge(s_tr[b], w + 1)
                    a.copy(hi[:, 4 * b:4 * b + 4, cols],
                           ps[2 + b].rearrange("p (k s) -> p k s", k=4)).then_inc(s_h2hi, 1)

            y_split(0)
            for w in range(NT):
                if w + 1 < NT:
                    y_split(w + 1)
                for m in (2, 3):
                    at_step = w - 2 * (m - 2)
                    if at_step == 1:
                        norm_squares(m)
                    if at_step == 2:
                        norm_std(m, 1)
                    if at_step == 3:
                        norm_rms_lru(m, 1)
                        norm_swish(m)
                    if at_step == 4:
                        norm_rms_cm(m, 0)
                if w >= 1:
                    h2_hi(w - 1)
                act.wait_ge(s_outf[3], w + 1)
                step(a.activation(junk[:, :], x2[:, w % TPH], ACT.Square, accum_out=ssq[:, w:w + 1]))
                a.activation(rstd[:, w:w + 1], ssq[:, w:w + 1], ACT.Sqrt, bias=eps[:, 0:1], scale=1.0 / D
                             ).then_inc(s_std2, 1)
            h2_hi(NT - 1)

            Q0 = PPAIRS + WOQ

            def ffn_hi(b, loaded, used):
                act.wait_ge(s_w[b], loaded)
                if used is not None:
                    act.wait_ge(s_pair[3], used)
                a.copy(wf_hi[b][:, :, :, :], w_raw[b][:, :, :, :]).then_inc(s_whi, 1)

            def down_hi(loaded, used):
                act.wait_ge(s_wd, loaded)
                if used is not None:
                    act.wait_ge(s_out[3], used)
                a.copy(wd_hi[:, :, :], wd_raw[:, :, :]).then_inc(s_wdhi, 1)

            act.wait_ge(s_out[3], NT)
            for b in range(2):
                ffn_hi(b, 16 * (Q0 + 2), None)
            down_hi(16, None)
            for h in range(NH):
                with act.Fori(0, FI) as i:
                    for b in range(2):
                        pairs = PPAIRS + 2 * FI * h + b + 1
                        for st in range(NS):
                            n = 2 * b + st
                            act.wait_ge(s_pair[2 * st], pairs + 2 * i)
                            a.activation(act_gate[n][:, :], ps[2 * st], ACT.Silu).then_inc(s_free[2 * st], 1)
                            act.wait_ge(s_free[2 * st + 1], pairs + 2 * i)
                            if n % 2 == 0:
                                act.wait_ge(s_out[3], NT + 4 * FI * h + 4 * i)
                            a.copy(f_hi[b][:, st * TILE:(st + 1) * TILE], act_gate[n][:, :]).then_inc(s_fhi, 1)
                        ffn_hi(b, 16 * (Q0 + 2 * FI * h + 4) + 32 * i, pairs + 2 * i)
                    down_hi(16 * (FI * h + 2) + 16 * i, NT + 4 * (FI * h + 1) + 4 * i)
                for i in range(TPH):
                    if i == 0:
                        act.wait_ge(s_outf[3], NT + 4 * FI * (h + 1))
                        if h == 1:
                            act.wait_ge(s_o, TPH)
                    step(a.activation(junk[:, :], x2[:, i], ACT.Square, accum_out=ssq[:, i:i + 1]))
                    a.activation(rstd[:, i:i + 1], ssq[:, i:i + 1], ACT.Sqrt, bias=eps[:, 0:1], scale=1.0 / D
                                 ).then_inc(s_fstd, 1)

        @block.vector
        def _(dve):
            v = nc.vector
            steps = [0]

            def step(ins):
                steps[0] += 1
                ins.then_inc(s_dve, 1)
                dve.wait_ge(s_dve, steps[0])

            def x_norm(g):
                dve.wait_ge(s_std, g + 1)
                step(v.reciprocal(rstd[:, g:g + 1], rstd[:, g:g + 1]))
                if g == 0:
                    dve.wait_ge(s_gmix, 16)
                v.scalar_tensor_tensor(out=xt[g % 3][:, :], in0=xt[g % 3][:, :], scalar=rstd[:, g:g + 1],
                                       in1=g_row[:, :], op0=ALU.mult, op1=ALU.mult).then_inc(s_xn, 1)

            def x_lo(g):
                i = g % TPH
                for b in range(2):
                    dve.wait_ge(s_hhi, 2 * g + b + 1)
                    cols = slice(i * P, (i + 1) * P)
                    v.tensor_tensor(h_lo[:, 4 * b:4 * b + 4, cols], ps[6 + b].rearrange("p (k s) -> p k s", k=4),
                                    f32(h_hi[:, 4 * b:4 * b + 4, cols]), ALU.subtract).then_inc(s_hlo, 1)

            def parameters():
                dve.wait_ge(s_part, 1)
                v.tensor_copy(par[:, :], ps[3][:, 0:NJ * NR]).then_inc(s_parc, 1)
                dve.wait_ge(s_parc, 1)
                lam = par[:, R_LAM:NJ * NR:NR]
                step(v.tensor_scalar(sp[1][:, :], lam, -1.0, None, ALU.mult))
                v.tensor_tensor(sp[0][:, :], lam, sp[1][:, :], ALU.min).then_inc(s_parc, 1)

            def decay_rate():
                lam = par[:, R_LAM:NJ * NR:NR]
                e, z, z2, poly = sp[1], sp[0], sp[2], sp[3]
                dve.wait_ge(s_rate, 1)
                step(v.tensor_scalar(z[:, :], e[:, :], 2.0, None, ALU.add))
                step(v.reciprocal(z[:, :], z[:, :]))
                step(v.tensor_tensor(z[:, :], z[:, :], e[:, :], ALU.mult))
                step(v.tensor_tensor(z2[:, :], z[:, :], z[:, :], ALU.mult))
                top = 10
                step(v.tensor_scalar(poly[:, :], z2[:, :], 1.0 / (2 * top + 1), 1.0 / (2 * top - 1), ALU.mult, ALU.add))
                for n in range(top - 2, -1, -1):
                    step(v.tensor_tensor(poly[:, :], poly[:, :], z2[:, :], ALU.mult))
                    step(v.tensor_scalar(poly[:, :], poly[:, :], 1.0 / (2 * n + 1), None, ALU.add))
                step(v.tensor_tensor(poly[:, :], poly[:, :], z[:, :], ALU.mult))
                step(v.tensor_scalar(z2[:, :], lam, -1.0, 0.0, ALU.mult, ALU.max))
                step(v.scalar_tensor_tensor(out=poly[:, :], in0=poly[:, :], scalar=2.0, in1=z2[:, :],
                                            op0=ALU.mult, op1=ALU.add))
                v.tensor_scalar(rate[:, :], poly[:, :], LRU_C / 2, None, ALU.mult).then_inc(s_rate, 1)
                v.tensor_scalar(rate2[:, :], poly[:, :], -LRU_C, None, ALU.mult).then_inc(s_rate, 1)

            def gate_weights_lo():
                dve.wait_ge(s_gws, 1)
                v.tensor_tensor(gw_lo[:, :, :, :], gw_raw[:, :, :, :], f32(gw_hi[:, :, :, :]), ALU.subtract
                                ).then_inc(s_gws, 1)

            x_norm(0)
            parameters()
            for g in range(1, TPH):
                x_norm(g)
                x_lo(g - 1)
            x_lo(TPH - 1)
            decay_rate()
            gate_weights_lo()

            def norm_centre(m, bank):
                dve.wait_ge(s_mean, m + 1)
                v.tensor_tensor(nd[m][:, :, :], nd[m][:, :, :], ps[bank][:, None, :].broadcast_to([P, NJ, TILE]),
                                ALU.subtract).then_inc(s_dc, 1)

            def norm_scale(m):
                dve.wait_ge(s_nstd, m + 1)
                step(v.reciprocal(nrs[m][:, :], nrs[m][:, :]))
                dve.wait_ge(s_sq, m + 1)
                v.tensor_tensor(nd[m][:, :, :], nd[m][:, :, :], nrs[m][:, None, :].broadcast_to([P, NJ, TILE]),
                                ALU.mult).then_inc(s_dn, 1)

            def norm_rms(m):
                dve.wait_ge(s_rsty, m + 1)
                dve.wait_ge(s_rsts, m + 1)
                v.reciprocal(rms[:, 8 * m:8 * m + 8], rms[:, 8 * m:8 * m + 8]).then_inc(s_rms, 1)

            def conv4(u):
                s, j = u % 2, u % NJ
                dve.wait_ge(s_tap0, u + 1)
                for k in range(1, TAPS4):
                    ins = v.scalar_tensor_tensor(out=cv[s][:, :], in0=xl[:, k:k + HALF], scalar=col(j, R_C4 + k),
                                                 in1=cv[s][:, :], op0=ALU.mult, op1=ALU.add)
                    if k == TAPS4 - 1:
                        ins.then_inc(s_conv4, 1)
                    else:
                        step(ins)

            def scan(u):
                h, j = divmod(u, NJ)
                s = u % 2
                dve.wait_ge(s_sic, u + 1)
                dve.wait_ge(s_a, u + 1)
                if u == NJ:
                    dve.wait_ge(s_hl, NJ)
                v.tensor_tensor_scan(cv[s][:, :], uw[:, :], su[:, :], 0.0 if h == 0 else hl[:, j:j + 1],
                                     ALU.mult, ALU.add).then_inc(s_h, 1)
                if h == 0:
                    dve.wait_ge(s_h, u + 1)
                    v.tensor_copy(hl[:, j:j + 1], cv[s][:, HALF - 1:HALF]).then_inc(s_hl, 1)

            between = {}

            def put(u, place, *steps_):
                between.setdefault((u, place), []).extend(steps_)

            T0 = TPH
            for place, steps_ in ((4, (("norm", T0),)), (5, (("norm", T0 + 1),)), (6, (("norm", T0 + 2),)),
                                  (7, (("lo", T0),)), (9, (("lo", T0 + 1), ("norm", T0 + 3))),
                                  (10, (("lo", T0 + 2),)), (11, (("norm", T0 + 4), ("lo", T0 + 3))),
                                  (12, (("norm", T0 + 5),)), (13, (("lo", T0 + 4), ("norm", T0 + 6))),
                                  (14, (("lo", T0 + 5), ("norm", T0 + 7))), (15, (("lo", T0 + 6),)),
                                  (16, (("lo", T0 + 7),))):
                put(NJ - 1, place, *steps_)

            def conv31(u):
                j = u % NJ
                t = glu[u % 2]
                last = [0, 0]
                for place, k in enumerate(TAP_ORDER):
                    for what, g in between.get((u, place), ()):
                        (x_norm if what == "norm" else x_lo)(g)
                    if place == (CONV4_AT_X if u == NJ - 1 else CONV4_AT):
                        conv4(u)
                    if place == CENTRE_AT and u == N0:
                        norm_centre(0, 6)
                    if u >= 1 and place == (SCAN_AT_LAST if u == UNITS - 1 else SCAN_AT):
                        scan(u - 1)
                    if place == SCAN_AT:
                        if u == N0 + 1:
                            norm_scale(0)
                        if u == UNITS - 1:
                            norm_centre(1, 0)
                    e = k % 2
                    sum_ = (acc, acc2)[e]
                    if k == 0:
                        dve.wait_ge(s_glu, (NS + 1) * (u + 1))
                        if u >= 1:
                            dve.wait_ge(s_dcopy, u)
                        ins = v.tensor_scalar(sum_[:, :], t[:, 0:HALF], col(j, R_DW), col(j, R_DWB), ALU.mult, ALU.add)
                    elif k == 1:
                        if u >= 1:
                            dve.wait_ge(s_dadd, u)
                        ins = v.tensor_scalar(sum_[:, :], t[:, 1:1 + HALF], col(j, R_DW + 1), None, ALU.mult)
                    else:
                        dve.wait_ge(s_dve, steps[0] if place == TAPS31 - 1 else last[e])
                        ins = v.scalar_tensor_tensor(out=sum_[:, :], in0=t[:, k:k + HALF], scalar=col(j, R_DW + k),
                                                     in1=sum_[:, :], op0=ALU.mult, op1=ALU.add)
                    if place == TAPS31 - 1:
                        ins.then_inc(s_conv31, 1)
                    else:
                        steps[0] += 1
                        last[e] = steps[0]
                        ins.then_inc(s_dve, 1)

            for u in range(UNITS):
                conv31(u)
            norm_scale(1)
            scan(UNITS - 1)
            norm_rms(0)

            def h2_lo(w):
                i = w % TPH
                hi, lo, cols = turned(w)
                for b in range(2):
                    dve.wait_ge(s_h2hi, 2 * w + b + 1)
                    v.tensor_tensor(lo[:, 4 * b:4 * b + 4, cols], ps[2 + b].rearrange("p (k s) -> p k s", k=4),
                                    f32(hi[:, 4 * b:4 * b + 4, cols]), ALU.subtract).then_inc(s_h2lo, 1)

            for w in range(NT):
                i, g = w % TPH, w
                if w == 2:
                    norm_rms(1)
                if w in (0, 4, TPH):
                    dve.wait_ge(s_rms, {0: 1, 4: 2, TPH: 4}[w])
                dve.wait_ge(s_xr[w % 4], 16 * (w // 4 + 1))
                for dh in range(2):
                    cols = slice(dh * TILE, (dh + 1) * TILE)
                    dve.wait_ge(s_out[2 * dh], w + 1)
                    v.scalar_tensor_tensor(out=x2[:, i, cols], in0=ps[4 + 2 * dh], scalar=rms[:, 2 * g:2 * g + 1],
                                           in1=x2[:, i, cols], op0=ALU.mult, op1=ALU.add).then_inc(s_outf[2 * dh], 1)
                    dve.wait_ge(s_out[2 * dh + 1], w + 1)
                    dve.wait_ge(s_outf[2 * dh], w + 1)
                    v.scalar_tensor_tensor(out=x2[:, i, cols], in0=ps[5 + 2 * dh], scalar=rms[:, 2 * g + 1:2 * g + 2],
                                           in1=x2[:, i, cols], op0=ALU.mult, op1=ALU.add).then_inc(s_outf[2 * dh + 1], 1)
                if w >= 1:
                    h2_lo(w - 1)
                dve.wait_ge(s_std2, w + 1)
                step(v.reciprocal(rstd[:, w:w + 1], rstd[:, w:w + 1]))
                if w == 0:
                    dve.wait_ge(s_gmix, 32)
                    dve.wait_ge(s_rm1, 1)
                if w >= 2:
                    dve.wait_ge(s_tr[1], w - 1)
                v.scalar_tensor_tensor(out=hn[w % 2][:, :], in0=x2[:, i], scalar=rstd[:, w:w + 1], in1=g_row[:, :],
                                       op0=ALU.mult, op1=ALU.mult).then_inc(s_hn, 1)
                for m in (2, 3):
                    at_step = w - 2 * (m - 2)
                    if at_step == 0:
                        norm_centre(m, 0)
                    if at_step == 2:
                        norm_scale(m)
                    if at_step == 4:
                        norm_rms(m)
            h2_lo(NT - 1)

            for h in range(NH):
                with dve.Fori(0, FI) as i:
                    for b in range(2):
                        pairs = PPAIRS + 2 * FI * h + b + 1
                        for st in range(NS):
                            n = 2 * b + st
                            done = 4 * FI * h + n + 1
                            dve.wait_ge(s_free[2 * st], pairs + 2 * i)
                            dve.wait_ge(s_pair[2 * st + 1], pairs + 2 * i)
                            v.tensor_tensor(act_gate[n][:, :], act_gate[n][:, :], ps[2 * st + 1], ALU.mult
                                            ).then_inc(s_free[2 * st + 1], 1)
                            dve.wait_ge(s_fhi, done + 4 * i)
                            v.tensor_tensor(f_lo[b][:, st * TILE:(st + 1) * TILE], act_gate[n][:, :],
                                            f32(f_hi[b][:, st * TILE:(st + 1) * TILE]), ALU.subtract
                                            ).then_inc(s_flo, 1)
                    for e in range(2 * TPH):
                        t, dh = divmod(e, 2)
                        bank, use = e % 4, e // 4
                        if e == 0:
                            for q in range(4):
                                dve.wait_ge(s_outf[q], NT + 4 * FI * h + 4 * i)
                            if h:
                                dve.wait_ge(s_x2ld, 16 * TPH)
                        dve.wait_ge(s_out[bank], NT + 4 * FI * h + use + 1 + 4 * i)
                        v.tensor_tensor(x2[:, t, dh * TILE:(dh + 1) * TILE], x2[:, t, dh * TILE:(dh + 1) * TILE],
                                        ps[4 + bank], ALU.add).then_inc(s_outf[bank], 1)
                if h == 0:
                    dve.wait_ge(s_gfin, 16)
                for i in range(TPH):
                    n = h * TPH + i
                    dve.wait_ge(s_fstd, n + 1)
                    step(v.reciprocal(rstd[:, i:i + 1], rstd[:, i:i + 1]))
                    if n >= 2:
                        dve.wait_ge(s_ost[n % 2], 16 * (n // 2))
                    v.scalar_tensor_tensor(out=hn[n % 2][:, :], in0=x2[:, i], scalar=rstd[:, i:i + 1], in1=gfin[:, :],
                                           op0=ALU.mult, op1=ALU.mult).then_inc(s_o, 1)

        @block.tensor
        def _(pe):
            def product(bank, lhs, rhs, chunks, start=True, stop=True, before=None):
                for n, c in enumerate(chunks):
                    if before:
                        before(c)
                    first, last = start and n == 0, stop and n == len(chunks) - 1
                    pe.matmul(bank, lhs[0](c), rhs[0](c), start=first, stop=False)
                    pe.matmul(bank, lhs[0](c), rhs[1](c), start=False, stop=False)
                    mm = pe.matmul(bank, lhs[1](c), rhs[0](c), start=False, stop=last)
                return mm

            def pair(whi, wlo, hhi, hlo, used, tile_ready=None, turn=None):
                for st in range(NS):
                    cols = slice(st * TILE, (st + 1) * TILE)
                    if tile_ready:
                        tile_ready(st)
                    for e in range(2):
                        if used is not None:
                            pe.wait_ge(s_free[2 * st + e], used)
                        product(ps[2 * st + e],
                                (lambda k: whi[:, e, k], lambda k: wlo[:, e, k]),
                                (lambda k: hhi[:, k, cols], lambda k: hlo[:, k, cols]),
                                range(KD), before=turn and (lambda k: turn(st, e, k))).then_inc(s_pair[2 * st + e], 1)

            def turn_x(g):
                pe.wait_ge(s_xn, g + 1)
                for b in range(2):
                    free_aux(b, aux_x(g))
                    for k in range(4):
                        c = (4 * b + k) * P
                        mm = pe.transpose(ps[6 + b][:, k * P:(k + 1) * P], xt[g % 3][:, c:c + P], ident[:, :])
                    mm.then_inc(s_aux_done[b], 1)

            def free_aux(b, use):
                turned = sum(aux_x(g) < use for g in range(NT))
                gates = sum(aux_g(u, st) < use for u in range(UNITS) for st in range(NS))
                if turned:
                    pe.wait_ge(s_hlo, 2 * (turned - 1) + b + 1)
                if gates:
                    pe.wait_ge(s_rr if b == 0 else s_ir, gates)

            def norm_mean(m, bank):
                pe.wait_ge(s_nld[m], 32)
                for j in range(NJ):
                    mm = pe.matmul(ps[bank], mean_w[:, :], nd[m][:, j], start=j == 0, stop=j == NJ - 1)
                mm.then_inc(s_mean, 1)

            def norm_var(m, bank):
                pe.wait_ge(s_sq, m + 1)
                for j in range(NJ):
                    mm = pe.matmul(ps[bank], mean_w[:, :], nsq[m][:, j], start=j == 0, stop=j == NJ - 1)
                mm.then_inc(s_var, 1)

            def norm_sums(bank, squares, done):
                for t in range(TILE // P):
                    for j in range(NJ):
                        mm = pe.matmul(ps[bank][:, t:t + 1], squares[:, j, t * P:(t + 1) * P], mean_w[:, 0:1],
                                       start=j == 0, stop=j == NJ - 1)
                mm.then_inc(done, 1)

            def norm_sums_lru(m, bank):
                pe.wait_ge(s_sqy, m + 1)
                norm_sums(bank, ny[m], s_rm2)

            def norm_sums_cm(m, bank):
                pe.wait_ge(s_sq2, m + 1)
                norm_sums(bank, nsq[m], s_rm1)

            pe.wait_ge(s_init, 10)
            turn_x(0)
            pe.wait_ge(s_par, 16 * 11)
            for j in range(NJ):
                mm = pe.transpose(ps[3][:, j * NR:(j + 1) * NR], par_rows[0:NR, j * P:(j + 1) * P], ident[0:NR, 0:NR])
            mm.then_inc(s_part, 1)
            for g in range(1, TPH // 2):
                turn_x(g)

            def project(q):
                h, r = divmod(q, 2 * NJ)
                pe.wait_ge(s_wlo, q + 1)

                def tiles(st):
                    pe.wait_ge(s_hlo, 2 * (h * TPH + (st + 1) * TILE // P))
                    if q == 0 and st == 1:
                        pe.wait_ge(s_parc, 1)

                def turn(st, e, k):
                    if q % 2 == 1 and q > 1 and (st, e, k) == GATES_REST:
                        gates_tile(q // 2 - 1, 1)
                    if r == 0 and (st, e, k) in TURN_REST:
                        turn_x(h * TPH + TURN_REST[st, e, k])
                    if r == 2 * NJ - 1 and h + 1 < NH and (st, e, k) in TURN_FIRST:
                        turn_x((h + 1) * TPH + TURN_FIRST[st, e, k])

                pair(w_hi[q % 2], w_lo[q % 2], h_hi, h_lo, q if q else None, tiles if r == 0 else None, turn)

            def gates_ready(u):
                pe.wait_ge(s_clo, u + 1)
                if u == 0:
                    pe.wait_ge(s_gws, 2)
                if u == N0:
                    pe.wait_ge(s_dc, 1)
                if u == N0 + 1:
                    pe.wait_ge(s_rsty, 1)
                    pe.wait_ge(s_nstd, 1)
                if u == N0 + 2:
                    pe.wait_ge(s_rsts, 1)

            def gates_tile(u, st):
                j = u % NJ
                cols = slice(st * TILE, (st + 1) * TILE)
                for e in range(2):
                    free_aux(e, aux_g(u, st))
                    product(ps[6 + e], (lambda c: gw_hi[:, j, e], lambda c: gw_lo[:, j, e]),
                            (lambda c: c_hi[:, cols], lambda c: c_lo[:, cols]), range(1)
                            ).then_inc(s_aux_done[e], 1)

            for u in range(UNITS):
                project(2 * u)
                if u >= 1:
                    gates_ready(u - 1)
                    gates_tile(u - 1, 0)
                project(2 * u + 1)
                if u >= N0:
                    pe.wait_ge(s_rr, NS * u)
                    pe.wait_ge(s_ir, NS * u)
                if u == N0:
                    norm_mean(0, 6)
                if u == N0 + 1:
                    norm_var(0, 7)
                    norm_sums_lru(0, 6)
                if u == N0 + 2:
                    norm_sums_cm(0, 6)
            gates_ready(UNITS - 1)
            for st in range(NS):
                gates_tile(UNITS - 1, st)
            for b in range(2):
                pe.wait_ge(s_free[b], PPAIRS)
            norm_mean(1, 0)
            norm_var(1, 1)
            pe.wait_ge(s_dc, 2)
            norm_sums_lru(1, 0)
            pe.wait_ge(s_nstd, 2)
            norm_sums_cm(1, 1)

            def turn_h2(w):
                pe.wait_ge(s_hn, w + 1)
                for b in range(2):
                    if w:
                        pe.wait_ge(s_h2lo, 2 * (w - 1) + b + 1)
                    for k in range(4):
                        c = (4 * b + k) * P
                        mm = pe.transpose(ps[2 + b][:, k * P:(k + 1) * P], hn[w % 2][:, c:c + P], ident[:, :])
                    mm.then_inc(s_tr[b], 1)

            for b in range(4):
                pe.wait_ge(s_free[b], PPAIRS)
            pe.wait_ge(s_dcopy, UNITS)
            free_aux(0, AUX_USES)
            free_aux(1, AUX_USES)
            pe.wait_ge(s_wlo, PPAIRS + WOQ)
            for w in range(NT):
                s = w % 2
                pe.wait_ge(s_ylo, w + 1)
                for dh in range(2):
                    cols = slice(dh * TILE, (dh + 1) * TILE)
                    for group in range(2):
                        if w:
                            pe.wait_ge(s_outf[2 * dh + group], w)
                        product(ps[4 + 2 * dh + group],
                                (lambda k: y_hi[s][:, k], lambda k: y_lo[s][:, k]),
                                (lambda k: wo_hi[:, k, cols], lambda k: wo_lo[:, k, cols]),
                                range(group * NJ, (group + 1) * NJ)).then_inc(s_out[2 * dh + group], 1)
                if w >= 1:
                    turn_h2(w - 1)
                for m in (2, 3):
                    at_step = w - 2 * (m - 2)
                    if at_step == 0:
                        pe.wait_ge(*((s_rsty, 2) if m == 2 else (s_dc, 3)))
                        norm_mean(m, 0)
                    if at_step == 1:
                        pe.wait_ge(*((s_rsts, 2) if m == 2 else (s_rsty, 3)))
                        norm_var(m, 1)
                    if at_step == 2:
                        pe.wait_ge(s_nstd, m + 1)
                        norm_sums_lru(m, 1)
                    if at_step == 3:
                        pe.wait_ge(s_dc, 4)
                        if m == 3:
                            pe.wait_ge(s_rsts, 3)
                        norm_sums_cm(m, 0)
            turn_h2(NT - 1)

            Q0 = PPAIRS + WOQ
            pe.wait_ge(s_h2lo, 2 * NT)
            for h in range(NH):
                if h:
                    for st in range(NS):
                        pe.wait_ge(s_h2ld[st], 32)
                with pe.Fori(0, FI) as i:
                    for b in range(2):
                        pe.wait_ge(s_wlo, Q0 + 2 * FI * h + b + 1 + 2 * i)
                        pair(wf_hi[b], wf_lo[b], h2_hi, h2_lo, PPAIRS + 2 * FI * h + b + 2 * i)
                    pe.wait_ge(s_wdlo, FI * h + 1 + i)
                    for t0 in range(0, TPH, 2):
                        for c in range(2):
                            if c == 0 and t0 == 0:
                                pe.wait_ge(s_flo, 4 * FI * h + 2 + 4 * i)
                            if c == 1 and t0 in (0, TPH // 2):
                                pe.wait_ge(s_flo, 4 * FI * h + (3 if t0 == 0 else 4) + 4 * i)
                            for e in range(4):
                                t, dh = t0 + e // 2, e % 2
                                rows, cols = slice(t * P, (t + 1) * P), slice(dh * TILE, (dh + 1) * TILE)
                                if c == 0:
                                    pe.wait_ge(s_outf[e], NT + 4 * FI * h + t0 // 2 + 4 * i)
                                mm = product(ps[4 + e], (lambda n: f_hi[n][:, rows], lambda n: f_lo[n][:, rows]),
                                             (lambda n: wd_hi[:, n, cols], lambda n: wd_lo[:, n, cols]),
                                             [c], start=c == 0, stop=c == 1)
                                if c == 1:
                                    mm.then_inc(s_out[e], 1)


_INS = ["x", "norm_mix", "w_in", "conv4_w", "conv4_b", "gate_a_w", "gate_a_b", "gate_x_w", "gate_x_b",
        "lru_lambda", "dw31_w", "dw31_b", "cm_ln_g", "cm_ln_b", "out_norm_lru", "out_norm_cm", "w_out",
        "norm_ffn", "w_gate", "w_up", "w_down", "norm_final"]


def kernel(**inputs):
    import numpy as np
    from concourse import bacc
    from concourse.bass_utils import run_bass_kernel_spmd

    nc = bacc.Bacc("TRN2", target_bir_lowering=False, num_devices=1, dynamic_dma_scratch_size=SCRATCH)
    arrays, args = {}, []
    for name in _INS:
        a = np.ascontiguousarray(inputs[name])
        arrays[f"in_{name}"] = a
        args.append(nc.dram_tensor(f"in_{name}", a.shape, mybir.dt.from_np(a.dtype), kind="ExternalInput").ap())
    shape = inputs["x"].shape
    args.append(nc.dram_tensor("out_block", shape, F32, kind="ExternalOutput").ap())
    hybrid_block(nc, *args)
    r = run_bass_kernel_spmd(nc, [arrays], core_ids=[0])
    return r.results[0]["out_block"]
```

```python
from contextlib import ExitStack

import concourse.bass as bass
from concourse import mybir

ALU = mybir.AluOpType
ACT = mybir.ActivationFunctionType
F32 = mybir.dt.float32
F32R = mybir.dt.float32r
BF16 = mybir.dt.bfloat16

P = 128
TILE = 512
KIB = 1024
EPS = 1e-6
LRU_C = 8.0
SCRATCH = 1024


def hybrid_block(nc, x, norm_mix, w_in, conv4_w, conv4_b, gate_a_w, gate_a_b, gate_x_w, gate_x_b,
                 lru_lambda, dw31_w, dw31_b, cm_ln_g, cm_ln_b, out_norm_lru, out_norm_cm,
                 w_out, norm_ffn, w_gate, w_up, w_down, norm_final, out):
    S, D = x.shape[1], x.shape[2]
    CH = conv4_b.shape[1]
    NJ = CH // P
    KD = D // P
    F = w_gate.shape[2]
    TAPS4, TAPS31 = conv4_w.shape[1], dw31_w.shape[1]
    HALF = 2 * TILE
    NH = S // HALF
    NS = HALF // TILE
    NT = S // P
    TPH = HALF // P
    UNITS = NH * NJ
    PPAIRS = 2 * UNITS
    FI = F // P // 2
    WOQ = KD // 2
    HD = gate_a_w.shape[2]
    PAD4, PAD31 = TAPS4 - 1, TAPS31 - 1
    assert D == 2 * CH == 1024 and F % (2 * P) == 0 and S == NH * HALF and NH == 2

    xr = x.rearrange("a (t p) d -> (a t) p d", p=P)
    outr = out.rearrange("a (t p) d -> (a t) p d", p=P)
    w_in_r = w_in.rearrange("a (k p) n -> p (a k) n", p=P)
    w_out_r = w_out.rearrange("a (k p) n -> p (a k) n", p=P)
    w_gate_r = w_gate.rearrange("a (k p) n -> p (a k) n", p=P)
    w_up_r = w_up.rearrange("a (k p) n -> p (a k) n", p=P)
    w_down_r = w_down.rearrange("a (k p) n -> p (a k) n", p=P)

    R_DW, R_DWB = 0, TAPS31
    R_C4 = R_DWB + 1
    R_C4B = R_C4 + TAPS4
    R_BA, R_BX, R_LAM, R_LNG, R_LNB, R_ONL, R_ONC = range(R_C4B + 1, R_C4B + 8)
    NR = R_ONC + 1

    d_scr = nc.dram_tensor("d_scr", [NJ, P, S], F32).ap()
    y_scr = nc.dram_tensor("y_scr", [NJ, P, S], F32).ap()
    hhi_scr = nc.dram_tensor("hhi_scr", [P, KD, HALF], F32).ap()
    hlo_scr = nc.dram_tensor("hlo_scr", [P, KD, HALF], F32).ap()
    x2_scr = nc.dram_tensor("x2_scr", [TPH, P, D], F32).ap()

    with ExitStack() as ctx:
        base = (nc.sbuf_base + 63) // 64 * 64

        def at(name, shape, dt, offset):
            return nc.alloc_sbuf_tensor_at(name, shape, dt, offset=base + offset)

        def sem(name):
            return ctx.enter_context(nc.semaphore(name))

        h_hi = at("h_hi", [P, KD, HALF], F32R, 0)
        h_lo = at("h_lo", [P, KD, HALF], F32R, 32 * KIB)
        wo_hi = at("wo_hi", [P, KD, D], F32R, 0)
        wo_lo = at("wo_lo", [P, KD, D], F32R, 32 * KIB)
        wf_hi = [at(f"wf_hi{s}", [P, 2, KD, P], F32R, 16 * s * KIB) for s in range(2)]
        wf_lo = [at(f"wf_lo{s}", [P, 2, KD, P], F32R, (8 + 16 * s) * KIB) for s in range(2)]
        wd_hi = at("wd_hi", [P, 2, D], F32R, 32 * KIB)
        wd_lo = at("wd_lo", [P, 2, D], F32R, 40 * KIB)
        f_hi = [at(f"f_hi{b}", [P, HALF], F32R, (48 + 4 * b) * KIB) for b in range(2)]
        f_lo = [at(f"f_lo{b}", [P, HALF], F32R, (56 + 4 * b) * KIB) for b in range(2)]
        w_hi = [at(f"w_hi{s}", [P, 2, KD, P], F32R, (64 + 16 * s) * KIB) for s in range(2)]
        w_lo = [at(f"w_lo{s}", [P, 2, KD, P], F32R, (72 + 16 * s) * KIB) for s in range(2)]
        gel = [at(f"gel{s}", [P, HALF], F32, (96 + 4 * s) * KIB) for s in range(2)]
        cv = [at(f"cv{s}", [P, HALF], F32, (104 + 4 * s) * KIB) for s in range(2)]
        c_hi = at("c_hi", [P, HALF], F32R, 112 * KIB)
        c_lo = at("c_lo", [P, HALF], F32R, 116 * KIB)
        gw_hi = at("gw_hi", [P, NJ, 2, P], F32R, 120 * KIB)
        gw_lo = at("gw_lo", [P, NJ, 2, P], F32R, 124 * KIB)
        h2_hi = at("h2_hi", [P, KD, HALF], F32R, 64 * KIB)
        h2_lo = at("h2_lo", [P, KD, HALF], F32R, 96 * KIB)
        w_raw = [at(f"w_raw{s}", [P, 2, KD, P], F32, (128 + 8 * s) * KIB) for s in range(2)]
        t_hi = [at(f"t_hi{s}", [P, KD, P], F32R, (128 + 8 * s) * KIB) for s in range(2)]
        t_lo = [at(f"t_lo{s}", [P, KD, P], F32R, (132 + 8 * s) * KIB) for s in range(2)]
        uw = at("uw", [P, HALF], F32, 144 * KIB)
        su = at("su", [P, HALF], F32, 148 * KIB)
        ib = at("ib", [P, HALF], F32, 152 * KIB)
        sg = at("sg", [P, HALF], F32, 156 * KIB)
        dst = [at(f"dst{s}", [P, HALF], F32, (160 + 4 * s) * KIB) for s in range(2)]
        y_raw = [at(f"y_raw{n}", [P, KD, P], F32, o * KIB) for n, o in enumerate((90, 112, 144, 148))]
        y_hi = [at(f"y_hi{n}", [P, KD, P], F32R, o * KIB) for n, o in enumerate((104, 120, 152, 160))]
        y_lo = [at(f"y_lo{n}", [P, KD, P], F32R, o * KIB) for n, o in enumerate((96, 124, 156, 164))]
        wd_raw = at("wd_raw", [P, 2, D], F32, 144 * KIB)
        act_gate = [at(f"act_gate{n}", [P, TILE], F32, (152 + 2 * n) * KIB) for n in range(4)]
        xt = [at(f"xt{s}", [P, D], F32, (168 + 4 * s) * KIB) for s in range(3)]
        gw_raw = at("gw_raw", [P, NJ, 2, P], F32, 180 * KIB)
        acc2 = at("acc2", [P, HALF], F32, 180 * KIB)
        xl = at("xl", [P, HALF + 32], F32, 184 * KIB)
        glu = [at(f"glu{s}", [P, HALF + 32], F32, 184 * KIB + 4224 * (1 + s)) for s in range(2)]
        x2 = at("x2", [P, TPH, D], F32, 168 * KIB)
        nd = [at(f"nd{m}", [P, NJ, TILE], F32, o * KIB) for m, o in enumerate((168, 64, 144, 64))]
        nrs = [at(f"nrs{m}", [P, TILE], F32, o * KIB) for m, o in enumerate((176, 88, 94, 88))]
        ny = [at(f"ny{m}", [P, NJ, TILE], F32, o * KIB) for m, o in enumerate((200, 72, 152, 72))]
        nsq = [at(f"nsq{m}", [P, NJ, TILE], F32, o * KIB) for m, o in enumerate((208, 80, 160, 80))]
        g_row = at("g_row", [P, D], F32, 200 * KIB)
        gfin = at("gfin", [P, D], F32, 204 * KIB)
        hn = [at(f"hn{s}", [P, D], F32, (208 + 4 * s) * KIB) for s in range(2)]
        junk = at("junk", [P, D], BF16, 216 * KIB)
        o = 218 * KIB

        def small(name, n, dt=F32):
            nonlocal o
            t = at(name, [P, n], dt, o)
            o += (4 * n + 31) // 32 * 32
            return t

        ident = small("ident", P)
        mean_w = small("mean_w", P)
        par = small("par", NJ * NR)
        rate = small("rate", NJ)
        rate2 = small("rate2", NJ)
        sp = [small(f"sp{n}", NJ) for n in range(4)]
        ssq = small("ssq", NT)
        rstd = small("rstd", NT)
        rms = small("rms", 2 * NT)
        xh = small("xh", NJ * PAD4)
        gh = small("gh", NJ * PAD31)
        hl = small("hl", NJ)
        eps = small("eps", 1)
        one = small("one", 1)
        two = small("two", 1)
        assert base + o <= nc.sbuf_usable_end, (base, o)
        par_rows = hn[0]

        def col(j, r):
            return par[:, j * NR + r:j * NR + r + 1]

        ps = [ctx.enter_context(nc.psum_tensor(f"ps{b}", [P, TILE], F32)) for b in range(4)]
        acc = ctx.enter_context(nc.psum_tensor("acc", [P, HALF], F32))
        ps += [acc[:, 0:TILE], acc[:, TILE:HALF]]
        ps += [ctx.enter_context(nc.psum_tensor(f"ps{b}", [P, TILE], F32)) for b in (6, 7)]
        ps = [b[:, :] for b in ps]
        f32 = lambda ap: ap.bitcast(F32)

        s_par = sem("par_loaded")
        s_gw = sem("gate_weights_loaded")
        s_gmix = sem("g_row_loaded")
        s_gfin = sem("gfin_loaded")
        s_init = sem("pool_constants")
        s_part = sem("par_transposed")
        s_parc = sem("par_copied")
        s_rate = sem("rate_ready")
        s_dve = sem("dve_step")
        s_act = sem("act_step")
        s_gws = sem("gate_weights_split")
        s_x = [sem(f"x_loaded{s}") for s in range(3)]
        s_std = sem("std_ready")
        s_xn = sem("x_normed")
        s_hhi = sem("h_hi_ready")
        s_hlo = sem("h_lo_ready")
        s_aux_done = [sem(f"aux_done{b}") for b in range(2)]
        s_rr = sem("r_ready")
        s_w = [sem(f"w_loaded{s}") for s in range(2)]
        s_whi = sem("w_hi_ready")
        s_wlo = sem("w_lo_ready")
        s_pair = [sem(f"pair_done{b}") for b in range(4)]
        s_free = [sem(f"pair_free{b}") for b in range(4)]
        s_tap0 = sem("tap0_done")
        s_conv4 = sem("conv4_done")
        s_chi = sem("c_hi_ready")
        s_clo = sem("c_lo_ready")
        s_glu = sem("glu_done")
        s_conv31 = sem("conv31_done")
        s_dcopy = sem("d_copied")
        s_dadd = sem("d_complete")
        s_te = sem("tanh_and_exp_ready")
        s_p = sem("one_minus_a_ready")
        s_q = sem("a2_minus_one_ready")
        s_root = sem("root_ready")
        s_a = sem("a_ready")
        s_ir = sem("i_ready")
        s_ic = sem("ic_done")
        s_sic = sem("sqrt_times_ic")
        s_h = sem("scan_done")
        s_hl = sem("last_state_kept")
        s_fin = sem("unit_final")
        s_dst = [sem(f"d_stored{s}") for s in range(2)]
        s_yst = [sem(f"y_stored{s}") for s in range(2)]
        s_nld = [sem(f"norm_loaded{m}") for m in range(S // TILE)]
        s_fold = sem("chunks_summed")
        s_mean = sem("mean_done")
        s_dc = sem("centred")
        s_sq = sem("squares_ready")
        s_var = sem("var_done")
        s_nstd = sem("ln_std")
        s_dn = sem("ln_scaled")
        s_ysw = sem("swish_done")
        s_sq2 = sem("squares2_ready")
        s_sqy = sem("squares_lru_ready")
        s_rm1 = sem("rms_cm_done")
        s_rm2 = sem("rms_lru_done")
        s_rsty = sem("rms_lru_read")
        s_rsts = sem("rms_cm_read")
        s_rms = sem("rms_ready")
        s_yswst = [sem(f"swish_stored{m}") for m in range(S // TILE)]
        s_yl = [sem(f"y_loaded{s}") for s in range(2)]
        s_yhi = sem("y_hi_ready")
        s_ylo = sem("y_lo_ready")
        s_out = [sem(f"out_bank_done{b}") for b in range(4)]
        s_outf = [sem(f"out_bank_read{b}") for b in range(4)]
        s_xr = [sem(f"residual_loaded{n}") for n in range(4)]
        s_tr = [sem(f"turned{b}") for b in range(2)]
        s_std2 = sem("std2_ready")
        s_hn = sem("hn_ready")
        s_h2hi = sem("h2_hi_ready")
        s_h2lo = sem("h2_lo_ready")
        s_h2st = [sem(f"h2_stored{n}") for n in range(2)]
        s_x2st = [sem(f"x2_stored{n}") for n in range(2)]
        s_wd = sem("w_down_loaded")
        s_wdhi = sem("wd_hi_ready")
        s_wdlo = sem("wd_lo_ready")
        s_fhi = sem("f_hi_ready")
        s_flo = sem("f_lo_ready")
        s_h2ld = [sem(f"h2_reloaded{st}") for st in range(NS)]
        s_x2ld = sem("x2_reloaded")
        s_fstd = sem("final_std")
        s_o = sem("out_row_ready")
        s_ost = [sem(f"out_stored{n}") for n in range(2)]

        HALVES = (1, 0)
        N0 = NJ + 1
        LEAD = 3
        even, odd = list(range(0, TAPS31, 2)), list(range(1, TAPS31, 2))
        TAP_ORDER = even[:LEAD]
        for n in range(len(odd)):
            TAP_ORDER += [odd[n]] + even[LEAD + n:LEAD + n + 1]
        CONV4_AT, SCAN_AT, CENTRE_AT, LATE_AT = 19, 21, 16, 27
        W_OUT_AT = (12, 14, 17, 19)
        CENTRE_AT_LAST, ROW0_AT = 16, 24
        CONV4_AT_X = 18
        X_NORM_AT = (7, 8, 9, 10, 12, 13, 14, 15)
        X_LO_AT = (9, 10, 11, 12, 14, 15, 16, 17)
        CONV4_AT_LAST, SCAN_AT_LAST = 9, 11
        NORM_STEP = {2: 2, 3: 5}
        TURN_FIRST = {(1, 0, 0): 0, (1, 0, 4): 1, (1, 1, 0): 2, (1, 1, 4): 3}
        TURN_REST = {(0, 0, 1): 4, (0, 0, 5): 5, (0, 1, 1): 6, (0, 1, 5): 7}
        GATES_REST = (0, 0, 5)
        NORM_BETWEEN = (0, 1, 2)
        TURN_LAST = {(0, 0, 0): NT - 2, (0, 0, 7): NT - 1}

        def aux_x(g):
            return g if g < TPH else g + NS * (NJ - 1)

        def aux_g(u, st):
            return (TPH if u < NJ - 1 else NT) + NS * u + st

        FOLDS = [(0, "mean"), (0, "lru"), (0, "var"), (1, "var"), (1, "cm")]
        FOLDS += [(2, "mean"), (2, "var"), (2, "lru"), (3, "mean"), (2, "cm"), (3, "var"), (3, "lru"), (3, "cm")]

        def folded(m, what):
            return 2 * (FOLDS.index((m, what)) + 1)

        def yb(w):
            return w % 2 + 2 * (w // TPH)

        AUX_USES = NT + NS * UNITS

        def turned(w):
            if w < TPH:
                return t_hi[w % 2], t_lo[w % 2], slice(0, P)
            return h2_hi, h2_lo, slice((w - TPH) * P, (w - TPH + 1) * P)

        def w_out_gain(k):
            return col(k % NJ, R_ONL if k < NJ else R_ONC)

        block = ctx.enter_context(nc.Block())

        @block.sync
        def _(sp_):
            def load_pair_from(q, a, b):
                sp_.dma_start(w_raw[q % 2][:, 0], a).then_inc(s_w[q % 2], 16)
                sp_.dma_start(w_raw[q % 2][:, 1], b).then_inc(s_w[q % 2], 16)

            def load_pair(q):
                u, which = divmod(q, 2)
                j = u % NJ
                if q >= 2:
                    sp_.wait_ge(s_wlo, q - 1)
                c0 = 2 * CH * (1 - which) + j * P
                load_pair_from(q, w_in_r[:, :, c0:c0 + P], w_in_r[:, :, c0 + CH:c0 + CH + P])

            def load_x(g):
                if g >= 3:
                    sp_.wait_ge(s_aux_done[1], aux_x(g - 3) + 1)
                sp_.dma_start(xt[g % 3][:, :], xr[g]).then_inc(s_x[g % 3], 16)

            def store_d(u):
                h, j = divmod(u, NJ)
                sp_.wait_ge(s_dadd, u + 1)
                sp_.dma_start(d_scr[j, :, h * HALF:(h + 1) * HALF], dst[u % 2][:, :]).then_inc(s_dst[u % 2], 16)

            def store_y(u):
                h, j = divmod(u, NJ)
                sp_.wait_ge(s_fin, u + 1)
                sp_.dma_start(y_scr[j, :, h * HALF:(h + 1) * HALF], gel[u % 2][:, :]).then_inc(s_yst[u % 2], 16)

            load_x(0)
            sp_.dma_start(g_row[:, :], norm_mix.broadcast_to([P, D])).then_inc(s_gmix, 16)
            load_x(1)
            load_x(2)
            load_pair(0)
            rows = [(dw31_w[0], R_DW, TAPS31), (dw31_b, R_DWB, 1), (conv4_w[0], R_C4, TAPS4), (conv4_b, R_C4B, 1),
                    (gate_a_b, R_BA, 1), (gate_x_b, R_BX, 1), (lru_lambda, R_LAM, 1), (cm_ln_g, R_LNG, 1),
                    (cm_ln_b, R_LNB, 1), (out_norm_lru, R_ONL, 1), (out_norm_cm, R_ONC, 1)]
            for src, r, n in rows:
                sp_.dma_start(par_rows[r:r + n, 0:CH], src).then_inc(s_par, 16)
            sp_.wait_ge(s_init, 1)
            for g, w in enumerate((gate_a_w, gate_x_w)):
                for b in range(P // HD):
                    sp_.dma_start(gw_raw[b * HD:(b + 1) * HD, :, g, b * HD:(b + 1) * HD],
                                  w[0].rearrange("(j b) i o -> b i j o", b=P // HD)[b]).then_inc(s_gw, 16)
            for g in range(3, TPH):
                load_x(g)
                if g == 4:
                    load_pair(1)
            def load_norm(m):
                cols = slice(m * TILE, (m + 1) * TILE)
                sp_.dma_start(nd[m][:, :, :], d_scr[:, :, cols].rearrange("j p s -> p j s")).then_inc(s_nld[m], 16)
                sp_.dma_start(ny[m][:, :, :], y_scr[:, :, cols].rearrange("j p s -> p j s")).then_inc(s_nld[m], 16)

            def store_swish(m):
                cols = slice(m * TILE, (m + 1) * TILE)
                sp_.wait_ge(s_ysw, NJ * (m + 1))
                sp_.dma_start(d_scr[:, :, cols].rearrange("j p s -> p j s"), nd[m][:, :, :]).then_inc(s_yswst[m], 16)

            def units_stored(n):
                for s in range(2):
                    sp_.wait_ge(s_dst[s], 16 * n // 2)
                    sp_.wait_ge(s_yst[s], 16 * n // 2)

            def load_w_out(n):
                q = PPAIRS + n
                sp_.wait_ge(s_wlo, q - 1)
                for e in range(2):
                    sp_.dma_start(w_raw[q % 2][:, e].rearrange("p k c -> p (k c)"),
                                  w_out_r[:, 2 * n + e]).then_inc(s_w[q % 2], 16)

            def load_raw(q):
                if q < PPAIRS:
                    load_pair(q)
                elif q < PPAIRS + WOQ:
                    load_w_out(q - PPAIRS)

            def load_y(w):
                if w >= 2:
                    sp_.wait_ge(s_ylo, w - 1)
                cols = slice(w * P, (w + 1) * P)
                sp_.dma_start(y_raw[yb(w)][:, 0:NJ], y_scr[:, :, cols].rearrange("j p s -> p j s")).then_inc(s_yl[w % 2], 16)
                sp_.dma_start(y_raw[yb(w)][:, NJ:KD], d_scr[:, :, cols].rearrange("j p s -> p j s")).then_inc(s_yl[w % 2], 16)

            def load_residual(w):
                i = w % TPH
                if w >= 4:
                    sp_.wait_ge(s_outf[0], w - 3)
                if w >= TPH:
                    sp_.wait_ge(s_x2st[i % 2], 16 * (i // 2 + 1))
                sp_.dma_start(x2[:, i], xr[w]).then_inc(s_xr[w % 4], 16)

            def store_h2(w):
                cols = slice(w * P, (w + 1) * P)
                sp_.wait_ge(s_hn, w + 1)
                sp_.dma_start(x2_scr[w], x2[:, w]).then_inc(s_x2st[w % 2], 16)
                sp_.wait_ge(s_h2lo, 2 * (w + 1))
                sp_.dma_start(hhi_scr[:, :, cols], f32(t_hi[w % 2][:, :, :])).then_inc(s_h2st[w % 2], 16)
                sp_.dma_start(hlo_scr[:, :, cols], f32(t_lo[w % 2][:, :, :])).then_inc(s_h2st[w % 2], 16)

            load_raw(2)
            load_raw(3)
            for u in range(UNITS):
                if u == NJ - 1:
                    load_raw(2 * u + 4)
                    for g in range(TPH + 3, NT):
                        load_x(g)
                    load_raw(2 * u + 5)
                elif u == UNITS - 1:
                    sp_.wait_ge(s_pair[3], PPAIRS)
                    load_norm(1)
                    store_swish(0)
                    sp_.wait_ge(s_yswst[0], 16)
                    load_y(0)
                else:
                    load_raw(2 * u + 4)
                    load_raw(2 * u + 5)
                if u == NJ - 2:
                    for g in range(TPH, TPH + 3):
                        load_x(g)
                if u >= 1:
                    store_d(u - 1)
                    store_y(u - 1)
                if u == NJ:
                    units_stored(NJ)
                    sp_.wait_ge(s_aux_done[1], aux_x(NT - 1) + 1)
                    load_norm(0)
            load_raw(PPAIRS + 2)
            load_raw(PPAIRS + 3)
            sp_.wait_ge(s_aux_done[1], AUX_USES)
            load_y(1)
            for w in range(3):
                load_residual(w)
            sp_.wait_ge(s_rm2, 1)
            sp_.dma_start(g_row[:, :], norm_ffn.broadcast_to([P, D])).then_inc(s_gmix, 16)
            sp_.dma_start(gfin[:, :], norm_final.rearrange("(a d) -> a d", a=1).broadcast_to([P, D])
                          ).then_inc(s_gfin, 16)
            load_y(2)
            load_y(3)
            store_d(UNITS - 1)
            store_y(UNITS - 1)
            load_residual(3)
            units_stored(UNITS)
            load_norm(2)
            store_swish(1)
            sp_.wait_ge(s_yswst[1], 16)
            for w in range(NT):
                for m, first in NORM_STEP.items():
                    if w == first + 4:
                        store_swish(m)
                        sp_.wait_ge(s_yswst[m], 16)
                        sp_.wait_ge(s_rm2, m + 1)
                        sp_.wait_ge(s_rm1, m + 1)
                if 2 <= w < NT - 2:
                    load_y(w + 2)
                if w == 3:
                    sp_.wait_ge(s_rm2, 2)
                    sp_.wait_ge(s_rm1, 2)
                    load_norm(3)
                if 1 <= w <= TPH:
                    store_h2(w - 1)
                if w + 4 < NT:
                    load_residual(w + 4)

            def load_ffn(q, b, f0):
                load_pair_from(q, w_gate_r[:, :, f0], w_up_r[:, :, f0])

            Q0 = PPAIRS + WOQ
            for n in range(2):
                sp_.wait_ge(s_h2st[n], 16 * TPH)
            for b in range(2):
                sp_.wait_ge(s_wlo, Q0 + b - 1)
                load_ffn(Q0 + b, b, slice(b * P, (b + 1) * P))
            sp_.wait_ge(s_ylo, NT)
            sp_.dma_start(wd_raw[:, :, :], w_down_r[:, 0:2]).then_inc(s_wd, 16)
            for h in range(NH):
                with sp_.Fori(0, FI - 1) as i:
                    for b in range(2):
                        sp_.wait_ge(s_wlo, Q0 + 2 * FI * h + b + 1 + 2 * i)
                        load_ffn(b, b, bass.ds((i + 1) * (2 * P) + b * P, P))
                    sp_.wait_ge(s_wdlo, FI * h + 1 + i)
                    sp_.dma_start(wd_raw[:, :, :], w_down_r[:, bass.ds((i + 1) * 2, 2)]).then_inc(s_wd, 16)
                if h + 1 < NH:
                    for b in range(2):
                        sp_.wait_ge(s_wlo, Q0 + 2 * FI * (h + 1) + b - 1)
                        load_ffn(b, b, slice(b * P, (b + 1) * P))
                    sp_.wait_ge(s_wdlo, FI * (h + 1))
                    sp_.dma_start(wd_raw[:, :, :], w_down_r[:, 0:2]).then_inc(s_wd, 16)
                if h + 1 < NH:
                    for st in range(NS):
                        cols = slice(st * TILE, (st + 1) * TILE)
                        sp_.wait_ge(s_pair[2 * st + 1], PPAIRS + 2 * FI * (h + 1))
                        sp_.dma_start(f32(h2_hi[:, :, cols]), hhi_scr[:, :, cols]).then_inc(s_h2ld[st], 16)
                        sp_.dma_start(f32(h2_lo[:, :, cols]), hlo_scr[:, :, cols]).then_inc(s_h2ld[st], 16)
                for i in range(TPH):
                    n = h * TPH + i
                    sp_.wait_ge(s_o, n + 1)
                    sp_.dma_start(outr[HALVES[h] * TPH + i], hn[n % 2][:, :]).then_inc(s_ost[n % 2], 16)
                    if h + 1 < NH:
                        sp_.dma_start(x2[:, i], x2_scr[i]).then_inc(s_x2ld, 16)
            for n in range(2):
                sp_.wait_ge(s_ost[n], 16 * NT // 2)

        @block.gpsimd
        def _(pool):
            g = nc.gpsimd
            g.memset(gw_raw[:, :, :, :], 0.0).then_inc(s_init, 1)
            g.memset(ident[:, :], 0.0).then_inc(s_init, 1)
            g.memset(mean_w[:, :], 1.0 / CH).then_inc(s_init, 1)
            g.memset(eps[:, :], EPS).then_inc(s_init, 1)
            g.memset(one[:, :], 1.0).then_inc(s_init, 1)
            g.memset(two[:, :], 2.0).then_inc(s_init, 1)
            g.memset(xl[:, 0:PAD4], 0.0).then_inc(s_init, 1)
            g.memset(glu[0][:, 0:PAD31], 0.0).then_inc(s_init, 1)
            g.memset(glu[1][:, 0:PAD31], 0.0).then_inc(s_init, 1)
            pool.wait_ge(s_init, 9)
            g.affine_select(out=ident[:, :], in_=ident[:, :], compare_op=ALU.not_equal, fill=1.0, base=0,
                            pattern=[[-1, P]], channel_multiplier=1).then_inc(s_init, 1)

            def split_lo(q):
                pool.wait_ge(s_whi, q + 1)
                g.tensor_tensor(w_lo[q % 2][:, :, :, :], w_raw[q % 2][:, :, :, :], f32(w_hi[q % 2][:, :, :, :]),
                                ALU.subtract).then_inc(s_wlo, 1)

            def output(u):
                pool.wait_ge(s_h, u + 1)
                g.tensor_tensor(gel[u % 2][:, :], gel[u % 2][:, :], cv[u % 2][:, :], ALU.mult).then_inc(s_fin, 1)

            split_lo(0)
            split_lo(1)

            def gated(u):
                h, j = divmod(u, NJ)
                s = u % 2
                for st in range(NS):
                    t = glu[s][:, PAD31 + st * TILE:PAD31 + (st + 1) * TILE]
                    pool.wait_ge(s_free[2 * st], 2 * u + 1)
                    pool.wait_ge(s_free[2 * st + 1], 2 * u + 1)
                    g.tensor_tensor(t, t, sg[:, st * TILE:(st + 1) * TILE], ALU.mult).then_inc(s_glu, 1)
                halo = gh[:, j * PAD31:(j + 1) * PAD31]
                if h == 0:
                    pool.wait_ge(s_glu, (NS + 1) * u + NS)
                    g.tensor_copy(halo, glu[s][:, HALF:HALF + PAD31]).then_inc(s_glu, 1)
                else:
                    pool.wait_ge(s_conv31, u - 1)
                    g.tensor_copy(glu[s][:, 0:PAD31], halo).then_inc(s_glu, 1)

            def gated_input(u):
                pool.wait_ge(s_ir, NS * (u + 1))
                pool.wait_ge(s_clo, u + 1)
                g.tensor_tensor(cv[u % 2][:, :], cv[u % 2][:, :], ib[:, :], ALU.mult).then_inc(s_ic, 1)

            def decay(u):
                pool.wait_ge(s_te, 2 * (u + 1))
                g.tensor_tensor(uw[:, :], uw[:, :], one[:, 0:1].broadcast_to([P, HALF]), ALU.add).then_inc(s_p, 1)
                pool.wait_ge(s_p, 2 * u + 1)
                g.tensor_tensor(uw[:, :], uw[:, :], su[:, :], ALU.mult).then_inc(s_p, 1)
                pool.wait_ge(s_p, 2 * u + 2)
                g.tensor_tensor(su[:, :], uw[:, :], two[:, 0:1].broadcast_to([P, HALF]), ALU.subtract).then_inc(s_q, 1)
                pool.wait_ge(s_q, 2 * u + 1)
                g.tensor_tensor(su[:, :], su[:, :], uw[:, :], ALU.mult).then_inc(s_q, 1)

            def scan_input(u):
                pool.wait_ge(s_root, u + 1)
                pool.wait_ge(s_ic, u + 1)
                g.tensor_tensor(su[:, :], su[:, :], cv[u % 2][:, :], ALU.mult).then_inc(s_sic, 1)

            def complete_d(u):
                pool.wait_ge(s_dcopy, u + 1)
                g.tensor_tensor(dst[u % 2][:, :], dst[u % 2][:, :], acc2[:, :], ALU.add).then_inc(s_dadd, 1)

            def fold(m, what):
                into = ny[m] if what == "lru" else nsq[m]
                source = nd[m] if what == "mean" else into
                pool.wait_ge(*{"mean": (s_nld[m], 32), "lru": (s_sqy, m + 1), "var": (s_sq, m + 1),
                               "cm": (s_sq2, m + 1)}[what])
                g.tensor_tensor(into[:, 0:2], source[:, 0:2], source[:, 2:4], ALU.add).then_inc(s_fold, 1)
                pool.wait_ge(s_fold, folded(m, what) - 1)
                g.tensor_tensor(into[:, 0], into[:, 0], into[:, 1], ALU.add).then_inc(s_fold, 1)

            gated(0)
            for u in range(UNITS):
                if u == N0:
                    fold(0, "mean")
                if u == N0 + 1:
                    fold(0, "lru")
                    fold(0, "var")
                if u >= 1:
                    complete_d(u - 1)
                if 2 * u + 2 < PPAIRS:
                    split_lo(2 * u + 2)
                if u >= 1:
                    gated_input(u - 1)
                    decay(u - 1)
                    scan_input(u - 1)
                if 2 * u + 3 < PPAIRS:
                    split_lo(2 * u + 3)
                pool.wait_ge(s_chi, u + 1)
                g.tensor_tensor(c_lo[:, :], cv[u % 2][:, :], f32(c_hi[:, :]), ALU.subtract).then_inc(s_clo, 1)
                if u >= 1:
                    output(u - 1)
                if u + 1 < UNITS:
                    gated(u + 1)

            def y_lo_part(w):
                pool.wait_ge(s_yhi, w + 1)
                g.tensor_tensor(y_lo[yb(w)][:, :, :], y_raw[yb(w)][:, :, :], f32(y_hi[yb(w)][:, :, :]),
                                ALU.subtract).then_inc(s_ylo, 1)

            gated_input(UNITS - 1)
            pool.wait_ge(s_yst[0], 16 * UNITS // 2)
            y_lo_part(0)
            decay(UNITS - 1)
            y_lo_part(1)
            scan_input(UNITS - 1)
            fold(1, "var")
            y_lo_part(2)
            complete_d(UNITS - 1)
            output(UNITS - 1)
            fold(1, "cm")
            for w in range(3, NT):
                y_lo_part(w)
                for m, first in NORM_STEP.items():
                    if w == {2: 3, 3: 5}[m]:
                        fold(m, "mean")
                    if w - first == 2:
                        fold(m, "var")
                        fold(m, "lru")
                    if w - first == 4:
                        fold(m, "cm")
            Q0 = PPAIRS + WOQ

            def split_down(count):
                pool.wait_ge(s_wdhi, count)
                g.tensor_tensor(wd_lo[:, :, :], wd_raw[:, :, :], f32(wd_hi[:, :, :]), ALU.subtract).then_inc(s_wdlo, 1)

            def split_ffn(b, count):
                pool.wait_ge(s_whi, count)
                g.tensor_tensor(wf_lo[b][:, :, :, :], w_raw[b][:, :, :, :], f32(wf_hi[b][:, :, :, :]),
                                ALU.subtract).then_inc(s_wlo, 1)

            split_ffn(0, Q0 + 1)
            split_ffn(1, Q0 + 2)
            split_down(1)
            with pool.Fori(0, NH * FI - 1) as i:
                split_ffn(0, Q0 + 3 + 2 * i)
                split_ffn(1, Q0 + 4 + 2 * i)
                split_down(2 + i)

        @block.scalar
        def _(act):
            a = nc.scalar
            steps = [0]

            def step(ins):
                steps[0] += 1
                ins.then_inc(s_act, 1)
                act.wait_ge(s_act, steps[0])

            def split_hi(q):
                act.wait_ge(s_w[q % 2], 32 * (q // 2 + 1))
                if q >= 2:
                    act.wait_ge(s_pair[3], q - 1)
                a.copy(w_hi[q % 2][:, :, :, :], w_raw[q % 2][:, :, :, :]).then_inc(s_whi, 1)

            def x_std(g):
                act.wait_ge(s_x[g % 3], 16 * (g // 3 + 1))
                step(a.activation(junk[:, :], xt[g % 3][:, :], ACT.Square, accum_out=ssq[:, g:g + 1]))
                a.activation(rstd[:, g:g + 1], ssq[:, g:g + 1], ACT.Sqrt, bias=eps[:, 0:1], scale=1.0 / D).then_inc(s_std, 1)

            def x_hi(g):
                i = g % TPH
                for b in range(2):
                    act.wait_ge(s_aux_done[b], aux_x(g) + 1)
                    if g == TPH and b == 0:
                        act.wait_ge(s_pair[1], PPAIRS // NH)
                    if g == TPH + TPH // 2 and b == 0:
                        act.wait_ge(s_pair[3], PPAIRS // NH)
                    a.copy(h_hi[:, 4 * b:4 * b + 4, i * P:(i + 1) * P],
                           ps[6 + b].rearrange("p (k s) -> p k s", k=4)).then_inc(s_hhi, 1)

            def copy_d(u):
                act.wait_ge(s_conv31, u + 1)
                if u >= 2:
                    act.wait_ge(s_dst[u % 2], 16 * (u // 2))
                a.copy(dst[u % 2][:, :], acc[:, :]).then_inc(s_dcopy, 1)

            def squares_lru(m):
                act.wait_ge(s_nld[m], 32)
                a.activation(ny[m][:, :, :], ny[m][:, :, :], ACT.Square).then_inc(s_sqy, 1)

            def squares_cm(m):
                act.wait_ge(s_dc, m + 1)
                a.activation(nsq[m][:, :, :], nd[m][:, :, :], ACT.Square).then_inc(s_sq, 1)

            def norm_std(m, bank):
                act.wait_ge(s_var, m + 1)
                a.activation(nrs[m][:, :], ps[bank], ACT.Sqrt, bias=eps[:, 0:1]).then_inc(s_nstd, 1)

            def norm_rms_lru(m, bank):
                act.wait_ge(s_rm2, m + 1)
                a.activation(rms[:, 8 * m:8 * m + 8:2], ps[bank][:, 0:4], ACT.Sqrt, bias=eps[:, 0:1]).then_inc(s_rsty, 1)

            def norm_rms_cm(m, bank):
                act.wait_ge(s_rm1, m + 1)
                a.activation(rms[:, 8 * m + 1:8 * m + 8:2], ps[bank][:, 0:4], ACT.Sqrt, bias=eps[:, 0:1]).then_inc(s_rsts, 1)

            def norm_swish(m):
                act.wait_ge(s_dn, m + 1)
                for j in range(NJ):
                    a.activation(nd[m][:, j], nd[m][:, j], ACT.Silu, scale=col(j, R_LNG), bias=col(j, R_LNB)
                                 ).then_inc(s_ysw, 1)
                act.wait_ge(s_ysw, NJ * (m + 1))
                a.activation(nsq[m][:, :, :], nd[m][:, :, :], ACT.Square).then_inc(s_sq2, 1)

            def evacuate(u, st, first):
                s = u % 2
                cols = slice(st * TILE, (st + 1) * TILE)
                done = 2 * u + (1 if first else 2)
                act.wait_ge(s_pair[2 * st], done)
                if first:
                    if st == 0 and u >= 2:
                        act.wait_ge(s_conv31, u - 1)
                        act.wait_ge(s_glu, (NS + 1) * (u - 1))
                    a.copy(glu[s][:, PAD31 + st * TILE:PAD31 + (st + 1) * TILE], ps[2 * st]).then_inc(s_free[2 * st], 1)
                else:
                    if st == 0 and u >= 1:
                        act.wait_ge(s_conv4, u)
                    a.copy(xl[:, PAD4 + st * TILE:PAD4 + (st + 1) * TILE], ps[2 * st]).then_inc(s_free[2 * st], 1)
                    if st == NS - 1:
                        tap0(u)
                act.wait_ge(s_pair[2 * st + 1], done)
                if first:
                    if u >= 1:
                        act.wait_ge(s_glu, (NS + 1) * (u - 1) + st + 1)
                    a.activation(sg[:, cols], ps[2 * st + 1], ACT.Sigmoid).then_inc(s_free[2 * st + 1], 1)
                else:
                    if st == 0 and u >= 2:
                        act.wait_ge(s_yst[s], 16 * (u // 2))
                    a.activation(gel[s][:, cols], ps[2 * st + 1], ACT.Gelu_apprx_tanh).then_inc(s_free[2 * st + 1], 1)

            def tap0(u):
                h, j = divmod(u, NJ)
                halo = xh[:, j * PAD4:(j + 1) * PAD4]
                act.wait_ge(s_free[2], 2 * u + 2)
                if h == 0:
                    step(a.copy(halo, xl[:, HALF:HALF + PAD4]))
                else:
                    step(a.copy(xl[:, 0:PAD4], halo))
                if u >= 2:
                    act.wait_ge(s_fin, u - 1)
                a.activation(cv[u % 2][:, :], xl[:, 0:HALF], ACT.Identity, scale=col(j, R_C4), bias=col(j, R_C4B)
                             ).then_inc(s_tap0, 1)

            def gates(u):
                j = u % NJ
                for st in range(NS):
                    cols = slice(st * TILE, (st + 1) * TILE)
                    act.wait_ge(s_aux_done[0], aux_g(u, st) + 1)
                    if st == 0 and u >= 1:
                        act.wait_ge(s_h, u)
                    a.activation(uw[:, cols], ps[6], ACT.Sigmoid, bias=col(j, R_BA)).then_inc(s_rr, 1)
                    act.wait_ge(s_aux_done[1], aux_g(u, st) + 1)
                    if st == 0 and u >= 1:
                        act.wait_ge(s_ic, u)
                    a.activation(ib[:, cols], ps[7], ACT.Sigmoid, bias=col(j, R_BX)).then_inc(s_ir, 1)

            def gate_functions(u):
                j = u % NJ
                act.wait_ge(s_rr, NS * (u + 1))
                if u == 0:
                    act.wait_ge(s_rate, 3)
                a.activation(su[:, :], uw[:, :], ACT.Tanh, scale=rate[:, j:j + 1]).then_inc(s_te, 1)
                a.activation(uw[:, :], uw[:, :], ACT.Exp, scale=rate2[:, j:j + 1]).then_inc(s_te, 1)

            def root(u):
                act.wait_ge(s_q, 2 * (u + 1))
                a.activation(su[:, :], su[:, :], ACT.Sqrt, scale=-1.0).then_inc(s_root, 1)
                a.activation(uw[:, :], uw[:, :], ACT.Identity, scale=-1.0, bias=1.0).then_inc(s_a, 1)

            def c_split(u):
                act.wait_ge(s_conv4, u + 1)
                if u >= 1:
                    act.wait_ge(s_aux_done[1], aux_g(u - 1, NS - 1) + 1)
                a.copy(c_hi[:, :], cv[u % 2][:, :]).then_inc(s_chi, 1)

            act.wait_ge(s_init, 10)
            for g in range(3):
                x_std(g)
            x_hi(0)
            split_hi(0)
            x_hi(1)
            for g in range(3, TPH):
                x_std(g)
                x_hi(g - 1)
            x_hi(TPH - 1)
            act.wait_ge(s_parc, 2)
            a.activation(sp[1][:, :], sp[0][:, :], ACT.Exp).then_inc(s_rate, 1)
            split_hi(1)
            act.wait_ge(s_gw, 16 * 4)
            a.copy(gw_hi[:, :, :, :], gw_raw[:, :, :, :]).then_inc(s_gws, 1)
            for u in range(UNITS):
                evacuate(u, 0, True)
                evacuate(u, 1, True)
                if 2 * u + 2 < PPAIRS:
                    split_hi(2 * u + 2)
                if u >= NJ:
                    gates(u - 1)
                    gate_functions(u - 1)
                    copy_d(u - 1)
                elif u >= 1:
                    copy_d(u - 1)
                    gates(u - 1)
                    gate_functions(u - 1)
                if u == NJ - 1:
                    for g in range(TPH, TPH + 3):
                        x_std(g)
                if u == N0 + 2:
                    norm_swish(0)
                evacuate(u, 0, False)
                if u == NJ - 1:
                    x_hi(TPH)
                    x_std(TPH + 3)
                    x_hi(TPH + 1)
                    x_std(TPH + 4)
                    x_hi(TPH + 2)
                    x_hi(TPH + 3)
                    x_std(TPH + 5)
                evacuate(u, 1, False)
                if u == NJ - 1:
                    x_hi(TPH + 4)
                    x_std(TPH + 6)
                if u == NJ - 1:
                    x_hi(TPH + 5)
                    x_std(TPH + 7)
                    x_hi(TPH + 6)
                if u >= 1:
                    root(u - 1)
                if u == NJ - 1:
                    x_hi(TPH + 7)
                if 2 * u + 3 < PPAIRS:
                    split_hi(2 * u + 3)
                c_split(u)
                if u == N0:
                    squares_lru(0)
                    squares_cm(0)
                if u == N0 + 1:
                    norm_std(0, 7)
                    norm_rms_lru(0, 6)
                if u == N0 + 2:
                    norm_rms_cm(0, 6)

            def w_out_hi(n):
                q = PPAIRS + n
                act.wait_ge(s_w[q % 2], 32 * (q // 2 + 1))
                if n == 0:
                    act.wait_ge(s_pair[3], PPAIRS)
                for e in range(2):
                    ins = a.activation(wo_hi[:, 2 * n + e], w_raw[q % 2][:, e].rearrange("p k c -> p (k c)"),
                                       ACT.Copy, scale=w_out_gain(2 * n + e))
                ins.then_inc(s_whi, 1)

            def y_split(w):
                act.wait_ge(s_yl[w % 2], 32 * (w // 2 + 1))
                if w >= 2:
                    act.wait_ge(s_out[3], w - 1)
                a.copy(y_hi[yb(w)][:, :, :], y_raw[yb(w)][:, :, :]).then_inc(s_yhi, 1)

            w_out_hi(0)
            w_out_hi(1)
            gates(UNITS - 1)
            act.wait_ge(s_fin, UNITS - 1)
            y_split(0)
            gate_functions(UNITS - 1)
            w_out_hi(2)
            w_out_hi(3)
            squares_lru(1)
            y_split(1)
            squares_cm(1)
            root(UNITS - 1)
            y_split(2)
            norm_rms_lru(1, 7)
            norm_std(1, 6)
            copy_d(UNITS - 1)

            Q0 = PPAIRS + WOQ

            def ffn_hi(b, loaded, used):
                act.wait_ge(s_w[b], loaded)
                if used is not None:
                    act.wait_ge(s_pair[3], used)
                a.copy(wf_hi[b][:, :, :, :], w_raw[b][:, :, :, :]).then_inc(s_whi, 1)

            def down_hi(loaded, used):
                act.wait_ge(s_wd, loaded)
                if used is not None:
                    act.wait_ge(s_out[3], used)
                a.copy(wd_hi[:, :, :], wd_raw[:, :, :]).then_inc(s_wdhi, 1)

            def h2_hi(w):
                hi, _, cols = turned(w)
                if w == 0:
                    act.wait_ge(s_wlo, PPAIRS + WOQ)
                elif 2 <= w < TPH:
                    act.wait_ge(s_h2st[w % 2], 32 * (w // 2))
                elif w == TPH:
                    act.wait_ge(s_yswst[3], 16)
                for b in range(2):
                    act.wait_ge(s_tr[b], w + 1)
                    a.copy(hi[:, 4 * b:4 * b + 4, cols],
                           ps[6 + b].rearrange("p (k s) -> p k s", k=4)).then_inc(s_h2hi, 1)

            for w in range(NT):
                if w == 1:
                    norm_swish(1)
                if 2 <= w < NT - 1:
                    y_split(w + 1)
                for m, first in NORM_STEP.items():
                    if w - first == 1:
                        squares_lru(m)
                        squares_cm(m)
                    if w - first == 2:
                        norm_std(m, 5)
                    if w - first == 3:
                        norm_rms_lru(m, 5)
                        norm_swish(m)
                    if w - first == 4:
                        norm_rms_cm(m, 5)
                if w == 3:
                    norm_rms_cm(1, 5)
                if w == NT - 1:
                    act.wait_ge(s_out[1], NT)
                    ffn_hi(0, 16 * (Q0 + 2), None)
                if w >= 1:
                    h2_hi(w - 1)
                act.wait_ge(s_outf[3], w + 1)
                step(a.activation(junk[:, :], x2[:, w % TPH], ACT.Square, accum_out=ssq[:, w:w + 1]))
                a.activation(rstd[:, w:w + 1], ssq[:, w:w + 1], ACT.Sqrt, bias=eps[:, 0:1], scale=1.0 / D
                             ).then_inc(s_std2, 1)

            act.wait_ge(s_out[3], NT)
            ffn_hi(1, 16 * (Q0 + 2), None)
            h2_hi(NT - 1)
            down_hi(16, None)

            def gate_and_hidden(h, i, more):
                for b in range(2):
                    pairs = PPAIRS + 2 * FI * h + b + 1
                    for st in range(NS):
                        n = 2 * b + st
                        act.wait_ge(s_pair[2 * st], pairs + 2 * i)
                        a.activation(act_gate[n][:, :], ps[2 * st], ACT.Silu).then_inc(s_free[2 * st], 1)
                        act.wait_ge(s_free[2 * st + 1], pairs + 2 * i)
                        if n % 2 == 0:
                            act.wait_ge(s_out[3], NT + 4 * FI * h + 4 * i)
                        a.copy(f_hi[b][:, st * TILE:(st + 1) * TILE], act_gate[n][:, :]).then_inc(s_fhi, 1)
                    if more:
                        ffn_hi(b, 16 * (Q0 + 2 * FI * h + 4) + 32 * i, pairs + 2 * i)

            for h in range(NH):
                more = h + 1 < NH
                with act.Fori(0, FI - 1) as i:
                    gate_and_hidden(h, i, True)
                    down_hi(16 * (FI * h + 2) + 16 * i, NT + 4 * (FI * h + 1) + 4 * i)
                gate_and_hidden(h, FI - 1, more)
                for t in range(TPH):
                    bank, use = (2 * t + 1) % 4, (2 * t + 1) // 4
                    act.wait_ge(s_outf[bank], NT + 4 * (FI * (h + 1) - 1) + use + 1)
                    if h and t == 0:
                        act.wait_ge(s_o, TPH)
                    step(a.activation(junk[:, :], x2[:, t], ACT.Square, accum_out=ssq[:, t:t + 1]))
                    a.activation(rstd[:, t:t + 1], ssq[:, t:t + 1], ACT.Sqrt, bias=eps[:, 0:1], scale=1.0 / D
                                 ).then_inc(s_fstd, 1)
                if more:
                    down_hi(16 * (FI * (h + 1) + 1), NT + 4 * FI * (h + 1))

        @block.vector
        def _(dve):
            v = nc.vector
            steps = [0]

            def step(ins):
                steps[0] += 1
                ins.then_inc(s_dve, 1)
                dve.wait_ge(s_dve, steps[0])

            def x_norm(g):
                dve.wait_ge(s_std, g + 1)
                step(v.reciprocal(rstd[:, g:g + 1], rstd[:, g:g + 1]))
                if g == 0:
                    dve.wait_ge(s_gmix, 16)
                v.scalar_tensor_tensor(out=xt[g % 3][:, :], in0=xt[g % 3][:, :], scalar=rstd[:, g:g + 1],
                                       in1=g_row[:, :], op0=ALU.mult, op1=ALU.mult).then_inc(s_xn, 1)

            def x_lo(g):
                i = g % TPH
                for b in range(2):
                    dve.wait_ge(s_hhi, 2 * g + b + 1)
                    cols = slice(i * P, (i + 1) * P)
                    v.tensor_tensor(h_lo[:, 4 * b:4 * b + 4, cols], ps[6 + b].rearrange("p (k s) -> p k s", k=4),
                                    f32(h_hi[:, 4 * b:4 * b + 4, cols]), ALU.subtract).then_inc(s_hlo, 1)

            def parameters():
                dve.wait_ge(s_part, 1)
                v.tensor_copy(par[:, :], ps[3][:, 0:NJ * NR]).then_inc(s_parc, 1)
                dve.wait_ge(s_parc, 1)
                lam = par[:, R_LAM:NJ * NR:NR]
                step(v.tensor_scalar(sp[1][:, :], lam, -1.0, None, ALU.mult))
                v.tensor_tensor(sp[0][:, :], lam, sp[1][:, :], ALU.min).then_inc(s_parc, 1)

            def decay_rate():
                lam = par[:, R_LAM:NJ * NR:NR]
                e, z, z2, poly = sp[1], sp[0], sp[2], sp[3]
                dve.wait_ge(s_rate, 1)
                step(v.tensor_scalar(z[:, :], e[:, :], 2.0, None, ALU.add))
                step(v.reciprocal(z[:, :], z[:, :]))
                step(v.tensor_tensor(z[:, :], z[:, :], e[:, :], ALU.mult))
                step(v.tensor_tensor(z2[:, :], z[:, :], z[:, :], ALU.mult))
                top = 10
                step(v.tensor_scalar(poly[:, :], z2[:, :], 1.0 / (2 * top + 1), 1.0 / (2 * top - 1), ALU.mult, ALU.add))
                for n in range(top - 2, -1, -1):
                    step(v.tensor_tensor(poly[:, :], poly[:, :], z2[:, :], ALU.mult))
                    step(v.tensor_scalar(poly[:, :], poly[:, :], 1.0 / (2 * n + 1), None, ALU.add))
                step(v.tensor_tensor(poly[:, :], poly[:, :], z[:, :], ALU.mult))
                step(v.tensor_scalar(z2[:, :], lam, -1.0, 0.0, ALU.mult, ALU.max))
                step(v.scalar_tensor_tensor(out=poly[:, :], in0=poly[:, :], scalar=2.0, in1=z2[:, :],
                                            op0=ALU.mult, op1=ALU.add))
                v.tensor_scalar(rate[:, :], poly[:, :], LRU_C / 2, None, ALU.mult).then_inc(s_rate, 1)
                v.tensor_scalar(rate2[:, :], poly[:, :], -LRU_C, None, ALU.mult).then_inc(s_rate, 1)

            def gate_weights_lo():
                dve.wait_ge(s_gws, 1)
                v.tensor_tensor(gw_lo[:, :, :, :], gw_raw[:, :, :, :], f32(gw_hi[:, :, :, :]), ALU.subtract
                                ).then_inc(s_gws, 1)

            for g in range(3):
                x_norm(g)
            x_lo(0)
            parameters()
            x_lo(1)
            for g in range(3, TPH):
                x_norm(g)
                x_lo(g - 1)
            x_lo(TPH - 1)
            decay_rate()
            gate_weights_lo()

            def norm_centre(m, bank):
                dve.wait_ge(s_mean, m + 1)
                v.tensor_tensor(nd[m][:, :, :], nd[m][:, :, :], ps[bank][:, None, :].broadcast_to([P, NJ, TILE]),
                                ALU.subtract).then_inc(s_dc, 1)

            def norm_scale(m):
                dve.wait_ge(s_nstd, m + 1)
                step(v.reciprocal(nrs[m][:, :], nrs[m][:, :]))
                dve.wait_ge(s_sq, m + 1)
                v.tensor_tensor(nd[m][:, :, :], nd[m][:, :, :], nrs[m][:, None, :].broadcast_to([P, NJ, TILE]),
                                ALU.mult).then_inc(s_dn, 1)

            def norm_rms(m):
                dve.wait_ge(s_rsty, m + 1)
                dve.wait_ge(s_rsts, m + 1)
                v.reciprocal(rms[:, 8 * m:8 * m + 8], rms[:, 8 * m:8 * m + 8]).then_inc(s_rms, 1)

            def conv4(u):
                s, j = u % 2, u % NJ
                dve.wait_ge(s_tap0, u + 1)
                for k in range(1, TAPS4):
                    ins = v.scalar_tensor_tensor(out=cv[s][:, :], in0=xl[:, k:k + HALF], scalar=col(j, R_C4 + k),
                                                 in1=cv[s][:, :], op0=ALU.mult, op1=ALU.add)
                    if k == TAPS4 - 1:
                        ins.then_inc(s_conv4, 1)
                    else:
                        step(ins)

            def scan(u):
                h, j = divmod(u, NJ)
                s = u % 2
                dve.wait_ge(s_sic, u + 1)
                dve.wait_ge(s_a, u + 1)
                if u == NJ:
                    dve.wait_ge(s_hl, NJ)
                v.tensor_tensor_scan(cv[s][:, :], uw[:, :], su[:, :], 0.0 if h == 0 else hl[:, j:j + 1],
                                     ALU.mult, ALU.add).then_inc(s_h, 1)
                if h == 0:
                    dve.wait_ge(s_h, u + 1)
                    v.tensor_copy(hl[:, j:j + 1], cv[s][:, HALF - 1:HALF]).then_inc(s_hl, 1)

            def w_out_lo(n):
                q = PPAIRS + n
                dve.wait_ge(s_whi, q + 1)
                for e in range(2):
                    k = 2 * n + e
                    ins = v.scalar_tensor_tensor(out=wo_lo[:, k], in0=w_raw[q % 2][:, e].rearrange("p k c -> p (k c)"),
                                                 scalar=w_out_gain(k), in1=f32(wo_hi[:, k]),
                                                 op0=ALU.mult, op1=ALU.subtract)
                ins.then_inc(s_wlo, 1)

            def add_row(w):
                if w == 4:
                    norm_rms(1)
                if w % 4 == 0:
                    dve.wait_ge(s_rms, w // 4 + 1)
                dve.wait_ge(s_xr[w % 4], 16 * (w // 4 + 1))
                row = x2[:, w % TPH]
                for group in range(2):
                    for dh in range(2):
                        e = 2 * group + dh
                        cols = slice(dh * TILE, (dh + 1) * TILE)
                        dve.wait_ge(s_out[e], w + 1)
                        if group:
                            dve.wait_ge(s_outf[dh], w + 1)
                        v.scalar_tensor_tensor(out=row[:, cols], in0=ps[e],
                                               scalar=rms[:, 2 * w + group:2 * w + group + 1],
                                               in1=row[:, cols], op0=ALU.mult, op1=ALU.add).then_inc(s_outf[e], 1)

            def conv31(u):
                j = u % NJ
                t = glu[u % 2]
                last = [0, 0]
                for place, k in enumerate(TAP_ORDER):
                    if u == NJ - 1:
                        for g in range(TPH):
                            if place == X_NORM_AT[g]:
                                x_norm(TPH + g)
                            if place == X_LO_AT[g]:
                                x_lo(TPH + g)
                    if place == {NJ - 1: CONV4_AT_X, UNITS - 1: CONV4_AT_LAST}.get(u, CONV4_AT):
                        conv4(u)
                    if place == CENTRE_AT and u == N0:
                        norm_centre(0, 6)
                    if u >= 1 and place == (SCAN_AT_LAST if u == UNITS - 1 else SCAN_AT):
                        scan(u - 1)
                    if u == UNITS - 1 and place == ROW0_AT:
                        norm_rms(0)
                        add_row(0)
                    if u == UNITS - 1 and place == CENTRE_AT_LAST:
                        norm_centre(1, 6)
                    if u == UNITS - 1 and place in W_OUT_AT:
                        w_out_lo(W_OUT_AT.index(place))
                    if place == LATE_AT:
                        if u == N0 + 1:
                            norm_scale(0)
                    e = k % 2
                    sum_ = (acc, acc2)[e]
                    if k == 0:
                        dve.wait_ge(s_glu, (NS + 1) * (u + 1))
                        if u >= 1:
                            dve.wait_ge(s_dcopy, u)
                        ins = v.tensor_scalar(sum_[:, :], t[:, 0:HALF], col(j, R_DW), col(j, R_DWB), ALU.mult, ALU.add)
                    elif k == 1:
                        if u >= 1:
                            dve.wait_ge(s_dadd, u)
                        ins = v.tensor_scalar(sum_[:, :], t[:, 1:1 + HALF], col(j, R_DW + 1), None, ALU.mult)
                    else:
                        dve.wait_ge(s_dve, steps[0] if place == TAPS31 - 1 else last[e])
                        ins = v.scalar_tensor_tensor(out=sum_[:, :], in0=t[:, k:k + HALF], scalar=col(j, R_DW + k),
                                                     in1=sum_[:, :], op0=ALU.mult, op1=ALU.add)
                    if place == TAPS31 - 1:
                        ins.then_inc(s_conv31, 1)
                    else:
                        steps[0] += 1
                        last[e] = steps[0]
                        ins.then_inc(s_dve, 1)

            for u in range(UNITS):
                conv31(u)
            scan(UNITS - 1)

            def h2_lo(w):
                i = w % TPH
                hi, lo, cols = turned(w)
                for b in range(2):
                    dve.wait_ge(s_h2hi, 2 * w + b + 1)
                    v.tensor_tensor(lo[:, 4 * b:4 * b + 4, cols], ps[6 + b].rearrange("p (k s) -> p k s", k=4),
                                    f32(hi[:, 4 * b:4 * b + 4, cols]), ALU.subtract).then_inc(s_h2lo, 1)

            for w in range(NT):
                i, g = w % TPH, w
                if w:
                    add_row(w)
                if w == 0:
                    norm_scale(1)
                if w >= 1:
                    h2_lo(w - 1)
                dve.wait_ge(s_std2, w + 1)
                step(v.reciprocal(rstd[:, w:w + 1], rstd[:, w:w + 1]))
                if w == 0:
                    dve.wait_ge(s_gmix, 32)
                    dve.wait_ge(s_rm1, 1)
                if w >= 2:
                    dve.wait_ge(s_tr[1], w - 1)
                v.scalar_tensor_tensor(out=hn[w % 2][:, :], in0=x2[:, i], scalar=rstd[:, w:w + 1], in1=g_row[:, :],
                                       op0=ALU.mult, op1=ALU.mult).then_inc(s_hn, 1)
                for m, first in NORM_STEP.items():
                    if w - first == 0:
                        norm_centre(m, 4)
                    if w - first == 2:
                        norm_scale(m)
                    if w - first == 4:
                        norm_rms(m)
            h2_lo(NT - 1)

            def hidden(h, i):
                for b in range(2):
                    pairs = PPAIRS + 2 * FI * h + b + 1
                    for st in range(NS):
                        n = 2 * b + st
                        done = 4 * FI * h + n + 1
                        dve.wait_ge(s_free[2 * st], pairs + 2 * i)
                        dve.wait_ge(s_pair[2 * st + 1], pairs + 2 * i)
                        v.tensor_tensor(act_gate[n][:, :], act_gate[n][:, :], ps[2 * st + 1], ALU.mult
                                        ).then_inc(s_free[2 * st + 1], 1)
                        dve.wait_ge(s_fhi, done + 4 * i)
                        v.tensor_tensor(f_lo[b][:, st * TILE:(st + 1) * TILE], act_gate[n][:, :],
                                        f32(f_hi[b][:, st * TILE:(st + 1) * TILE]), ALU.subtract
                                        ).then_inc(s_flo, 1)

            def down_sum(h, i, e):
                t, dh = divmod(e, 2)
                bank, use = e % 4, e // 4
                if e == 0:
                    for q in range(4):
                        dve.wait_ge(s_outf[q], NT + 4 * FI * h + 4 * i)
                    if h:
                        dve.wait_ge(s_x2ld, 16 * TPH)
                dve.wait_ge(s_out[bank], NT + 4 * FI * h + use + 1 + 4 * i)
                v.tensor_tensor(x2[:, t, dh * TILE:(dh + 1) * TILE], x2[:, t, dh * TILE:(dh + 1) * TILE],
                                ps[4 + bank], ALU.add).then_inc(s_outf[bank], 1)

            def final_row(h, t):
                n = h * TPH + t
                if n == 0:
                    dve.wait_ge(s_gfin, 16)
                dve.wait_ge(s_fstd, n + 1)
                step(v.reciprocal(rstd[:, t:t + 1], rstd[:, t:t + 1]))
                if n >= 2:
                    dve.wait_ge(s_ost[n % 2], 16 * (n // 2))
                v.scalar_tensor_tensor(out=hn[n % 2][:, :], in0=x2[:, t], scalar=rstd[:, t:t + 1], in1=gfin[:, :],
                                       op0=ALU.mult, op1=ALU.mult).then_inc(s_o, 1)

            for h in range(NH):
                with dve.Fori(0, FI - 1) as i:
                    hidden(h, i)
                    for e in range(2 * TPH):
                        down_sum(h, i, e)
                hidden(h, FI - 1)
                for e in range(2 * TPH):
                    down_sum(h, FI - 1, e)
                    for t in {7: (0, 1), 11: (2, 3), 15: (4, 5, 6, 7)}.get(e, ()):
                        final_row(h, t)

        @block.tensor
        def _(pe):
            def product(bank, lhs, rhs, chunks, start=True, stop=True, before=None):
                for n, c in enumerate(chunks):
                    if before:
                        before(c)
                    first, last = start and n == 0, stop and n == len(chunks) - 1
                    pe.matmul(bank, lhs[0](c), rhs[0](c), start=first, stop=False)
                    pe.matmul(bank, lhs[0](c), rhs[1](c), start=False, stop=False)
                    mm = pe.matmul(bank, lhs[1](c), rhs[0](c), start=False, stop=last)
                return mm

            def pair(whi, wlo, hhi, hlo, used, tile_ready=None, turn=None):
                for st in range(NS):
                    cols = slice(st * TILE, (st + 1) * TILE)
                    if tile_ready:
                        tile_ready(st)
                    for e in range(2):
                        if used is not None:
                            pe.wait_ge(s_free[2 * st + e], used)
                        product(ps[2 * st + e],
                                (lambda k: whi[:, e, k], lambda k: wlo[:, e, k]),
                                (lambda k: hhi[:, k, cols], lambda k: hlo[:, k, cols]),
                                range(KD), before=turn and (lambda k: turn(st, e, k))).then_inc(s_pair[2 * st + e], 1)

            def turn_x(g):
                pe.wait_ge(s_xn, g + 1)
                for b in range(2):
                    free_aux(b, aux_x(g))
                    for k in range(4):
                        c = (4 * b + k) * P
                        mm = pe.transpose(ps[6 + b][:, k * P:(k + 1) * P], xt[g % 3][:, c:c + P], ident[:, :])
                    mm.then_inc(s_aux_done[b], 1)

            def free_aux(b, use):
                turned = sum(aux_x(g) < use for g in range(NT))
                gates = sum(aux_g(u, st) < use for u in range(UNITS) for st in range(NS))
                if turned:
                    pe.wait_ge(s_hlo, 2 * (turned - 1) + b + 1)
                if gates:
                    pe.wait_ge(s_rr if b == 0 else s_ir, gates)

            def summed(m, what):
                if (m, what) in FOLDS:
                    pe.wait_ge(s_fold, folded(m, what))
                    return (ny if what == "lru" else nsq)[m], 1
                tile, ready = {"mean": (nd[m], s_nld[m]), "lru": (ny[m], s_sqy),
                               "var": (nsq[m], s_sq), "cm": (nsq[m], s_sq2)}[what]
                pe.wait_ge(ready, 32 if what == "mean" else m + 1)
                return tile, NJ

            def norm_rows(m, what, bank, done):
                tile, chunks = summed(m, what)
                for j in range(chunks):
                    mm = pe.matmul(ps[bank], mean_w[:, :], tile[:, j], start=j == 0, stop=j == chunks - 1)
                mm.then_inc(done, 1)

            def norm_columns(m, what, bank, done):
                tile, chunks = summed(m, what)
                for t in range(TILE // P):
                    for j in range(chunks):
                        mm = pe.matmul(ps[bank][:, t:t + 1], tile[:, j, t * P:(t + 1) * P], mean_w[:, 0:1],
                                       start=j == 0, stop=j == chunks - 1)
                mm.then_inc(done, 1)

            def norm_mean(m, bank):
                norm_rows(m, "mean", bank, s_mean)

            def norm_var(m, bank):
                norm_rows(m, "var", bank, s_var)

            def norm_sums_lru(m, bank):
                norm_columns(m, "lru", bank, s_rm2)

            def norm_sums_cm(m, bank):
                norm_columns(m, "cm", bank, s_rm1)

            pe.wait_ge(s_init, 10)
            turn_x(0)
            pe.wait_ge(s_par, 16 * 11)
            for j in range(NJ):
                mm = pe.transpose(ps[3][:, j * NR:(j + 1) * NR], par_rows[0:NR, j * P:(j + 1) * P], ident[0:NR, 0:NR])
            mm.then_inc(s_part, 1)
            for g in range(1, TPH // 2):
                turn_x(g)

            def project(q):
                h, r = divmod(q, 2 * NJ)
                pe.wait_ge(s_wlo, q + 1)

                def tiles(st):
                    pe.wait_ge(s_hlo, 2 * (h * TPH + (st + 1) * TILE // P))
                    if q == 0 and st == 1:
                        pe.wait_ge(s_parc, 1)

                def turn(st, e, k):
                    if q % 2 == 1 and q > 1 and (st, e, k) == GATES_REST:
                        gates_tile(q // 2 - 1, 1)
                    if q in (2 * N0 + 2, 2 * N0 + 4) and (st, e, k) == NORM_BETWEEN:
                        pe.wait_ge(s_rr, NS * (q // 2 - 1))
                        pe.wait_ge(s_ir, NS * (q // 2 - 1))
                        if q == 2 * N0 + 2:
                            norm_mean(0, 6)
                        else:
                            norm_var(0, 7)
                            norm_sums_lru(0, 6)
                    if r == 0 and (st, e, k) in TURN_REST:
                        turn_x(h * TPH + TURN_REST[st, e, k])
                    if r == 2 * NJ - 1 and h + 1 < NH and (st, e, k) in TURN_FIRST:
                        turn_x((h + 1) * TPH + TURN_FIRST[st, e, k])

                pair(w_hi[q % 2], w_lo[q % 2], h_hi, h_lo, q if q else None, tiles if r == 0 else None, turn)

            def gates_ready(u):
                pe.wait_ge(s_clo, u + 1)
                if u == 0:
                    pe.wait_ge(s_gws, 2)
                if u == N0:
                    pe.wait_ge(s_dc, 1)
                if u == N0 + 1:
                    pe.wait_ge(s_rsty, 1)
                    pe.wait_ge(s_nstd, 1)
                if u == N0 + 2:
                    pe.wait_ge(s_rsts, 1)

            def gates_tile(u, st):
                j = u % NJ
                cols = slice(st * TILE, (st + 1) * TILE)
                for e in range(2):
                    free_aux(e, aux_g(u, st))
                    product(ps[6 + e], (lambda c: gw_hi[:, j, e], lambda c: gw_lo[:, j, e]),
                            (lambda c: c_hi[:, cols], lambda c: c_lo[:, cols]), range(1)
                            ).then_inc(s_aux_done[e], 1)

            for u in range(UNITS):
                project(2 * u)
                if u >= 1:
                    gates_ready(u - 1)
                    gates_tile(u - 1, 0)
                project(2 * u + 1)
            pe.wait_ge(s_rr, NS * (UNITS - 1))
            norm_sums_cm(0, 6)
            gates_ready(UNITS - 1)
            for st in range(NS):
                gates_tile(UNITS - 1, st)
            def turn_h2(w):
                pe.wait_ge(s_hn, w + 1)
                for b in range(2):
                    if w:
                        pe.wait_ge(s_h2lo, 2 * (w - 1) + b + 1)
                    else:
                        pe.wait_ge(s_nstd if b == 0 else s_rsty, 2)
                    for k in range(4):
                        c = (4 * b + k) * P
                        mm = pe.transpose(ps[6 + b][:, k * P:(k + 1) * P], hn[w % 2][:, c:c + P], ident[:, :])
                    mm.then_inc(s_tr[b], 1)

            free_aux(0, AUX_USES)
            norm_mean(1, 6)
            for b in range(4):
                pe.wait_ge(s_free[b], PPAIRS)
            def norm_steps(w):
                if w == NORM_STEP[2] + 1:
                    pe.wait_ge(s_dcopy, UNITS)
                    norm_sums_cm(1, 5)
                for m, first in NORM_STEP.items():
                    if w - first == 1:
                        pe.wait_ge(*((s_dcopy, UNITS) if m == 2 else (s_dc, 3)))
                        norm_mean(m, 4)
                    if w - first == 2:
                        pe.wait_ge(s_rsts, m)
                        norm_var(m, 5)
                    if w - first == 3:
                        pe.wait_ge(s_nstd, m + 1)
                        norm_sums_lru(m, 5)
                    if w - first == 4:
                        pe.wait_ge(s_rsty, m + 1)
                        norm_sums_cm(m, 5)

            for w in range(NT):
                b = yb(w)
                pe.wait_ge(s_ylo, w + 1)
                for group in range(2):
                    if group:
                        norm_steps(w)
                    if w == 0:
                        pe.wait_ge(s_wlo, PPAIRS + WOQ // 2 * (group + 1))
                    for dh in range(2):
                        e = 2 * group + dh
                        cols = slice(dh * TILE, (dh + 1) * TILE)
                        if w:
                            pe.wait_ge(s_outf[e], w)
                        product(ps[e],
                                (lambda k: y_hi[b][:, k], lambda k: y_lo[b][:, k]),
                                (lambda k: wo_hi[:, k, cols], lambda k: wo_lo[:, k, cols]),
                                range(group * NJ, (group + 1) * NJ)).then_inc(s_out[e], 1)
                if w == 0:
                    free_aux(1, AUX_USES)
                    norm_sums_lru(1, 7)
                    pe.wait_ge(s_dc, 2)
                    norm_var(1, 6)
                if 1 <= w < NT - 1:
                    turn_h2(w - 1)

            Q0 = PPAIRS + WOQ

            def last_rows(st, e, k):
                if (st, e, k) in TURN_LAST:
                    turn_h2(TURN_LAST[st, e, k])

            def last_tiles(st):
                pe.wait_ge(s_h2lo, 2 * (TPH + (st + 1) * TILE // P))
                for e in range(2):
                    pe.wait_ge(s_outf[2 * st + e], NT)

            def iteration(h, i, first=False):
                for b in range(2):
                    pe.wait_ge(s_wlo, Q0 + 2 * FI * h + b + 1 + 2 * i)
                    if first and b == 0:
                        pair(wf_hi[b], wf_lo[b], h2_hi, h2_lo, PPAIRS, last_tiles, last_rows)
                    else:
                        pair(wf_hi[b], wf_lo[b], h2_hi, h2_lo, PPAIRS + 2 * FI * h + b + 2 * i)
                pe.wait_ge(s_wdlo, FI * h + 1 + i)
                for t0 in range(0, TPH, 2):
                    for c in range(2):
                        if c == 0 and t0 == 0:
                            pe.wait_ge(s_flo, 4 * FI * h + 2 + 4 * i)
                        if c == 1 and t0 in (0, TPH // 2):
                            pe.wait_ge(s_flo, 4 * FI * h + (3 if t0 == 0 else 4) + 4 * i)
                        for e in range(4):
                            t, dh = t0 + e // 2, e % 2
                            rows, cols = slice(t * P, (t + 1) * P), slice(dh * TILE, (dh + 1) * TILE)
                            if c == 0:
                                pe.wait_ge(s_outf[e], NT + 4 * FI * h + t0 // 2 + 4 * i)
                            mm = product(ps[4 + e], (lambda n: f_hi[n][:, rows], lambda n: f_lo[n][:, rows]),
                                         (lambda n: wd_hi[:, n, cols], lambda n: wd_lo[:, n, cols]),
                                         [c], start=c == 0, stop=c == 1)
                            if c == 1:
                                mm.then_inc(s_out[e], 1)

            pe.wait_ge(s_rsty, 4)
            pe.wait_ge(s_rsts, 4)
            iteration(0, 0, first=True)
            for h in range(NH):
                if h:
                    for st in range(NS):
                        pe.wait_ge(s_h2ld[st], 32)
                with pe.Fori(0 if h else 1, FI) as i:
                    iteration(h, i)


_INS = ["x", "norm_mix", "w_in", "conv4_w", "conv4_b", "gate_a_w", "gate_a_b", "gate_x_w", "gate_x_b",
        "lru_lambda", "dw31_w", "dw31_b", "cm_ln_g", "cm_ln_b", "out_norm_lru", "out_norm_cm", "w_out",
        "norm_ffn", "w_gate", "w_up", "w_down", "norm_final"]


def kernel(**inputs):
    import numpy as np
    from concourse import bacc
    from concourse.bass_utils import run_bass_kernel_spmd

    nc = bacc.Bacc("TRN2", target_bir_lowering=False, num_devices=1, dynamic_dma_scratch_size=SCRATCH)
    arrays, args = {}, []
    for name in _INS:
        a = np.ascontiguousarray(inputs[name])
        arrays[f"in_{name}"] = a
        args.append(nc.dram_tensor(f"in_{name}", a.shape, mybir.dt.from_np(a.dtype), kind="ExternalInput").ap())
    shape = inputs["x"].shape
    args.append(nc.dram_tensor("out_block", shape, F32, kind="ExternalOutput").ap())
    hybrid_block(nc, *args)
    r = run_bass_kernel_spmd(nc, [arrays], core_ids=[0])
    return r.results[0]["out_block"]
```
